# Optimizing a Trainium2 kernel written in Bass

```python
import jax, jax.numpy as jnp
from jax import lax
import numpy as np

D_MODEL = 1024
BATCH = 1
SEQ = 128
DEPTH = 1
DEC_BATCH = 1
DEC_SEQ = 1024
PAST_LEN = 128

GRID_W = 64
H_A = 8
DK_A = 128
DV_A = 128
D_QK = H_A * DK_A
D_VA = H_A * DV_A
CHUNK = 64
CONV_K = 4
CONV_PAD_L = 2
D_B = 1024
NB_B = 8
BW_B = D_B // NB_B
LRU_C = 8.0
EPS = 1e-6
OFF_QKV = 2 * D_QK + D_VA
OFF_ZA = OFF_QKV + D_VA
OFF_XB = OFF_ZA + D_B
OFF_ZB = OFF_XB + D_B
IN_COLS = OFF_ZB + 4 * H_A

kernel_name = 'hybrid_gdn_rglru_prefix_diffusion_step'

def rmsnorm(x, w):
    xf = x.astype(jnp.float32)
    y = xf * lax.rsqrt(jnp.mean(xf * xf, axis=-1, keepdims=True) + EPS)
    return (y * w.astype(jnp.float32)).astype(x.dtype)

def l2norm(x):
    xf = x.astype(jnp.float32)
    return xf * lax.rsqrt(jnp.sum(xf * xf, axis=-1, keepdims=True) + EPS)

def dwconv_centred(x, w, b):
    n = x.shape[1]
    xp = jnp.pad(x, ((0, 0), (CONV_PAD_L, CONV_K - 1 - CONV_PAD_L), (0, 0)))
    y = xp[:, 0:n] * w[0]
    for i in range(1, CONV_K):
        y = y + xp[:, i:i + n] * w[i]
    return y + b

def delta_rule_chunked(q, k, v, g, beta, s0):
    b, h, n, dk = q.shape
    dv = v.shape[-1]
    nc = n // CHUNK
    f32 = jnp.float32
    q = (q.astype(f32) * (dk ** -0.5)).reshape(b, h, nc, CHUNK, dk)
    k = k.astype(f32).reshape(b, h, nc, CHUNK, dk)
    v = v.astype(f32).reshape(b, h, nc, CHUNK, dv)
    g = jnp.cumsum(g.astype(f32).reshape(b, h, nc, CHUNK), axis=-1)
    beta = beta.astype(f32).reshape(b, h, nc, CHUNK, 1)
    idx = jnp.arange(CHUNK)
    incl = idx[:, None] >= idx[None, :]
    strict = idx[:, None] > idx[None, :]
    decay = jnp.exp(jnp.where(incl, g[..., :, None] - g[..., None, :], -jnp.inf))
    kb = k * beta
    a_mat = jnp.where(strict, jnp.einsum('bhnik,bhnjk->bhnij', kb, k) * decay, 0.0)
    lower = a_mat + jnp.eye(CHUNK, dtype=f32)
    rhs = jnp.concatenate([v * beta, kb * jnp.exp(g)[..., None]], axis=-1)
    sol = lax.linalg.triangular_solve(lower, rhs, left_side=True, lower=True, unit_diagonal=True)
    u, w = sol[..., :dv], sol[..., dv:]
    qk = jnp.einsum('bhnik,bhnjk->bhnij', q, k) * decay
    qg = q * jnp.exp(g)[..., None]
    g_last = g[..., -1]
    kd = k * jnp.exp(g_last[..., None] - g)[..., None]
    decay_last = jnp.exp(g_last)

    def step(s, xs):
        w_c, u_c, qg_c, qk_c, kd_c, dl_c = xs
        v_new = u_c - jnp.einsum('bhck,bhkv->bhcv', w_c, s)
        o_c = jnp.einsum('bhck,bhkv->bhcv', qg_c, s) + jnp.einsum('bhcj,bhjv->bhcv', qk_c, v_new)
        s = s * dl_c[..., None, None] + jnp.einsum('bhck,bhcv->bhkv', kd_c, v_new)
        return s, o_c

    xs = tuple(jnp.moveaxis(t, 2, 0) for t in (w, u, qg, qk, kd, decay_last))
    s_fin, o = lax.scan(step, s0.astype(f32), xs)
    o = jnp.moveaxis(o, 0, 2).reshape(b, h, n, dv)
    return o, s_fin

def gdn_branch(qkv, z, gate_cols, p, s_f, s_b):
    bsz, n, _ = qkv.shape
    qkv = jax.nn.silu(dwconv_centred(qkv, p['conv_a_w'], p['conv_a_b']))
    q, k, v = jnp.split(qkv, [D_QK, 2 * D_QK], axis=-1)
    heads = lambda t, d: t.reshape(bsz, n, H_A, d).transpose(0, 2, 1, 3)
    q = l2norm(heads(q, DK_A))
    k = l2norm(heads(k, DK_A))
    v = heads(v, DV_A)
    alpha_f, beta_f, alpha_b, beta_b = jnp.split(gate_cols.astype(jnp.float32), 4, axis=-1)

    def gates(a, bt, a_log, dt_bias):
        g = -jnp.exp(a_log.astype(jnp.float32)) * jax.nn.softplus(a + dt_bias.astype(jnp.float32))
        return g.transpose(0, 2, 1), jax.nn.sigmoid(bt).transpose(0, 2, 1)

    g_f, bet_f = gates(alpha_f, beta_f, p['a_log_fwd'], p['dt_bias_fwd'])
    g_b, bet_b = gates(alpha_b, beta_b, p['a_log_bwd'], p['dt_bias_bwd'])
    o_f, sf_new = delta_rule_chunked(q, k, v, g_f, bet_f, s_f)
    flip = lambda t: jnp.flip(t, axis=2)
    o_b, sb_new = delta_rule_chunked(flip(q), flip(k), flip(v), flip(g_b), flip(bet_b), s_b)
    o = rmsnorm(o_f + flip(o_b), p['onorm_a_w'])
    o = o.transpose(0, 2, 1, 3).reshape(bsz, n, D_VA).astype(z.dtype)
    return o * jax.nn.silu(z), sf_new, sb_new

def blockdiag(x, w, b):
    bsz, n, _ = x.shape
    y = jnp.einsum('bnhi,hij->bnhj', x.reshape(bsz, n, NB_B, BW_B), w).reshape(bsz, n, D_B)
    return y + b

def rglru(x, wa, ba, wx, bx, lam, h0):
    f32 = jnp.float32
    xf = x.astype(f32)
    r = jax.nn.sigmoid(blockdiag(xf, wa.astype(f32), ba.astype(f32)))
    ig = jax.nn.sigmoid(blockdiag(xf, wx.astype(f32), bx.astype(f32)))
    log_a = -LRU_C * r * jax.nn.softplus(-lam.astype(f32))
    a = jnp.exp(log_a)
    bx_t = jnp.sqrt(-jnp.expm1(2.0 * log_a)) * (ig * xf)
    bx_t = bx_t.at[:, 0].add(a[:, 0] * h0.astype(f32))

    def comb(left, right):
        a_l, b_l = left
        a_r, b_r = right
        return a_l * a_r, a_r * b_l + b_r

    _, hs = lax.associative_scan(comb, (a, bx_t), axis=1)
    return hs, hs[:, -1]

def lru_branch(xb, z, p, h_f, h_b, col_major):
    bsz, n, _ = xb.shape
    if col_major:
        rows = n // GRID_W
        to_order = lambda t: t.reshape(bsz, rows, GRID_W, -1).transpose(0, 2, 1, 3).reshape(bsz, n, -1)
        from_order = lambda t: t.reshape(bsz, GRID_W, rows, -1).transpose(0, 2, 1, 3).reshape(bsz, n, -1)
    else:
        to_order = lambda t: t
        from_order = lambda t: t
    xc = dwconv_centred(to_order(xb), p['conv_b_w'], p['conv_b_b'])
    hf, hf_last = rglru(xc, p['lru_wa_fwd'], p['lru_ba_fwd'], p['lru_wx_fwd'], p['lru_bx_fwd'],
                       p['lru_lambda_fwd'], h_f)
    hb, hb_last = rglru(jnp.flip(xc, axis=1), p['lru_wa_bwd'], p['lru_ba_bwd'], p['lru_wx_bwd'],
                        p['lru_bx_bwd'], p['lru_lambda_bwd'], h_b)
    hsum = from_order(hf + jnp.flip(hb, axis=1)).astype(z.dtype)
    return hsum * jax.nn.silu(z), hf_last, hb_last

def trunk_layer(x, mod, s_af, s_ab, s_bf, s_bb, col_major, p):
    shift, scale, gate = jnp.split(mod, 3, axis=-1)
    h = rmsnorm(x, p['norm_w']) * (1 + scale) + shift
    proj = h @ p['w_in']
    qkv, z_a, x_b, z_b, gate_cols = jnp.split(proj, [OFF_QKV, OFF_ZA, OFF_XB, OFF_ZB], axis=-1)
    o_a, sfa, sba = gdn_branch(qkv, z_a, gate_cols, p, s_af, s_ab)
    o_b, sfb, sbb = lru_branch(x_b, z_b, p, s_bf, s_bb, col_major)
    pa = o_a @ p['w_proj_a']
    pb = o_b @ p['w_proj_b']
    g_a, g_b = jnp.split(jax.nn.sigmoid(h @ p['w_gate'] + p['b_gate']), 2, axis=-1)
    mixed = (g_a * pa + g_b * pb) @ p['w_out']
    return x + gate * mixed, sfa, sba, sfb, sbb

def setup_inputs(seed: int = 0) -> dict:
    key = jax.random.key(seed)
    ks = iter(jax.random.split(key, 64))
    nk = lambda: next(ks)
    nrm = lambda shape, s: jax.random.normal(nk(), shape, jnp.float32) * s
    L = DEPTH
    dt = jnp.exp(jax.random.uniform(nk(), (L, H_A), jnp.float32, np.log(1e-3), np.log(1e-1)))
    dt2 = jnp.exp(jax.random.uniform(nk(), (L, H_A), jnp.float32, np.log(1e-3), np.log(1e-1)))
    inv_sp = lambda d: d + jnp.log(-jnp.expm1(-d))
    a0 = jax.random.uniform(nk(), (L, D_B), jnp.float32, 0.9, 0.999)
    a1 = jax.random.uniform(nk(), (L, D_B), jnp.float32, 0.9, 0.999)
    logit = lambda a: jnp.log(a) - jnp.log1p(-a)
    return {
        'x_prompt': nrm((BATCH, SEQ, D_MODEL), 1.0),
        'x_sample': nrm((DEC_BATCH, DEC_SEQ, D_MODEL), 1.0),
        'state_a_fwd': nrm((DEC_BATCH, DEPTH, H_A, DK_A, DV_A), 0.5),
        'state_a_bwd': nrm((DEC_BATCH, DEPTH, H_A, DK_A, DV_A), 0.5),
        'state_b_fwd': nrm((DEC_BATCH, DEPTH, D_B), 0.5),
        'state_b_bwd': nrm((DEC_BATCH, DEPTH, D_B), 0.5),
        'c': nrm((DEC_BATCH, D_MODEL), 1.0),
        'c_ctx': nrm((D_MODEL,), 1.0),
        'norm_w': 1.0 + nrm((L, D_MODEL), 0.02),
        'w_mod': nrm((L, D_MODEL, 3 * D_MODEL), 0.5 * D_MODEL ** -0.5),
        'b_mod': nrm((L, 3 * D_MODEL), 0.01),
        'w_in': nrm((L, D_MODEL, IN_COLS), D_MODEL ** -0.5),
        'conv_a_w': nrm((L, CONV_K, OFF_QKV), CONV_K ** -0.5),
        'conv_a_b': nrm((L, OFF_QKV), 0.01),
        'a_log_fwd': jnp.log(jax.random.uniform(nk(), (L, H_A), jnp.float32, 1.0, 16.0)),
        'dt_bias_fwd': inv_sp(dt),
        'a_log_bwd': jnp.log(jax.random.uniform(nk(), (L, H_A), jnp.float32, 1.0, 16.0)),
        'dt_bias_bwd': inv_sp(dt2),
        'onorm_a_w': 1.0 + nrm((L, DV_A), 0.02),
        'conv_b_w': nrm((L, CONV_K, D_B), CONV_K ** -0.5),
        'conv_b_b': nrm((L, D_B), 0.01),
        'lru_wa_fwd': nrm((L, NB_B, BW_B, BW_B), BW_B ** -0.5),
        'lru_ba_fwd': nrm((L, D_B), 0.01),
        'lru_wx_fwd': nrm((L, NB_B, BW_B, BW_B), BW_B ** -0.5),
        'lru_bx_fwd': nrm((L, D_B), 0.01),
        'lru_lambda_fwd': logit(a0),
        'lru_wa_bwd': nrm((L, NB_B, BW_B, BW_B), BW_B ** -0.5),
        'lru_ba_bwd': nrm((L, D_B), 0.01),
        'lru_wx_bwd': nrm((L, NB_B, BW_B, BW_B), BW_B ** -0.5),
        'lru_bx_bwd': nrm((L, D_B), 0.01),
        'lru_lambda_bwd': logit(a1),
        'w_proj_a': nrm((L, D_VA, D_MODEL), D_VA ** -0.5),
        'w_proj_b': nrm((L, D_B, D_MODEL), D_B ** -0.5),
        'w_gate': nrm((L, D_MODEL, 2 * D_MODEL), D_MODEL ** -0.5),
        'b_gate': nrm((L, 2 * D_MODEL), 0.01),
        'w_out': nrm((L, D_MODEL, D_MODEL), D_MODEL ** -0.5),
        'final_norm_w': 1.0 + nrm((D_MODEL,), 0.02),
    }

def reference(x_prompt, x_sample, state_a_fwd, state_a_bwd, state_b_fwd, state_b_bwd, c, c_ctx,
              norm_w, w_mod, b_mod, w_in, conv_a_w, conv_a_b, a_log_fwd, dt_bias_fwd, a_log_bwd,
              dt_bias_bwd, onorm_a_w, conv_b_w, conv_b_b, lru_wa_fwd, lru_ba_fwd, lru_wx_fwd,
              lru_bx_fwd, lru_lambda_fwd, lru_wa_bwd, lru_ba_bwd, lru_wx_bwd, lru_bx_bwd,
              lru_lambda_bwd, w_proj_a, w_proj_b, w_gate, b_gate, w_out, final_norm_w):
    bp = x_prompt.shape[0]
    xp, xs = x_prompt, x_sample
    new_af, new_ab, new_bf, new_bb = [], [], [], []
    for l in range(DEPTH):
        p = {
            'norm_w': norm_w[l], 'w_in': w_in[l], 'conv_a_w': conv_a_w[l], 'conv_a_b': conv_a_b[l],
            'a_log_fwd': a_log_fwd[l], 'dt_bias_fwd': dt_bias_fwd[l],
            'a_log_bwd': a_log_bwd[l], 'dt_bias_bwd': dt_bias_bwd[l], 'onorm_a_w': onorm_a_w[l],
            'conv_b_w': conv_b_w[l], 'conv_b_b': conv_b_b[l],
            'lru_wa_fwd': lru_wa_fwd[l], 'lru_ba_fwd': lru_ba_fwd[l], 'lru_wx_fwd': lru_wx_fwd[l],
            'lru_bx_fwd': lru_bx_fwd[l], 'lru_lambda_fwd': lru_lambda_fwd[l],
            'lru_wa_bwd': lru_wa_bwd[l], 'lru_ba_bwd': lru_ba_bwd[l], 'lru_wx_bwd': lru_wx_bwd[l],
            'lru_bx_bwd': lru_bx_bwd[l], 'lru_lambda_bwd': lru_lambda_bwd[l],
            'w_proj_a': w_proj_a[l], 'w_proj_b': w_proj_b[l], 'w_gate': w_gate[l],
            'b_gate': b_gate[l], 'w_out': w_out[l],
        }
        mod_ctx = (jax.nn.silu(c_ctx) @ w_mod[l] + b_mod[l])[None, None, :]
        mod_lat = (jax.nn.silu(c) @ w_mod[l] + b_mod[l])[:, None, :]
        za = jnp.zeros((bp, H_A, DK_A, DV_A), jnp.float32)
        zb = jnp.zeros((bp, D_B), jnp.float32)
        xp, saf, sab, sbf, sbb = trunk_layer(xp, mod_ctx, za, za, zb, zb, False, p)
        new_af.append(saf.astype(x_prompt.dtype))
        new_ab.append(sab.astype(x_prompt.dtype))
        new_bf.append(sbf.astype(x_prompt.dtype))
        new_bb.append(sbb.astype(x_prompt.dtype))
        xs, _, _, _, _ = trunk_layer(xs, mod_lat, state_a_fwd[:, l], state_a_bwd[:, l],
                                     state_b_fwd[:, l], state_b_bwd[:, l], True, p)
    y_prompt = rmsnorm(xp, final_norm_w)
    y_sample = rmsnorm(xs, final_norm_w)
    new_state_a_fwd = jnp.stack(new_af, axis=1)
    new_state_a_bwd = jnp.stack(new_ab, axis=1)
    new_state_b_fwd = jnp.stack(new_bf, axis=1)
    new_state_b_bwd = jnp.stack(new_bb, axis=1)
    return (y_prompt, y_sample, new_state_a_fwd, new_state_a_bwd, new_state_b_fwd, new_state_b_bwd)


_drawn_inputs = setup_inputs


def setup_inputs(seed=0):
    import zlib

    import numpy as np

    out = dict(_drawn_inputs(seed))
    spreads = {}
    factors = {'state_a_fwd': 3.649,
     'state_a_bwd': 3.41,
     'state_b_fwd': 8.0,
     'state_b_bwd': 8.0,
     'conv_a_b': 4.312,
     'onorm_a_w': 37.614,
     'lru_ba_fwd': 24.826,
     'lru_bx_fwd': 8.0,
     'lru_ba_bwd': 25.688,
     'lru_bx_bwd': 8.0,
     'b_gate': 22.601,
     'final_norm_w': 2.682}
    for name, (base, spread) in spreads.items():
        noise = np.random.default_rng([zlib.crc32(name.encode()), seed]).standard_normal(out[name].shape)
        drawn = base * np.exp(spread * noise) if base else spread * noise
        out[name] = __import__('jax').numpy.asarray(drawn.astype(out[name].dtype))
    for name, factor in factors.items():
        out[name] = (out[name] * factor).astype(out[name].dtype)
    return out
```

```python
from contextlib import ExitStack

import concourse.bass as bass
import numpy as np
from concourse import mybir

F32 = mybir.dt.float32
F32R = mybir.dt.float32r
ALU = mybir.AluOpType
ACT = mybir.ActivationFunctionType
AX = mybir.AxisListType

P = 128
D = 1024
KT = D // P
H = 8
CTX, LAT = 128, 1024
TOK = CTX + LAT
NT = TOK // P
TG = 3
NG = NT // TG
GW = TG * P
DIRS = 2
NI = NT * DIRS
NGD = NG * DIRS
LEVELS = 7
GRID_W = 64
GRID_R = LAT // GRID_W
TAPS, PAD_L = 4, 2
GAP = TAPS - 1
RAW = PAD_L + CTX + GAP + LAT + 1
CONV = RAW - GAP
LAT0 = CTX + GAP
EPS = 1e-6
LRU_C = 8.0

PA_CONV = 0
PA_NORM = 120
PB = 128
PB_LRU = PB
PB_GATE = PB + 88
PB_ONORM = PB + 104
PC = 256
NLP = 11

G_DECAY, G_BETA, G_EXPCUM, G_EXPREST, G_EXPALL = range(5)


def tile_at(t):
    return 0 if t == 0 else LAT0 + (t - 1) * P


def constants():
    r, c = np.mgrid[0:P, 0:P]
    out = [r <= c, r >= c, r < c, r > c, r == c, np.ones((P, P))]
    for level in range(LEVELS):
        b = 1 << level
        pair = (c // b == r // b + 1) & ((r // b) % 2 == 0)
        fwd = (r == c).astype(np.float32) - pair.astype(np.float32)
        out += [fwd, fwd.T]
    return np.concatenate([np.asarray(m, np.float32) for m in out], axis=1)


M_TRIU, M_TRIL, M_STRIU, M_STRIL, M_ID, M_ONE, M_LEVEL = 0, 1, 2, 3, 4, 5, 6
NM = M_LEVEL + 2 * LEVELS


class Resident:

    def __init__(self, nc, ctx):
        sb = lambda name, shape, dt=F32: ctx.enter_context(nc.sbuf_tensor(name, shape, dt))
        self.masks = sb("masks", [P, NM * P])
        self.par = sb("par", [P, 3 * P])
        self.hhi = sb("h_hi", [P, KT, TOK], F32R)
        self.hlo = sb("h_lo", [P, KT, TOK], F32R)
        self.gates = sb("gates", [P, 5, NI, H])
        self.rate = sb("lru_rate", [P, 2, DIRS, H])
        self.newb = sb("new_state_b_cols", [P, DIRS, H])

    def m(self, k, n=1):
        return self.masks[:, k * P:(k + n) * P]

    def level(self, level, d):
        return self.m(M_LEVEL + 2 * level + d)


def bc(ap, n):
    return ap.unsqueeze(1).broadcast_to([P, n, P])


def cols(ap, n):
    return ap.unsqueeze(2).broadcast_to([P, n, P])


def v3(ap):
    return ap.rearrange("p (j c) -> p j c", c=P)


def setup_stage(nc, R, A, gate_rows):
    with ExitStack() as ctx:
        sb = lambda name, shape, dt=F32: ctx.enter_context(nc.sbuf_tensor(name, shape, dt))
        sems = []

        def sem(name):
            sems.append(nc.alloc_semaphore(name))
            return sems[-1]

        rows = sb("rows", [P, 3, P])
        wmod = sb("wmod", [P, 4, 3 * D])
        bmod = sb("bmod", [2, 3 * D])
        modrow = sb("modrow", [2, 3 * D])
        sc = sb("silu_c", [P, 2, KT])
        sct = sb("silu_c_tanh", [P, 2 * KT])
        mod = sb("mod_cols", [P, 2 * KT, 2])
        gain = sb("gain", [P, 2, KT])
        shift = sb("shift", [P, 2, KT])
        x = sb("x", [P, 2, D])
        xsq = sb("xsq", [P, D])
        xn = sb("xn", [P, D])
        ss = sb("ss", [P, 1])
        ms = sb("ms", [P, 1])
        rstd = sb("rstd", [P, 1])
        mhalf = sb("minus_half", [P, 1])
        hf = sb("hf", [P, KT, P])
        wg = sb("wg", [P, KT, 4 * H])
        graw = sb("graw", [P, NT, 4 * H])
        dtb = sb("dt_bias", [P, DIRS, H])
        alog = sb("a_log", [P, DIRS, H])
        ea = sb("exp_a_log", [P, DIRS, H])
        gx = sb("gate_x", [P, NT, DIRS, H])
        gu = sb("gate_u", [P, NT * DIRS * H])
        gw = sb("gate_w1", [P, NT * DIRS * H])
        gl = sb("gate_ln", [P, NT * DIRS * H])
        gr = sb("gate_r", [P, NT * DIRS * H])
        gt = sb("gate_t", [P, NT * DIRS * H])
        lu = sb("lam_u", [P, DIRS * H])
        lw = sb("lam_w", [P, DIRS * H])
        ll = sb("lam_l", [P, DIRS * H])
        lr = sb("lam_r", [P, DIRS * H])
        bank = [ctx.enter_context(nc.psum_tensor(f"sb{i}", [P, 512], F32)) for i in range(8)]

        consts_in, rows_in, rows_zero = sem("consts_in"), sem("rows_in"), sem("rows_zero")
        small_in, wmod_in, x_in = sem("small_in"), [sem(f"wmod_in{i}") for i in range(4)], [sem(f"x_in{i}") for i in range(2)]
        rows_t, par_done, silu_t, silu_done = sem("rows_t"), sem("par_done"), sem("silu_t"), sem("silu_done")
        mod_k, mod_row, mod_t, mod_done = sem("mod_k"), sem("mod_row"), sem("mod_t"), sem("mod_done")
        half_set, gate_out = sem("half_set"), sem("gate_out")
        x_sq, x_rstd, x_n, x_t, h_f, h_hi, h_lo, g_mm, g_copy = (sem(n) for n in (
            "x_sq", "x_rstd", "x_n", "x_t", "h_f", "h_hi", "h_lo", "g_mm", "g_copy"))
        dve_own, pool_own = sem("dve_own"), sem("pool_own")
        act_exp, dve_w, act_ln, act_th, gates_raw, cum_mm, cum_exp = (sem(n) for n in (
            "act_exp", "dve_w", "act_ln", "act_th", "gates_raw", "cum_mm", "cum_exp"))
        ctx.callback(nc.all_engine_barrier)
        ctx.callback(lambda: nc.clear_and_free_semaphores(sems))
        block = ctx.enter_context(nc.Block())
        conv_a = A["conv_a_w"][0].rearrange("a (r p) -> (a r) p", p=P)
        row1 = lambda name: A[name][0].rearrange("(r p) -> r p", p=P)
        bcast = lambda name: A[name].broadcast_to([P, H])
        sources = [
            (0, 0, conv_a, 96), (0, 96, row1("conv_a_b"), 24), (0, 120, row1("norm_w"), KT),
            (1, 0, A["conv_b_w"][0].rearrange("a (r p) -> (a r) p", p=P), 32), (1, 32, row1("conv_b_b"), 8),
            (1, 40, row1("lru_ba_fwd"), 8), (1, 48, row1("lru_bx_fwd"), 8),
            (1, 56, row1("lru_ba_bwd"), 8), (1, 64, row1("lru_bx_bwd"), 8),
            (1, 72, row1("lru_lambda_fwd"), 8), (1, 80, row1("lru_lambda_bwd"), 8),
            (1, 88, row1("b_gate"), 16), (1, 104, row1("onorm_a_w"), 1),
            (2, 0, A["c_ctx"].rearrange("(r p) -> r p", p=P), 8), (2, 8, row1("c"), 8),
            (2, 16, A["state_b_fwd"][0, 0].rearrange("(r p) -> r p", p=P), 8),
            (2, 24, A["state_b_bwd"][0, 0].rearrange("(r p) -> r p", p=P), 8),
        ]
        small = [(dtb[:, 0, :], bcast("dt_bias_fwd")), (dtb[:, 1, :], bcast("dt_bias_bwd")),
                 (alog[:, 0, :], bcast("a_log_fwd")), (alog[:, 1, :], bcast("a_log_bwd")),
                 (bmod[:, :], A["b_mod"].broadcast_to([2, 3 * D])),
                 (wg[:, :, :], A["w_in"][0, :, 6 * D:6 * D + 4 * H].rearrange("(k p) n -> p k n", p=P))]

        @block.sync
        def _(sp):
            sp.wait_ge(rows_zero, 1)
            for t, r, src, n in sources:
                sp.dma_start(rows[r:r + n, t, :], src).then_inc(rows_in, 16)
            sp.dma_start(R.masks[:, :], A["consts"]).then_inc(consts_in, 16)
            for k in range(KT):
                if k >= 4:
                    sp.wait_ge(mod_k, k - 3)
                sp.dma_start(wmod[:, k % 4, :], A["w_mod"][0, k * P:(k + 1) * P, :]).then_inc(wmod_in[k % 4], 16)
            for dst, src in small:
                sp.dma_start(dst, src).then_inc(small_in, 16)
            for t in range(NT):
                src = A["x_prompt"][0] if t == 0 else A["x_sample"][0, (t - 1) * P:t * P, :]
                if t >= 2:
                    sp.wait_ge(x_n, t - 1)
                sp.dma_start(x[:, t % 2, :], src).then_inc(x_in[t % 2], 16)
            sp.wait_ge(mod_row, 1)
            sp.dma_start(gate_rows, modrow[:, 2 * D:3 * D]).then_inc(gate_out, 16)
            sp.wait_ge(gate_out, 16)

        @block.gpsimd
        def _(pool):
            pool.memset(rows[:, :, :], 0.0).then_inc(rows_zero, 1)
            pool.memset(mhalf[:, :], -0.5).then_inc(half_set, 1)
            pool.wait_ge(half_set, 1)
            for t in range(NT):
                pool.wait_ge(x_sq, t + 1)
                if t:
                    pool.wait_ge(x_n, t)
                pool.tensor_scalar(ms[:, :], ss[:, :], 1.0 / D, EPS, ALU.mult, ALU.add).then_inc(pool_own, 1)
                pool.wait_ge(pool_own, t + 1)
                pool.tensor_tensor(rstd[:, :], ms[:, :], mhalf[:, :], ALU.pow).then_inc(x_rstd, 1)
                pool.wait_ge(h_hi, t + 1)
                ts = slice(t * P, (t + 1) * P)
                pool.tensor_tensor(R.hlo[:, :, ts], hf[:, :, :], R.hhi[:, :, ts].bitcast(F32),
                                   ALU.subtract).then_inc(h_lo, 1)

        @block.scalar
        def _(act):
            act.wait_ge(par_done, 3)
            act.activation(sct[:, :], R.par[:, PC:PC + 16], ACT.Tanh, scale=0.5).then_inc(silu_t, 1)
            for t in range(NT):
                act.wait_ge(x_in[t % 2], 16 * (t // 2 + 1))
                if t:
                    act.wait_ge(x_rstd, t)
                    act.wait_ge(x_sq, t)
                act.activation(xsq[:, :], x[:, t % 2, :], ACT.Square, accum_out=ss[:, :]).then_inc(x_sq, 1)
                act.wait_ge(x_rstd, t + 1)
                if t:
                    act.wait_ge(x_t, t)
                act.activation(xn[:, :], x[:, t % 2, :], ACT.Copy, scale=rstd[:, 0:1]).then_inc(x_n, 1)
                act.wait_ge(h_f, t + 1)
                act.activation(R.hhi[:, :, t * P:(t + 1) * P], hf[:, :, :], ACT.Copy).then_inc(h_hi, 1)
            act.wait_ge(gates_raw, 1)
            act.activation(gu[:, :], gt[:, :], ACT.Exp, scale=-1.0).then_inc(act_exp, 1)
            act.activation(ea[:, :, :], alog[:, :, :], ACT.Exp).then_inc(act_exp, 1)
            act.activation(lu[:, :], lr[:, :], ACT.Exp, scale=-1.0).then_inc(act_exp, 1)
            act.wait_ge(dve_w, 2)
            act.activation(gl[:, :], gw[:, :], ACT.Ln).then_inc(act_ln, 1)
            act.activation(ll[:, :], lw[:, :], ACT.Ln).then_inc(act_ln, 1)
            beta = R.gates[:, G_BETA].rearrange("p (g d j) h -> p g d j h", g=NG, d=DIRS)
            for d in range(DIRS):
                for g in range(NG):
                    act.activation(beta[:, g, d], graw[:, TG * g:TG * (g + 1), (2 * d + 1) * H:(2 * d + 2) * H],
                                   ACT.Tanh, scale=0.5).then_inc(act_th, 1)
            kinds = (G_EXPCUM, G_EXPREST, G_EXPALL)
            for n, kind in enumerate(kinds):
                act.wait_ge(cum_mm, n + 1)
                act.activation(R.gates[:, kind], bank[5 + n][:, 0:NI * H].rearrange("p (n h) -> p n h", h=H),
                               ACT.Exp).then_inc(cum_exp, 1)

        @block.tensor
        def _(pe):
            pe.wait_ge(rows_in, 16 * len(sources))
            pe.wait_ge(consts_in, 16)
            for t in range(3):
                pe.transpose(bank[6][:, t * P:(t + 1) * P], rows[:, t, :], R.m(M_ID)).then_inc(rows_t, 1)
            pe.wait_ge(silu_done, 1)
            for k in range(KT):
                pe.wait_ge(wmod_in[k % 4], 16 * (k // 4 + 1))
                for n in range(6):
                    mm = pe.matmul(bank[n][0:2, :], sc[:, :, k], wmod[:, k % 4, n * 512:(n + 1) * 512],
                                   start=(k == 0), stop=(k == KT - 1))
                mm.then_inc(mod_k, 1)
            pe.wait_ge(mod_row, 1)
            for n in range(2 * KT):
                mm = pe.transpose(bank[6][:, 2 * n:2 * n + 2], modrow[:, n * P:(n + 1) * P],
                                  R.masks[0:2, M_ID * P:M_ID * P + 2])
            mm.then_inc(mod_t, 1)
            for t in range(NT):
                pe.wait_ge(x_n, t + 1)
                if t:
                    pe.wait_ge(h_f, t)
                for k in range(KT):
                    mm = pe.transpose(bank[k // 4][:, (k % 4) * P:(k % 4 + 1) * P], xn[:, k * P:(k + 1) * P],
                                      R.m(M_ID))
                mm.then_inc(x_t, 1)
                pe.wait_ge(h_f, t + 1)
                if t == 0:
                    pe.wait_ge(small_in, 16 * len(small))
                if t:
                    pe.wait_ge(g_copy, t)
                for k in range(KT):
                    mm = pe.matmul(bank[3][:, 0:4 * H], hf[:, k, :], wg[:, k, :], start=(k == 0), stop=(k == KT - 1))
                mm.then_inc(g_mm, 1)
            pe.wait_ge(gates_raw, 2)
            sums = ((M_TRIU, M_TRIL), (M_STRIL, M_STRIU), (M_ONE, M_ONE))
            gam = R.gates[:, G_DECAY].rearrange("p (g d j) h -> p g d (j h)", g=NG, d=DIRS)
            for n, pair in enumerate(sums):
                for d in range(DIRS):
                    out = bank[5 + n][:, 0:NI * H].rearrange("p (g d x) -> p g d x", g=NG, d=DIRS)[:, :, d, :]
                    mm = pe.matmul(out, R.m(pair[d]), gam[:, :, d, :], start=True, stop=True)
                mm.then_inc(cum_mm, 1)

        @block.vector
        def _(dve):
            links = [0]

            def link(ins):
                links[0] += 1
                ins.then_inc(dve_own, 1)
                dve.wait_ge(dve_own, links[0])

            for t in range(3):
                dve.wait_ge(rows_t, 3)
                dve.tensor_copy(R.par[:, t * P:(t + 1) * P], bank[6][:, t * P:(t + 1) * P]).then_inc(par_done, 1)
            dve.wait_ge(silu_t, 1)
            dve.wait_ge(par_done, 3)
            link(dve.scalar_tensor_tensor(out=sct[:, :], in0=sct[:, :], scalar=1.0, in1=R.par[:, PC:PC + 16],
                                          op0=ALU.add, op1=ALU.mult))
            dve.tensor_scalar(sc[:, :, :], sct[:, :].rearrange("p (a k) -> p a k", a=2), 0.5, None,
                              ALU.mult).then_inc(silu_done, 1)
            link(dve.tensor_scalar(R.par[:, PB + 40:PB + 72], R.par[:, PB + 40:PB + 72], 0.5, None, ALU.mult))
            link(dve.tensor_scalar(R.par[:, PB_GATE:PB_GATE + 17], R.par[:, PB_GATE:PB_GATE + 17], 0.5, None, ALU.mult))
            dve.wait_ge(mod_k, KT)
            dve.wait_ge(small_in, 16 * len(small))
            for n in range(6):
                ns = slice(n * 512, (n + 1) * 512)
                mm = dve.tensor_tensor(modrow[:, ns], bank[n][0:2, :], bmod[:, ns], ALU.add)
            mm.then_inc(mod_row, 1)
            dve.wait_ge(mod_t, 1)
            link(dve.tensor_copy(mod[:, :, :], bank[6][:, 0:4 * KT].rearrange("p (k a) -> p k a", a=2)))
            for a in range(2):
                dve.scalar_tensor_tensor(out=gain[:, a, :], in0=mod[:, KT:2 * KT, a], scalar=1.0,
                                         in1=R.par[:, PA_NORM:PA_NORM + KT], op0=ALU.add, op1=ALU.mult)
                link(dve.tensor_copy(shift[:, a, :], mod[:, 0:KT, a]))
            for t in range(NT):
                a = 0 if t == 0 else 1
                dve.wait_ge(x_t, t + 1)
                if t:
                    dve.wait_ge(h_lo, t)
                    dve.wait_ge(g_mm, t)
                for half in range(2):
                    ks = slice(4 * half, 4 * half + 4)
                    ins = dve.tensor_tensor(hf[:, ks, :], v3(bank[half][:, :]), cols(gain[:, a, ks], 4), ALU.mult)
                link(ins)
                dve.tensor_tensor(hf[:, :, :], hf[:, :, :], cols(shift[:, a, :], KT), ALU.add).then_inc(h_f, 1)
                dve.wait_ge(g_mm, t + 1)
                dve.tensor_copy(graw[:, t, :], bank[3][:, 0:4 * H]).then_inc(g_copy, 1)
            dve.wait_ge(g_copy, NT)
            for d in range(DIRS):
                ins = dve.tensor_tensor(gx[:, :, d, :], graw[:, :, 2 * d * H:(2 * d + 1) * H],
                                        dtb[:, d, :].unsqueeze(1).broadcast_to([P, NT, H]), ALU.add)
            link(ins)
            gxf = gx[:, :, :, :].rearrange("p t d h -> p (t d h)")
            lam = R.par[:, PB + 72:PB + 88]
            link(dve.tensor_scalar(gt[:, :], gxf, -1.0, None, ALU.mult))
            dve.tensor_tensor(gt[:, :], gt[:, :], gxf, ALU.max).then_inc(dve_own, 1)
            links[0] += 1
            link(dve.tensor_scalar(lr[:, :], lam, -1.0, None, ALU.mult))
            dve.tensor_tensor(lr[:, :], lr[:, :], lam, ALU.max).then_inc(gates_raw, 1)
            dve.wait_ge(act_exp, 3)
            dve.tensor_scalar(gw[:, :], gu[:, :], 1.0, None, ALU.add).then_inc(dve_w, 1)
            dve.tensor_scalar(lw[:, :], lu[:, :], 1.0, None, ALU.add).then_inc(dve_w, 1)
            dve.wait_ge(dve_w, 2)
            for u, w, r, ln, xx, sign in ((gu, gw, gr, gl, gxf, 1.0), (lu, lw, lr, ll, lam, -1.0)):
                link(dve.reciprocal(r[:, :], w[:, :]))
                t_ = gt if u is gu else sct
                link(dve.tensor_scalar(t_[:, :], w[:, :], -1.0, None, ALU.add))
                link(dve.tensor_tensor(t_[:, :], u[:, :], t_[:, :], ALU.subtract))
                link(dve.tensor_tensor(t_[:, :], t_[:, :], r[:, :], ALU.mult))
                dve.wait_ge(act_ln, 2)
                link(dve.tensor_tensor(t_[:, :], t_[:, :], ln[:, :], ALU.add))
                link(dve.tensor_scalar(r[:, :], xx, sign, 0.0, ALU.mult, ALU.max))
                link(dve.tensor_tensor(t_[:, :], t_[:, :], r[:, :], ALU.add))
            rate = R.rate[:, :, :, :].rearrange("p s d h -> p s (d h)")
            dve.tensor_scalar(rate[:, 0], sct[:, :], LRU_C / 2, None, ALU.mult)
            dve.tensor_scalar(rate[:, 1], sct[:, :], -LRU_C / 2, None, ALU.mult)
            link(dve.tensor_scalar(ea[:, :, :], ea[:, :, :], -1.0, None, ALU.mult))
            gam = R.gates[:, G_DECAY].rearrange("p (g d j) h -> p g d j h", g=NG, d=DIRS)
            sp_ = gt[:, :].rearrange("p (g j d h) -> p g j d h", g=NG, j=TG, d=DIRS)
            for d in range(DIRS):
                for g in range(NG):
                    ins = dve.tensor_tensor(gam[:, g, d], sp_[:, g, :, d, :],
                                            ea[:, d, :].unsqueeze(1).broadcast_to([P, TG, H]), ALU.mult)
            ins.then_inc(gates_raw, 1)
            dve.wait_ge(act_th, DIRS * NG)
            dve.tensor_scalar(R.gates[:, G_BETA], R.gates[:, G_BETA], 1.0, 0.5, ALU.add, ALU.mult).then_inc(dve_own, 1)


def split_product(pe, out, hi, lo, rhi, rlo, k, last, stop=True):
    pe.matmul(out, hi, rhi, start=(k == 0), stop=False)
    pe.matmul(out, hi, rlo, start=False, stop=False)
    return pe.matmul(out, lo, rhi, start=False, stop=(last and stop))


def delta_stage(nc, R, A, oa):
    with ExitStack() as ctx:
        sb = lambda name, shape, dt=F32: ctx.enter_context(nc.sbuf_tensor(name, shape, dt))
        sem = lambda name: ctx.enter_context(nc.semaphore(name))
        wst = sb("d_w", [P, KT, P])
        whi = sb("d_w_hi", [P, 2, KT, P], F32R)
        wlo = sb("d_w_lo", [P, 2, KT, P], F32R)
        raw = sb("d_raw", [P, 3, RAW])
        zraw = sb("d_z", [P, TOK])
        q2 = sb("d_q", [P, CONV])
        ework = sb("d_e", [P, 2 * CONV])
        rwork = sb("d_r", [P, 2 * CONV])
        lmat = sb("d_l", [P, NI * P])
        xmat = sb("d_x", [P, NI * P])
        ymat = sb("d_y", [P, NI * P])
        kn = sb("d_kn", [P, NT, P])
        vt = sb("d_v", [P, NT, P])
        kacc = sb("d_kacc", [P, NT, P])
        gs = sb("d_gs", [P, 2, GW])
        state = sb("d_state", [P, DIRS, P])
        state0 = sb("d_state0", [P, DIRS, P])
        vn = sb("d_vn", [P, 2, DIRS, P])
        vk = sb("d_vk", [P, 2, DIRS, P])
        cw = sb("d_cw", [P, 5, 3, 1])
        gh = sb("d_gh", [P, 5, NI, 1])
        ssk = sb("d_ssk", [P, NT])
        rk = sb("d_rk", [P, NT])
        ssq = sb("d_ssq", [P, NT])
        sso = sb("d_sso", [P, NT])
        ro = sb("d_ro", [P, NT])
        mhalf = sb("d_mhalf", [P, NT])
        bank = [ctx.enter_context(nc.psum_tensor(f"db{i}", [P, 512], F32)) for i in range(8)]
        proj = bank[6:8]
        ca, cb_ = rwork[:, 0:CONV], rwork[:, CONV:2 * CONV]
        cc, cd = ework[:, 0:CONV], ework[:, CONV:2 * CONV]

        S = {n: sem("d_" + n) for n in (
            "w_in", "w_hi", "w_lo", "proj_mm", "proj_out", "pads", "half",
            "par", "cw", "taps", "silu_t", "silu", "sq", "ss_mm", "ssk", "rk", "ssq", "kt", "kn", "vt", "vt_out", "knt",
            "knt_out", "gs", "dec", "dexp", "dmask", "kk", "gq", "l_raw", "qk", "l_done", "lt", "y0", "x0", "r", "r_out",
            "xy", "x_out", "y_out", "yb", "ybe", "nw", "nw_out", "qt", "qt_out", "st_in", "vnew", "vn_out", "vk_out",
            "su", "st_new", "st0", "ov", "acc", "own", "own2", "st_store", "osq", "osum", "ro", "ofac", "ot", "z_t", "z_s", "fin",
            "oa_store")}
        block = ctx.enter_context(nc.Block())
        w_in = A["w_in"][0].rearrange("(k p) n -> p k n", p=P)
        QKV = (1, 2, 0)
        PRE, PERW = 3, 4
        KB = (4, 5, 3)
        g_ = PERW * NG
        levels = LEVELS - 1

        def turns(eng, body):
            body(0, True, False)
            with eng.Fori(1, H - 1) as i:
                body(i, False, False)
            body(H - 1, False, True)

        @block.sync
        def _(sp):
            def load(col, need):
                if need is not None:
                    sp.wait_ge(S["w_lo"], need)
                sp.dma_start(wst[:, :, :], w_in[:, :, bass.ds(col, P)]).then_inc(S["w_in"], 16)

            for j, c in enumerate(QKV + (3,)):
                load(c * D, j or None)

            def turn(i, first, last):
                val = int if first or last else sp.snap
                cols_ = [] if last else [val(i * P + (c * D + P)) for c in QKV + (3,)]
                need = [val(i * PERW + PERW + k) for k in range(PERW)]
                ov, row, st0 = val(i * NT), val(i * 1), val(i * 1 + 1)
                fin, orow = val(i * NG + NG), val(i * P)
                if not first:
                    sp.wait_ge(S["ov"], ov)
                for d, name in enumerate(("state_a_fwd", "state_a_bwd")):
                    sp.dma_start(state[:, d, :], A[name][0, 0, bass.ds(row, 1)].rearrange("a k v -> k (a v)")
                                 ).then_inc(S["st_in"], 16)
                for c, n in zip(cols_[:NG], need):
                    load(c, n)
                sp.wait_ge(S["st0"], st0)
                for d, name in enumerate(("new_af", "new_ab")):
                    sp.dma_start(A[name][0, 0, bass.ds(row, 1)].rearrange("a k v -> k (a v)"), state0[:, d, :]
                                 ).then_inc(S["st_store"], 16)
                if not last:
                    load(cols_[NG], need[NG])
                sp.wait_ge(S["fin"], fin)
                sp.dma_start(oa[bass.ds(orow, P), :], cc[:, 0:TOK]).then_inc(S["oa_store"], 16)

            turns(sp, turn)
            sp.wait_ge(S["st_store"], 16 * DIRS * H)
            sp.wait_ge(S["oa_store"], 16 * H)

        @block.gpsimd
        def _(pool):
            pool.memset(raw[:, :, 0:PAD_L], 0.0)
            pool.memset(raw[:, :, PAD_L + CTX:PAD_L + CTX + GAP], 0.0)
            pool.memset(raw[:, :, RAW - 1:RAW], 0.0).then_inc(S["pads"], 1)
            pool.memset(mhalf[:, :], -0.5).then_inc(S["half"], 1)
            pool.wait_ge(S["half"], 1)
            one = pool.to_reg(1.0)

            def low(j, slot):
                pool.wait_ge(S["w_hi"], j + 1)
                pool.tensor_tensor(wlo[:, slot], wst[:, :, :], whi[:, slot].bitcast(F32),
                                   ALU.subtract).then_inc(S["w_lo"], 1)

            for j in range(PRE + 1):
                low(j, j % 2)

            def rsqrt_k(j):
                pool.wait_ge(S["ssk"], j + 1)
                pool.tensor_tensor(rk[:, :], ssk[:, :], mhalf[:, :], ALU.pow).then_inc(S["rk"], 1)

            rsqrt_k(0)

            def turn(i, first, last):
                def steps(n):
                    if n == 0:
                        pool.wait_ge(S["par"], i + 1)
                    if n >= 2:
                        pool.wait_ge(S["dec"], i * NGD + n - 1)
                    elif not first:
                        pool.wait_ge(S["dec"], i * NGD)
                    pool.tensor_tensor(v3(gs[:, n % 2, :]), bc(R.m(M_STRIU if n % DIRS else M_STRIL), TG),
                                       gh[:, G_DECAY, n * TG:(n + 1) * TG, 0:1].broadcast_to([P, TG, P]),
                                       ALU.mult).then_inc(S["gs"], 1)

                def mask_decays(n):
                    ns = slice(n * GW, (n + 1) * GW)
                    pool.wait_ge(S["dexp"], i * NGD + n + 1)
                    pool.tensor_tensor(v3(ework[:, ns]), v3(ework[:, ns]),
                                       bc(R.m(M_TRIU if n % DIRS else M_TRIL), TG), ALU.mult).then_inc(S["dmask"], 1)

                for n in range(NGD):
                    steps(n)
                    if n >= 3:
                        mask_decays(n - 3)
                for n in range(NGD - 3, NGD):
                    if n == NGD - 1:
                        pool.wait_ge(S["l_raw"], i * NGD + 3)
                    mask_decays(n)

                def diagonal(n):
                    ns = slice(n * GW, (n + 1) * GW)
                    pool.affine_select(out=v3(lmat[:, ns]), in_=v3(lmat[:, ns]), compare_op=ALU.not_equal, fill=one,
                                       base=0, pattern=[[0, TG], [-1, P]], channel_multiplier=1
                                       ).then_inc(S["l_done"], 1)

                def first_inverse(n):
                    ns = slice(n * GW, (n + 1) * GW)
                    pool.wait_ge(S["l_done"], i * NGD + n + 1)
                    pool.tensor_tensor(v3(xmat[:, ns]), v3(lmat[:, ns]), bc(R.level(0, 1 - n % DIRS), TG),
                                       ALU.mult).then_inc(S["x0"], 1)

                for n in range(3):
                    diagonal(n)
                pool.wait_ge(S["l_raw"], i * NGD + NGD)
                first_inverse(0)
                for n in range(3, NGD):
                    diagonal(n)
                for n in range(1, NGD):
                    first_inverse(n)
                if not last:
                    for k in (1, 2):
                        low(i * PERW + PRE + k, (PRE + k) % 2)
                for n in range(NGD):
                    ns = slice(n * GW, (n + 1) * GW)
                    pool.wait_ge(S["yb"], i * NGD + n + 1)
                    pool.tensor_tensor(v3(rwork[:, ns]), v3(ymat[:, ns]),
                                       gh[:, G_EXPCUM, n * TG:(n + 1) * TG, 0:1].broadcast_to([P, TG, P]),
                                       ALU.mult).then_inc(S["ybe"], 1)
                if not last:
                    low(i * PERW + PRE + 3, (PRE + 3) % 2)
                    low(i * PERW + PRE + 4, (PRE + 4) % 2)
                    rsqrt_k(i + 1)
                pool.wait_ge(S["osum"], i + 1)
                pool.tensor_tensor(ro[:, :], sso[:, :], mhalf[:, :], ALU.pow).then_inc(S["ro"], 1)

            turns(pool, turn)

        @block.scalar
        def _(act):
            def high(j, slot, mm):
                act.wait_ge(S["w_in"], 16 * j + 16)
                if mm is not None:
                    act.wait_ge(S["proj_mm"], mm)
                act.activation(whi[:, slot], wst[:, :, :], ACT.Copy).then_inc(S["w_hi"], 1)

            def evac(gidx, par, c, g):
                act.wait_ge(S["proj_mm"], gidx + 1)
                src = proj[par]
                if c is None:
                    act.activation(zraw[:, g * GW:(g + 1) * GW], src[:, 0:GW], ACT.Copy).then_inc(S["proj_out"], 1)
                elif g == 0:
                    act.activation(raw[:, c, PAD_L:PAD_L + CTX], src[:, 0:CTX], ACT.Copy)
                    act.activation(raw[:, c, PAD_L + LAT0:PAD_L + LAT0 + GW - CTX], src[:, CTX:GW],
                                   ACT.Copy).then_inc(S["proj_out"], 1)
                else:
                    at = PAD_L + GAP + g * GW
                    act.activation(raw[:, c, at:at + GW], src[:, 0:GW], ACT.Copy).then_inc(S["proj_out"], 1)

            act.wait_ge(S["pads"], 1)
            high(0, 0, None)
            high(1, 1, None)
            def silu_tanh(h, s):
                act.wait_ge(S["taps"], h * 3 + s + 1)
                act.activation(cb_, (ca, cd, q2[:, :])[s], ACT.Tanh, scale=0.5).then_inc(S["silu_t"], 1)

            def square(h, s):
                act.wait_ge(S["silu"], h * 3 + s + 1)
                src, dst = (ca, cc) if s == 0 else (q2[:, :], cb_)
                act.activation(dst, src, ACT.Square).then_inc(S["sq"], 1)

            for j in range(PRE):
                for g in range(NG):
                    evac(j * NG + g, (j * NG + g) % 2, j, g)
                if j < 2:
                    high(j + 2, j, (j + 1) * NG)
                if j == 1:
                    silu_tanh(0, 0)
                    square(0, 0)
            silu_tanh(0, 1)

            def turn(i, first, last):
                base = i * g_ + PRE * NG
                if not first:
                    act.wait_ge(S["fin"], i * NG)
                for g in range(2):
                    evac(base + g, (PRE * NG + g) % 2, None, g)
                for g in range(NG):
                    act.wait_ge(S["vt"], i * NG + g + 1)
                    act.activation(vt[:, TG * g:TG * (g + 1), :], v3(bank[g][:, 0:GW]), ACT.Copy,
                                   scale=0.5).then_inc(S["vt_out"], 1)
                evac(base + 2, (PRE * NG + 2) % 2, None, 2)
                for g in range(NG):
                    act.wait_ge(S["knt"], i * NG + g + 1)
                    act.activation(kacc[:, TG * g:TG * (g + 1), :], v3(bank[KB[g]][:, 0:GW]),
                                   ACT.Copy).then_inc(S["knt_out"], 1)
                if not first:
                    act.wait_ge(S["oa_store"], i * 16)
                for n in range(NGD):
                    act.wait_ge(S["dec"], i * NGD + n + 1)
                    act.activation(ework[:, n * GW:(n + 1) * GW], bank[n % 2][:, 0:GW], ACT.Exp).then_inc(S["dexp"], 1)
                    if n == 1:
                        silu_tanh(i, 2)
                    elif n == 3:
                        square(i, 2)
                if not last:
                    high(i * PERW + PRE + 1, (PRE + 1) % 2, i * g_ + PRE * NG)
                for lev in range(levels - 1):
                    if lev == 2 and not last:
                        high(i * PERW + PRE + 2, (PRE + 2) % 2, base + NG)
                    for n in range(NGD):
                        idx, ns = lev * NGD + n, slice(n * GW, (n + 1) * GW)
                        act.wait_ge(S["xy"], i * levels * NGD + idx + 1)
                        act.activation(ymat[:, ns], bank[4 + n % 2][:, 0:GW], ACT.Copy).then_inc(S["y_out"], 1)
                        act.activation(xmat[:, ns], bank[2 + n % 2][:, 0:GW], ACT.Copy).then_inc(S["x_out"], 1)
                for n in range(NGD):
                    act.wait_ge(S["nw"], i * NGD + n + 1)
                    act.activation(xmat[:, n * GW:(n + 1) * GW], bank[n % 2][:, 0:GW], ACT.Copy,
                                   scale=-1.0).then_inc(S["nw_out"], 1)
                for s in range(NT):
                    act.wait_ge(S["vnew"], i * NT + s + 1)
                    if s < NT - 1:
                        act.wait_ge(S["vk_out"], i * (NT - 1) + s + 1)
                    act.activation(vn[:, s % 2], bank[s % 2][:, 0:2 * P].rearrange("p (d v) -> p d v", d=DIRS),
                                   ACT.Copy).then_inc(S["vn_out"], 1)
                    if s == 0:
                        act.wait_ge(S["su"], i * (NT - 1) + 1)
                        if not first:
                            act.wait_ge(S["st_store"], i * 16 * DIRS)
                        act.activation(state0[:, :, :], bank[4][:, 0:2 * P].rearrange("p (d v) -> p d v", d=DIRS),
                                       ACT.Copy).then_inc(S["st0"], 1)
                    if not last:
                        if s == 5:
                            silu_tanh(i + 1, 0)
                        elif s == 6:
                            square(i + 1, 0)
                        elif s == 8:
                            silu_tanh(i + 1, 1)
                        c, g = s // NG, s % NG
                        evac(base + NG + s, (PRE * NG + NG + s) % 2, c, g)
                        if s == NG - 1:
                            high(i * PERW + PRE + 3, (PRE + 3) % 2, base + 2 * NG)
                        elif s == 6:
                            high(i * PERW + PRE + 4, (PRE + 4) % 2, base + 3 * NG)
                act.wait_ge(S["acc"], i * NT + NT)
                if not last:
                    act.wait_ge(S["silu"], i * 3 + 5)
                act.activation(cb_[:, 0:TOK], kacc[:, :, :].rearrange("p t c -> p (t c)"),
                               ACT.Square).then_inc(S["osq"], 1)
                if not last:
                    act.wait_ge(S["ss_mm"], i * 2 + 3)
                act.wait_ge(S["proj_out"], base + NG)
                act.activation(cc[:, 0:TOK], zraw[:, :], ACT.Tanh, scale=0.5).then_inc(S["z_t"], 1)

            turns(act, turn)

        @block.tensor
        def _(pe):
            ident = R.m(M_ID)

            def project(gidx, par, slot, g, ks):
                ts = slice(g * GW, (g + 1) * GW)
                for k in ks:
                    mm = split_product(pe, proj[par][:, 0:GW], whi[:, slot, k, :], wlo[:, slot, k, :],
                                       R.hhi[:, k, ts], R.hlo[:, k, ts], k, k == KT - 1)
                if ks[-1] == KT - 1:
                    mm.then_inc(S["proj_mm"], 1)

            for j in range(PRE):
                pe.wait_ge(S["w_lo"], j + 1)
                for g in range(NG):
                    n = j * NG + g
                    if n >= 2:
                        pe.wait_ge(S["proj_out"], n - 1)
                    project(n, n % 2, j % 2, g, range(KT))

            def sums(h, at, src):
                pe.wait_ge(S["sq"], h)
                for t in range(NT):
                    mm = pe.matmul(at[:, t:t + 1], src[:, tile_at(t):tile_at(t) + P],
                                   R.masks[:, M_ONE * P:M_ONE * P + 1], start=True, stop=True)
                mm.then_inc(S["ss_mm"], 1)

            def z_groups(h, gs_):
                pe.wait_ge(S["w_lo"], h * PERW + PRE + 1)
                for g in gs_:
                    pe.wait_ge(S["proj_out"], h * g_ + (PRE * NG + g - 1))
                    project(None, (PRE * NG + g) % 2, PRE % 2, g, range(KT))

            z_groups(0, (0, 1))
            sums(1, bank[3], cc)

            def turn(i, first, last):
                base = i * g_ + PRE * NG
                pe.wait_ge(S["silu"], i * 3 + 2)
                for t in range(NT):
                    if t == 2 * TG:
                        pe.wait_ge(S["ssk"], i + 1)
                    mm = pe.transpose(bank[KB[t // TG]][:, (t % TG) * P:(t % TG + 1) * P],
                                      ca[:, tile_at(t):tile_at(t) + P], ident)
                    if t % TG == TG - 1:
                        mm.then_inc(S["kt"], 1)
                if not first:
                    pe.wait_ge(S["fin"], i * NG)
                for t in range(NT):
                    mm = pe.transpose(bank[t // TG][:, (t % TG) * P:(t % TG + 1) * P],
                                      cd[:, tile_at(t):tile_at(t) + P], ident)
                    if t % TG == TG - 1:
                        mm.then_inc(S["vt"], 1)
                z_groups(i, (2,))
                for t in range(NT):
                    if t % TG == 0:
                        pe.wait_ge(S["kn"], i * NG + t // TG + 1)
                    mm = pe.transpose(bank[KB[t // TG]][:, (t % TG) * P:(t % TG + 1) * P], kn[:, t, :], ident)
                    if t % TG == TG - 1:
                        mm.then_inc(S["knt"], 1)
                pe.wait_ge(S["vt_out"], i * NG + NG)
                for g in range(NG):
                    for d in range(DIRS):
                        n = g * DIRS + d
                        pe.wait_ge(S["gs"], i * NGD + n + 1)
                        if g:
                            pe.wait_ge(S["dexp"], i * NGD + n - 1)
                        pe.matmul(bank[d][:, 0:GW], R.m(M_TRIL if d else M_TRIU), gs[:, n % 2, :],
                                  start=True, stop=True).then_inc(S["dec"], 1)
                    if g == 0:
                        pe.wait_ge(S["knt_out"], i * NG + NG)
                    if g == 2:
                        pe.wait_ge(S["l_raw"], i * NGD + DIRS)
                    for j in range(TG):
                        t, js = TG * g + j, slice(j * P, (j + 1) * P)
                        mm = pe.matmul(bank[2 + g % 2][:, js], kacc[:, t, :], kacc[:, t, :], start=True, stop=True)
                    mm.then_inc(S["kk"], 1)
                pe.wait_ge(S["silu"], i * 3 + 3)
                for g in range(NG):
                    if g == 2:
                        pe.wait_ge(S["proj_out"], base + NG)
                        sums(i * 2 + 2, bank[6], cb_)
                        pe.wait_ge(S["qk"], i * NGD + DIRS)
                    for j in range(TG):
                        t, js = TG * g + j, slice(j * P, (j + 1) * P)
                        mm = pe.matmul(bank[4 + g % 2][:, js], q2[:, tile_at(t):tile_at(t) + P], kacc[:, t, :],
                                       start=True, stop=True)
                    mm.then_inc(S["gq"], 1)
                pe.wait_ge(S["dexp"], i * NGD + NGD)
                for n in range(NGD):
                    pe.wait_ge(S["l_done"], i * NGD + n + 1)
                    if n >= 2:
                        pe.wait_ge(S["y0"], i * NGD + n - 1)
                    for j in range(TG):
                        sl = slice((n * TG + j) * P, (n * TG + j + 1) * P)
                        mm = pe.transpose(bank[n % 2][:, j * P:(j + 1) * P], lmat[:, sl], ident)
                    mm.then_inc(S["lt"], 1)

                def factor(lev, n):
                    idx = lev * NGD + n
                    if lev == 0:
                        pe.wait_ge(S["y0"], i * NGD + min(NGD, n + NGD - 1))
                    else:
                        pe.wait_ge(S["y_out"], i * (levels - 1) * NGD + idx - NGD + 1)
                    if idx >= 2:
                        pe.wait_ge(S["r_out"], i * levels * NGD + idx - 1)
                    for j in range(TG):
                        sl = slice((n * TG + j) * P, (n * TG + j + 1) * P)
                        mm = pe.matmul(bank[n % 2][:, j * P:(j + 1) * P], lmat[:, sl], ymat[:, sl],
                                       start=True, stop=True)
                    mm.then_inc(S["r"], 1)

                def update(lev, n):
                    idx = lev * NGD + n
                    pe.wait_ge(S["r_out"], i * levels * NGD + idx + 1)
                    if lev == 0:
                        pe.wait_ge(S["x0"], i * NGD + n + 1)
                        if n == 0:
                            pe.wait_ge(S["qk"], i * NGD + NGD)
                    if idx >= 2:
                        pe.wait_ge(S["x_out"], i * (levels - 1) * NGD + (idx - 1 if lev < levels - 1 else (levels - 1) * NGD))
                    if lev == levels - 1 and n >= 2:
                        pe.wait_ge(S["yb"], i * NGD + n - 1)
                    for j in range(TG):
                        sl, js = slice((n * TG + j) * P, (n * TG + j + 1) * P), slice(j * P, (j + 1) * P)
                        if lev < levels - 1:
                            pe.matmul(bank[2 + n % 2][:, js], rwork[:, sl], xmat[:, sl], start=True, stop=True)
                        mm = pe.matmul(bank[4 + n % 2][:, js], xmat[:, sl], rwork[:, sl], start=True, stop=True)
                    mm.then_inc(S["xy"], 1)

                for lev in range(levels):
                    factor(lev, 0)
                    for n in range(1, NGD):
                        factor(lev, n)
                        update(lev, n - 1)
                    update(lev, NGD - 1)
                for n in range(NGD):
                    if n >= 2:
                        pe.wait_ge(S["qt_out"], i * NGD + n - 1)
                    for j in range(TG):
                        sl = slice((n * TG + j) * P, (n * TG + j + 1) * P)
                        mm = pe.transpose(bank[2 + n % 2][:, j * P:(j + 1) * P], ework[:, sl], ident)
                    mm.then_inc(S["qt"], 1)
                for n in range(NGD):
                    pe.wait_ge(S["ybe"], i * NGD + n + 1)
                    if n >= 2:
                        pe.wait_ge(S["nw_out"], i * NGD + n - 1)
                    for j in range(TG):
                        t = TG * (n // DIRS) + j
                        sl = slice((n * TG + j) * P, (n * TG + j + 1) * P)
                        mm = pe.matmul(bank[n % 2][:, j * P:(j + 1) * P], kn[:, t, :], rwork[:, sl],
                                       start=True, stop=True)
                    mm.then_inc(S["nw"], 1)
                pe.wait_ge(S["nw_out"], i * NGD + NGD)
                pe.wait_ge(S["qt_out"], i * NGD + NGD)
                pe.wait_ge(S["st_in"], i * 16 * DIRS + 16 * DIRS)
                for s in range(NT):
                    b0, b1, b2 = bank[s % 2], bank[2 + s % 2], bank[4 + s % 2]
                    place = [step_tile(s, d) for d in range(DIRS)]
                    if s >= 2:
                        pe.wait_ge(S["st_new"], i * (NT - 2) + s - 1)
                        pe.wait_ge(S["acc"], i * NT + s - 1)
                    for d, (t, n) in enumerate(place):
                        sl, ds_ = slice(n * P, (n + 1) * P), slice(d * P, (d + 1) * P)
                        mm = pe.matmul(b0[:, ds_], ymat[:, sl], vt[:, t, :], start=True, stop=(s == 0))
                        if s:
                            mm = pe.matmul(b0[:, ds_], xmat[:, sl], state[:, d, :], start=False, stop=True)
                    mm.then_inc(S["vnew"], 1)
                    if s:
                        for d, (t, n) in enumerate(place):
                            pe.matmul(b1[:, d * P:(d + 1) * P], q2[:, tile_at(t):tile_at(t) + P], state[:, d, :],
                                      start=True, stop=True)
                    if not last:
                        slot, par = (PRE + 1 + s // NG) % 2, (PRE * NG + NG + s) % 2
                        if s % NG == 0:
                            pe.wait_ge(S["w_lo"], i * PERW + PRE + 2 + s // NG)
                        pe.wait_ge(S["proj_out"], base + NG + s - 1)
                        project(None, par, slot, s % NG, range(KT // 2))
                    if s < NT - 1:
                        pe.wait_ge(S["vk_out"], i * (NT - 1) + s + 1)
                        if s == 2:
                            pe.wait_ge(S["st0"], i + 1)
                        for d, (t, n) in enumerate(place):
                            mm = pe.matmul(b2[:, d * P:(d + 1) * P], kn[:, t, :], vk[:, s % 2, d, :],
                                           start=True, stop=True)
                        mm.then_inc(S["su"], 1)
                    pe.wait_ge(S["vn_out"], i * NT + s + 1)
                    for d, (t, n) in enumerate(place):
                        mm = pe.matmul(b1[:, (2 + d) * P:(3 + d) * P], lmat[:, n * P:(n + 1) * P], vn[:, s % 2, d, :],
                                       start=True, stop=True)
                    mm.then_inc(S["ov"], 1)
                    if not last:
                        project(None, par, slot, s % NG, range(KT // 2, KT))
                if not last:
                    pe.wait_ge(S["acc"], i * NT + NT - 1)
                    sums(i * 2 + 3, bank[3], cc)
                    z_groups(i + 1, (0, 1))
                pe.wait_ge(S["ofac"], i + 1)
                for t in range(NT):
                    mm = pe.transpose(bank[t // TG][:, (t % TG) * P:(t % TG + 1) * P], kacc[:, t, :], ident)
                    if t % TG == TG - 1:
                        mm.then_inc(S["ot"], 1)

            turns(pe, turn)

        @block.vector
        def _(dve):
            n_own = [0]

            def link(ins, turn):
                n_own[0] += 1
                ins.then_inc(S["own"], 1)
                dve.wait_ge(S["own"], n_own[0] if turn is None else turn * DVE_OWN + (OWN0 + n_own[0]))

            def taps_in(h, hs):
                dve.tensor_copy(cw[:, :, :, :], R.par[:, PA_CONV:PA_CONV + 120].rearrange(
                    "p (a b c) -> p a b c", a=5, b=3)[:, :, :, hs]).then_inc(S["cw"], 1)
                dve.wait_ge(S["cw"], h + 1)

            def conv(h, s, taps, turn):
                dst, c = (ca, cd, q2[:, :])[s], QKV[s]
                for a in taps:
                    if a == 0:
                        dve.wait_ge(S["proj_out"], h * g_ + (s + 1) * NG)
                        ins = dve.tensor_scalar(dst, raw[:, s, 0:CONV], cw[:, 0, c, 0:1], cw[:, 4, c, 0:1],
                                                ALU.mult, ALU.add)
                    else:
                        ins = dve.scalar_tensor_tensor(out=dst, in0=raw[:, s, a:a + CONV], scalar=cw[:, a, c, 0:1],
                                                       in1=dst, op0=ALU.mult, op1=ALU.add)
                    if a < TAPS - 1:
                        link(ins, turn)
                    else:
                        ins.then_inc(S["taps"], 1)

            def silu(h, s):
                dst = (ca, cd, q2[:, :])[s]
                dve.wait_ge(S["silu_t"], h * 3 + s + 1)
                dve.scalar_tensor_tensor(out=dst, in0=cb_, scalar=1.0, in1=dst, op0=ALU.add,
                                         op1=ALU.mult).then_inc(S["silu"], 1)

            def norm_k(h):
                dve.wait_ge(S["ss_mm"], h * 2 + 1)
                dve.tensor_scalar(ssk[:, :], bank[3][:, 0:NT], 4 * EPS, None, ALU.add).then_inc(S["ssk"], 1)

            taps_in(0, slice(0, 1))
            for s in range(2):
                conv(0, s, range(TAPS), None)
                silu(0, s)
            norm_k(0)
            OWN0 = n_own[0]

            def turn(i, first, last):
                n_own[0] = 0
                hs = slice(i, i + 1) if first or last else bass.ds(i, 1)
                if not first:
                    dve.wait_ge(S["ybe"], i * NGD)
                dve.tensor_copy(gh[:, :, :, :], R.gates[:, :, :, hs]).then_inc(S["par"], 1)
                dve.wait_ge(S["par"], i + 1)
                dve.wait_ge(S["rk"], i + 1)
                for g in range(NG):
                    dve.wait_ge(S["kt"], i * NG + g + 1)
                    gsl = slice(TG * g, TG * (g + 1))
                    dve.tensor_tensor(kn[:, gsl, :], v3(bank[KB[g]][:, 0:GW]), cols(rk[:, gsl], TG),
                                      ALU.mult).then_inc(S["kn"], 1)
                conv(i, 2, range(TAPS), i)
                for n in range(NGD):
                    g = n // DIRS
                    dve.wait_ge(S["dmask"], i * NGD + n + 1)
                    dve.wait_ge(S["kk"], i * NG + g + 1)
                    for j in range(TG):
                        sl = slice((n * TG + j) * P, (n * TG + j + 1) * P)
                        ins = dve.scalar_tensor_tensor(out=lmat[:, sl], in0=bank[2 + g % 2][:, j * P:(j + 1) * P],
                                                       scalar=gh[:, G_BETA, n * TG + j, 0:1], in1=ework[:, sl],
                                                       op0=ALU.mult, op1=ALU.mult)
                    ins.then_inc(S["l_raw"], 1)
                    if n == 1:
                        silu(i, 2)
                dve.wait_ge(S["l_raw"], i * NGD + NGD)
                for n in range(NGD):
                    g, ns = n // DIRS, slice(n * GW, (n + 1) * GW)
                    dve.wait_ge(S["gq"], i * NG + g + 1)
                    dve.tensor_tensor(ework[:, ns], bank[4 + g % 2][:, 0:GW], ework[:, ns], ALU.mult
                                      ).then_inc(S["qk"], 1)
                dve.wait_ge(S["ss_mm"], i * 2 + 2)
                dve.tensor_scalar(ssq[:, :], bank[6][:, 0:NT], P * EPS, P * EPS * 4 * EPS, ALU.mult,
                                  ALU.add).then_inc(S["ssq"], 1)
                for n in range(NGD):
                    dve.wait_ge(S["lt"], i * NGD + n + 1)
                    dve.tensor_tensor(v3(ymat[:, n * GW:(n + 1) * GW]), v3(bank[n % 2][:, 0:GW]),
                                      bc(R.level(0, n % DIRS), TG), ALU.mult).then_inc(S["y0"], 1)
                for lev in range(levels):
                    for n in range(NGD):
                        idx = lev * NGD + n
                        dve.wait_ge(S["r"], i * levels * NGD + idx + 1)
                        if lev:
                            dve.wait_ge(S["xy"], i * levels * NGD + idx - NGD + 1)
                        dve.tensor_tensor(v3(rwork[:, n * GW:(n + 1) * GW]), v3(bank[n % 2][:, 0:GW]),
                                          bc(R.level(lev + 1, n % DIRS), TG), ALU.mult).then_inc(S["r_out"], 1)
                        if lev == levels - 1 and n:
                            inverse_out(i, n - 1)
                inverse_out(i, NGD - 1)
                for n in range(NGD):
                    dve.wait_ge(S["qt"], i * NGD + n + 1)
                    dve.tensor_copy(lmat[:, n * GW:(n + 1) * GW], bank[2 + n % 2][:, 0:GW]).then_inc(S["qt_out"], 1)
                for s in range(NT):
                    b0, b1, b2 = bank[s % 2], bank[2 + s % 2], bank[4 + s % 2]
                    place = [step_tile(s, d) for d in range(DIRS)]
                    if s < NT - 1:
                        dve.wait_ge(S["vnew"], i * NT + s + 1)
                        for d, (t, n) in enumerate(place):
                            ins = dve.tensor_scalar(vk[:, s % 2, d, :], b0[:, d * P:(d + 1) * P],
                                                    gh[:, G_EXPREST, n, 0:1], None, ALU.mult)
                        ins.then_inc(S["vk_out"], 1)
                        if s:
                            dve.wait_ge(S["su"], i * (NT - 1) + s + 1)
                            if s >= 2:
                                dve.wait_ge(S["st_new"], i * (NT - 2) + s - 1)
                            for d, (t, n) in enumerate(place):
                                ins = dve.scalar_tensor_tensor(out=state[:, d, :], in0=state[:, d, :],
                                                               scalar=gh[:, G_EXPALL, n, 0:1],
                                                               in1=b2[:, d * P:(d + 1) * P], op0=ALU.mult, op1=ALU.add)
                            ins.then_inc(S["st_new"], 1)
                    dve.wait_ge(S["ov"], i * NT + s + 1)
                    if s:
                        for d, (t, n) in enumerate(place):
                            eg = gh[:, G_EXPCUM, n, 0:1]
                            if s <= NT // 2:
                                ins = dve.tensor_scalar(kacc[:, t, :], b1[:, d * P:(d + 1) * P], eg, None, ALU.mult)
                            else:
                                ins = dve.scalar_tensor_tensor(out=kacc[:, t, :], in0=b1[:, d * P:(d + 1) * P], scalar=eg,
                                                               in1=kacc[:, t, :], op0=ALU.mult, op1=ALU.add)
                        link(ins, i)
                        for d, (t, n) in enumerate(place):
                            ins = dve.tensor_tensor(kacc[:, t, :], b1[:, (2 + d) * P:(3 + d) * P], kacc[:, t, :], ALU.add)
                        ins.then_inc(S["acc"], 1)
                        dve.wait_ge(S["acc"], i * NT + s + 1)
                    else:
                        link(dve.tensor_copy(kacc[:, 0, :], b1[:, 2 * P:3 * P]), i)
                        dve.tensor_tensor(kacc[:, 0, :], b1[:, 3 * P:4 * P], kacc[:, 0, :], ALU.add).then_inc(S["acc"], 1)
                    if not last:
                        if s == 2:
                            taps_in(i + 1, slice(1, 2) if first else bass.ds(i + 1, 1))
                        elif s == 5:
                            silu(i + 1, 0)
                        elif s == 8:
                            silu(i + 1, 1)
                            norm_k(i + 1)
                        elif s > 2:
                            conv(i + 1, s // 5, ((0, 1), (2, 3))[(s - 3) % 3], i)
                dve.wait_ge(S["osq"], i + 1)
                link(dve.tensor_reduce(sso[:, :], v3(cb_[:, 0:TOK]), AX.X, ALU.add), i)
                dve.scalar_tensor_tensor(out=sso[:, :], in0=sso[:, :], scalar=1.0 / P, in1=ssq[:, :], op0=ALU.mult,
                                         op1=ALU.add).then_inc(S["osum"], 1)
                dve.wait_ge(S["ro"], i + 1)
                dve.tensor_tensor(kacc[:, :, :], kacc[:, :, :], cols(ro[:, :], NT), ALU.mult).then_inc(S["ofac"], 1)
                dve.wait_ge(S["z_t"], i + 1)
                link(dve.scalar_tensor_tensor(out=zraw[:, :], in0=cc[:, 0:TOK], scalar=1.0, in1=zraw[:, :],
                                              op0=ALU.add, op1=ALU.mult), i)
                for g in range(NG):
                    gsl = slice(g * GW, (g + 1) * GW)
                    dve.wait_ge(S["ot"], i * NG + g + 1)
                    dve.scalar_tensor_tensor(out=cc[:, gsl], in0=bank[g][:, 0:GW], scalar=R.par[:, PB_ONORM:PB_ONORM + 1],
                                             in1=zraw[:, gsl], op0=ALU.mult, op1=ALU.mult).then_inc(S["fin"], 1)
                assert last or n_own[0] == DVE_OWN

            def inverse_out(i, n):
                dve.wait_ge(S["xy"], i * levels * NGD + (levels - 1) * NGD + n + 1)
                dve.tensor_tensor(v3(ymat[:, n * GW:(n + 1) * GW]), v3(bank[4 + n % 2][:, 0:GW]),
                                  gh[:, G_BETA, n * TG:(n + 1) * TG, 0:1].broadcast_to([P, TG, P]),
                                  ALU.mult).then_inc(S["yb"], 1)

            DVE_OWN = 3 * (TAPS - 1) + NT + 2
            turns(dve, turn)


def step_tile(s, d):
    t = s if (s == 0 or d == 0) else NT - s
    return t, (t // TG * DIRS + d) * TG + t % TG


def lru_stage(nc, R, A, ob):
    with ExitStack() as ctx:
        sb = lambda name, shape, dt=F32: ctx.enter_context(nc.sbuf_tensor(name, shape, dt))
        sem = lambda name: ctx.enter_context(nc.semaphore(name))
        wst = sb("l_w", [P, 2, KT, P])
        whi = sb("l_w_hi", [P, 2, KT, P], F32R)
        wlo = sb("l_w_lo", [P, 2, KT, P], F32R)
        gw = sb("l_gate_w", [P, 4, P])
        raw = sb("l_raw", [P, RAW])
        zraw = sb("l_z", [P, TOK])
        z2 = sb("l_z2", [P, TOK])
        xc = sb("l_xc", [P, CONV])
        tg = sb("l_tg", [P, 4, CONV])
        a = sb("l_a", [P, DIRS, CONV])
        th = sb("l_th", [P, DIRS, CONV])
        out = sb("l_out", [P, TOK])
        lp = sb("l_par", [P, NLP, 1])
        rate = sb("l_rate", [P, 2, DIRS, 1])
        h0 = sb("l_h0", [P, DIRS, 1])
        nb = sb("l_newb", [DIRS * H, P])
        bank = [ctx.enter_context(nc.psum_tensor(f"lb{i}", [P, 512], F32)) for i in range(8)]
        proj = bank[6:8]
        S = {n: sem("l_" + n) for n in (
            "w_in0", "w_in1", "gw_in", "w_hi", "w_lo", "proj_mm", "proj_out", "pads", "par", "taps", "own", "gate_mm", "gate_t",
            "z_t", "z2", "a", "th", "a2", "m", "root", "p", "b", "scan", "states", "out", "store", "nb_t", "nb")}
        block = ctx.enter_context(nc.Block())
        w_in = A["w_in"][0].rearrange("(k p) n -> p k n", p=P)
        gate_w = [A[n][0] for n in ("lru_wa_fwd", "lru_wx_fwd", "lru_wa_bwd", "lru_wx_bwd")]
        PER = 2
        g_ = PER * NG
        GN = CONV // NG
        NGATE = 4 * NG

        def turns(eng, body):
            body(0, True, False)
            with eng.Fori(1, H - 1) as i:
                body(i, False, False)
            body(H - 1, False, True)

        @block.sync
        def _(sp):
            for j in range(PER):
                sp.dma_start(wst[:, j, :, :], w_in[:, :, bass.ds((4 + j) * D, P)]).then_inc(S[f"w_in{j}"], 16)
            for k in range(4):
                sp.dma_start(gw[:, k, :], gate_w[k][0]).then_inc(S["gw_in"], 16)
            for j in range(PER):
                sp.wait_ge(S["w_lo"], j + 1)
                sp.dma_start(wst[:, j, :, :], w_in[:, :, bass.ds((4 + j) * D + P, P)]).then_inc(S[f"w_in{j}"], 16)

            def turn(i, ahead):
                val = int if isinstance(i, int) else sp.snap
                outs, row = val(i * 2 + 2), val(i * P)
                if ahead > 1:
                    c = [val(i * P + ((4 + j) * D + 2 * P)) for j in range(PER)]
                    need = [val(i * PER + PER + j + 1) for j in range(PER)]
                    for j in range(PER):
                        sp.wait_ge(S["w_lo"], need[j])
                        sp.dma_start(wst[:, j, :, :], w_in[:, :, bass.ds(c[j], P)]).then_inc(S[f"w_in{j}"], 16)
                if ahead > 0:
                    nxt, gm = val(i * 1 + 1), val(i * NGATE + NGATE)
                    sp.wait_ge(S["gate_mm"], gm)
                    for k in range(4):
                        sp.dma_start(gw[:, k, :], gate_w[k][bass.ds(nxt, 1)].rearrange("a i j -> i (a j)")
                                     ).then_inc(S["gw_in"], 16)
                sp.wait_ge(S["out"], outs)
                sp.dma_start(ob[bass.ds(row, P), :], out[:, :]).then_inc(S["store"], 16)

            turn(0, 2)
            with sp.Fori(1, H - 2) as i:
                turn(i, 2)
            turn(H - 2, 1)
            turn(H - 1, 0)
            for d, name in enumerate(("new_bf", "new_bb")):
                sp.wait_ge(S["nb"], 1)
                sp.dma_start(A[name][0, 0].rearrange("(r p) -> r p", p=P), nb[d * H:(d + 1) * H, :]
                             ).then_inc(S["store"], 16)
            sp.wait_ge(S["store"], 16 * (H + DIRS))

        @block.gpsimd
        def _(pool):
            pool.memset(raw[:, 0:PAD_L], 0.0)
            pool.memset(raw[:, PAD_L + CTX:PAD_L + CTX + GAP], 0.0)
            pool.memset(raw[:, RAW - 1:RAW], 0.0).then_inc(S["pads"], 1)

            def low(j, slot):
                pool.wait_ge(S["w_hi"], j + 1)
                pool.tensor_tensor(wlo[:, slot], wst[:, slot], whi[:, slot].bitcast(F32),
                                   ALU.subtract).then_inc(S["w_lo"], 1)

            for j in range(PER):
                low(j, j)

            def turn(i, first, last):
                if not last:
                    for j in range(PER):
                        low(i * PER + PER + j, j)

            turns(pool, turn)

        @block.scalar
        def _(act):
            def high(turn, slot, mm):
                act.wait_ge(S[f"w_in{slot}"], 16 * turn + 16)
                if mm is not None:
                    act.wait_ge(S["proj_mm"], mm)
                act.activation(whi[:, slot], wst[:, slot], ACT.Copy).then_inc(S["w_hi"], 1)

            def evac(gidx, par, q):
                act.wait_ge(S["proj_mm"], gidx + 1)
                g, src = q % NG, proj[par]
                if q >= NG:
                    act.activation(zraw[:, g * GW:(g + 1) * GW], src[:, 0:GW], ACT.Copy).then_inc(S["proj_out"], 1)
                    return
                if g == 0:
                    act.activation(raw[:, PAD_L:PAD_L + CTX], src[:, 0:CTX], ACT.Copy)
                t0 = max(g * GW, CTX)
                r0, r1 = (t0 - CTX) // GRID_W, ((g + 1) * GW - CTX) // GRID_W
                lat = raw[:, PAD_L + LAT0:PAD_L + LAT0 + LAT].rearrange("p (w r) -> p r w", r=GRID_R)
                act.activation(lat[:, r0:r1, :], src[:, t0 - g * GW:GW].rearrange("p (r w) -> p r w", w=GRID_W),
                               ACT.Copy).then_inc(S["proj_out"], 1)

            act.wait_ge(S["pads"], 1)
            for j in range(PER):
                high(0, j, None)
            for q in range(g_):
                evac(q, q % 2, q)

            def turn(i, first, last):
                base = i * g_ + g_
                if not last:
                    for j in range(PER):
                        high(i + 1, j, i * g_ + (j + 1) * NG)
                if not first:
                    act.wait_ge(S["z2"], i)
                if not first:
                    act.wait_ge(S["b"], i * DIRS)
                act.wait_ge(S["proj_out"], base)
                act.activation(th[:, 0, 0:TOK], zraw[:, :], ACT.Tanh, scale=0.5).then_inc(S["z_t"], 1)
                act.wait_ge(S["taps"], i + 1)
                if not first:
                    act.wait_ge(S["scan"], i * 4)
                if not first:
                    act.wait_ge(S["out"], i * 2)
                for n in range(NGATE):
                    kind, g = n % 4, n // 4
                    act.wait_ge(S["gate_mm"], i * NGATE + n + 1)
                    act.activation(tg[:, kind, g * GN:(g + 1) * GN], bank[n % 6][:, 0:GN], ACT.Tanh, scale=0.5,
                                   bias=lp[:, 5 + kind, 0:1]).then_inc(S["gate_t"], 1)
                act.wait_ge(S["gate_t"], i * NGATE + NGATE)
                act.wait_ge(S["z2"], i + 1)
                for d in range(DIRS):
                    act.activation(a[:, d, :], tg[:, 2 * d, :], ACT.Exp, scale=rate[:, 1, d, 0:1],
                                   bias=rate[:, 1, d, 0:1]).then_inc(S["a"], 1)
                    act.activation(th[:, d, :], tg[:, 2 * d, :], ACT.Tanh, scale=rate[:, 0, d, 0:1],
                                   bias=rate[:, 0, d, 0:1]).then_inc(S["th"], 1)
                if not last:
                    evac(base, 0, 0)
                for d in range(DIRS):
                    act.wait_ge(S["a"], i * DIRS + d + 1)
                    act.wait_ge(S["th"], i * DIRS + d + 1)
                    act.activation(tg[:, 2 * d, :], a[:, d, :], ACT.Square).then_inc(S["a2"], 1)
                if not last:
                    evac(base + 1, 1, 1)
                for d in range(DIRS):
                    act.wait_ge(S["m"], i * DIRS + d + 1)
                    act.activation(th[:, d, :], th[:, d, :], ACT.Sqrt, scale=0.25).then_inc(S["root"], 1)
                if not last:
                    for q in range(2, g_):
                        evac(base + q, q % 2, q)

            turns(act, turn)

        @block.tensor
        def _(pe):
            def project(base, q):
                slot, g = q // NG, q % NG
                ts = slice(g * GW, (g + 1) * GW)
                for k in range(KT):
                    mm = split_product(pe, proj[q % 2][:, 0:GW], whi[:, slot, k, :], wlo[:, slot, k, :],
                                       R.hhi[:, k, ts], R.hlo[:, k, ts], k, k == KT - 1)
                mm.then_inc(S["proj_mm"], 1)

            for q in range(g_):
                if q % NG == 0:
                    pe.wait_ge(S["w_lo"], q // NG + 1)
                if q >= 2:
                    pe.wait_ge(S["proj_out"], q - 1)
                project(0, q)

            def turn(i, first, last):
                base = i * g_ + g_
                for n in range(NGATE):
                    kind, g = n % 4, n // 4
                    if n == 0:
                        pe.wait_ge(S["taps"], i + 1)
                        pe.wait_ge(S["gw_in"], i * 64 + 64)
                    if n >= 6:
                        pe.wait_ge(S["gate_t"], i * NGATE + n - 5)
                    elif n == 0 and not first:
                        pe.wait_ge(S["gate_t"], i * NGATE)
                    pe.matmul(bank[n % 6][:, 0:GN], gw[:, kind, :], xc[:, g * GN:(g + 1) * GN],
                              start=True, stop=True).then_inc(S["gate_mm"], 1)
                if not last:
                    for q in range(g_):
                        if q % NG == 0:
                            pe.wait_ge(S["w_lo"], i * PER + PER + q // NG + 1)
                        pe.wait_ge(S["proj_out"], base + q - 1)
                        project(base, q)

            turns(pe, turn)
            pe.wait_ge(S["states"], H * DIRS)
            pe.transpose(bank[0][0:DIRS * H, 0:P], R.newb[:, :, :].rearrange("p d h -> p (d h)"),
                         R.m(M_ID)).then_inc(S["nb_t"], 1)

        @block.vector
        def _(dve):
            OWN = TAPS

            def turn(i, first, last):
                n_own = [0]

                def link(ins):
                    n_own[0] += 1
                    ins.then_inc(S["own"], 1)
                    dve.wait_ge(S["own"], i * OWN + n_own[0])

                hs = slice(i, i + 1) if first or last else bass.ds(i, 1)
                if not first:
                    dve.wait_ge(S["root"], i * DIRS)
                dve.tensor_copy(lp[:, :, :], R.par[:, PB_LRU:PB_LRU + NLP * H].rearrange(
                    "p (a c) -> p a c", c=H)[:, :, hs]).then_inc(S["par"], 1)
                dve.tensor_copy(rate[:, :, :, :], R.rate[:, :, :, hs]).then_inc(S["par"], 1)
                dve.tensor_copy(h0[:, :, :], R.par[:, PC + 16:PC + 32].rearrange(
                    "p (d c) -> p d c", c=H)[:, :, hs]).then_inc(S["par"], 1)
                dve.wait_ge(S["par"], i * 3 + 3)
                dve.wait_ge(S["proj_out"], i * g_ + NG)
                if not first:
                    dve.wait_ge(S["gate_mm"], i * NGATE)
                link(dve.tensor_scalar(xc[:, :], raw[:, 0:CONV], lp[:, 0, 0:1], lp[:, 4, 0:1], ALU.mult, ALU.add))
                for k in range(1, TAPS):
                    ins = dve.scalar_tensor_tensor(out=xc[:, :], in0=raw[:, k:k + CONV], scalar=lp[:, k, 0:1],
                                                   in1=xc[:, :], op0=ALU.mult, op1=ALU.add)
                    if k < TAPS - 1:
                        link(ins)
                ins.then_inc(S["taps"], 1)
                dve.wait_ge(S["z_t"], i + 1)
                if not first:
                    dve.wait_ge(S["out"], i * 2)
                dve.scalar_tensor_tensor(out=z2[:, :], in0=th[:, 0, 0:TOK], scalar=1.0, in1=zraw[:, :], op0=ALU.add,
                                         op1=ALU.mult).then_inc(S["z2"], 1)
                dve.wait_ge(S["gate_t"], i * NGATE + NGATE)
                dve.wait_ge(S["taps"], i + 1)
                for d in range(DIRS):
                    dve.scalar_tensor_tensor(out=tg[:, 2 * d + 1, :], in0=tg[:, 2 * d + 1, :], scalar=1.0,
                                             in1=xc[:, :], op0=ALU.add, op1=ALU.mult).then_inc(S["p"], 1)
                for d in range(DIRS):
                    dve.wait_ge(S["a2"], i * DIRS + d + 1)
                    dve.scalar_tensor_tensor(out=th[:, d, :], in0=tg[:, 2 * d, :], scalar=1.0, in1=th[:, d, :],
                                             op0=ALU.add, op1=ALU.mult).then_inc(S["m"], 1)
                for d in range(DIRS):
                    dve.wait_ge(S["root"], i * DIRS + d + 1)
                    dve.wait_ge(S["p"], i * DIRS + d + 1)
                    dve.tensor_tensor(tg[:, 2 * d + 1, :], tg[:, 2 * d + 1, :], th[:, d, :],
                                      ALU.mult).then_inc(S["b"], 1)
                for d in range(DIRS):
                    dve.wait_ge(S["b"], i * DIRS + d + 1)
                    for c0, c1, init in ((0, CTX, 0.0), (LAT0, CONV, h0[:, d, 0:1])):
                        rows = [v[:, c0:c1] if d == 0 else v[:, c0:c1][:, ::-1]
                                for v in (tg[:, 2 * d, :], a[:, d, :], tg[:, 2 * d + 1, :])]
                        dve.tensor_tensor_scan(rows[0], rows[1], rows[2], init, ALU.mult, ALU.add
                                               ).then_inc(S["scan"], 1)
                dve.wait_ge(S["scan"], i * 4 + 4)
                for d in range(DIRS):
                    end = CTX - 1 if d == 0 else 0
                    dve.tensor_copy(R.newb[:, d, hs], tg[:, 2 * d, end:end + 1]).then_inc(S["states"], 1)
                if not first:
                    dve.wait_ge(S["store"], i * 16)
                link(dve.tensor_tensor(tg[:, 1, :], tg[:, 0, :], tg[:, 2, :], ALU.add))
                dve.scalar_tensor_tensor(out=out[:, 0:CTX], in0=tg[:, 1, 0:CTX], scalar=0.5, in1=z2[:, 0:CTX],
                                         op0=ALU.mult, op1=ALU.mult).then_inc(S["out"], 1)
                rw = lambda v: v.rearrange("p (r w) -> p r w", w=GRID_W)
                dve.scalar_tensor_tensor(
                    out=rw(out[:, CTX:TOK]), in0=tg[:, 1, LAT0:CONV].rearrange("p (w r) -> p r w", r=GRID_R),
                    scalar=0.5, in1=rw(z2[:, CTX:TOK]), op0=ALU.mult, op1=ALU.mult).then_inc(S["out"], 1)
                assert n_own[0] == OWN

            turns(dve, turn)
            dve.wait_ge(S["nb_t"], 1)
            dve.tensor_copy(nb[:, :], bank[0][0:DIRS * H, 0:P]).then_inc(S["nb"], 1)


def merge_stage(nc, R, A, oa, ob, mixed):
    with ExitStack() as ctx:
        sb = lambda name, shape, dt=F32: ctx.enter_context(nc.sbuf_tensor(name, shape, dt))
        sem = lambda name: ctx.enter_context(nc.semaphore(name))
        NO = 3
        wst = sb("m_w", [P, 2, KT, P])
        whi = sb("m_w_hi", [P, 2, KT, P], F32R)
        wlo = sb("m_w_lo", [P, 2, KT, P], F32R)
        sgb = sb("m_gates", [P, KT, TOK])
        ost = sb("m_o", [P, NO, TOK])
        tmp = sb("m_tmp", [P, 2, GW])
        bg = sb("m_bias", [P, 2])
        bank = [ctx.enter_context(nc.psum_tensor(f"mb{i}", [P, 512], F32)) for i in range(8)]
        S = {n: sem("m_" + n) for n in ("w_in0", "w_in1", "w_hi", "w_lo", "mm", "gate", "bias", "o_in0", "o_in1",
                                        "o_in2", "o_hi", "o_lo", "fold", "mix")}
        block = ctx.enter_context(nc.Block())
        w_gate = A["w_gate"][0].rearrange("(k p) n -> p k n", p=P)
        w_br = [A[n][0].rearrange("(k p) n -> p k n", p=P) for n in ("w_proj_a", "w_proj_b")]
        NM_ = 2 * KT
        SKEW = 2

        @block.sync
        def _(sp):
            def load(src, col, slot, need):
                if need is not None:
                    sp.wait_ge(S["w_lo"], need)
                sp.dma_start(wst[:, slot, :, :], src[:, :, bass.ds(col, P)]).then_inc(S[f"w_in{slot}"], 16)

            load(w_gate, 0, 0, None)
            load(w_gate, P, 1, None)
            with sp.Fori(1, NM_ // 2) as i:
                c = [sp.snap(i * 2 * P + s * P) for s in range(2)]
                need = [sp.snap(i * 2 + s - 1) for s in range(2)]
                for s in range(2):
                    load(w_gate, c[s], s, need[s])
            for br in range(2):
                for s in range(2):
                    load(w_br[br], s * P, s, NM_ + br * KT + s - 1)
                for k in range(KT):
                    n = br * KT + k
                    if n >= NO:
                        sp.wait_ge(S["o_lo"], n - NO + 1)
                    sp.dma_start(ost[:, n % NO, :], (oa, ob)[br][k * P:(k + 1) * P, :]).then_inc(S[f"o_in{n % NO}"], 16)
                with sp.Fori(1, KT // 2) as i:
                    c = [sp.snap(i * 2 * P + s * P) for s in range(2)]
                    need = [sp.snap(i * 2 + NM_ + br * KT + s - 1) for s in range(2)]
                    for s in range(2):
                        load(w_br[br], c[s], s, need[s])

        @block.gpsimd
        def _(pool):
            def low(j, slot):
                pool.wait_ge(S["w_hi"], j + 1)
                pool.tensor_tensor(wlo[:, slot], wst[:, slot], whi[:, slot].bitcast(F32),
                                   ALU.subtract).then_inc(S["w_lo"], 1)

            def blocks(first, n):
                with pool.Fori(0, n // 2) as i:
                    for s in range(2):
                        low(i * 2 + first + s, s)

            blocks(0, NM_)
            for br in range(2):
                for s in range(2):
                    low(NM_ + br * KT + s, s)
                for k in range(KT):
                    n = br * KT + k
                    pool.wait_ge(S["o_hi"], n + 1)
                    pool.tensor_tensor(R.hlo[:, k, :], ost[:, n % NO, :], R.hhi[:, k, :].bitcast(F32),
                                       ALU.subtract).then_inc(S["o_lo"], 1)
                blocks(NM_ + br * KT + 2, KT - 2)

        @block.scalar
        def _(act):
            def high(turn, slot, mm):
                act.wait_ge(S[f"w_in{slot}"], 16 * turn + 16)
                if mm is not None:
                    act.wait_ge(S["mm"], mm)
                act.activation(whi[:, slot], wst[:, slot], ACT.Copy).then_inc(S["w_hi"], 1)

            high(0, 0, None)
            high(0, 1, None)
            for br, sg in enumerate((mixed, sgb)):
                with act.Fori(0, KT // 2) as i:
                    for s in range(2):
                        act.wait_ge(S["bias"], i * 2 + br * KT + s + 1)
                        for g in range(NG):
                            n = s * NG + g
                            act.wait_ge(S["mm"], i * 2 * NG + br * KT * NG + n + 1)
                            act.activation(sg[:, bass.ds(i * 2 + s, 1), g * GW:(g + 1) * GW].rearrange("p a n -> p (a n)"),
                                           bank[n][:, 0:GW], ACT.Tanh, scale=0.5,
                                           bias=bg[:, s:s + 1]).then_inc(S["gate"], 1)
                        high(i + (br * KT // 2 + 1), s, i * 2 * NG + br * KT * NG + (s + 1) * NG)
            for br in range(2):
                base = (NM_ + br * KT) * NG
                act.wait_ge(S["mm"], base)
                for k in range(KT):
                    n = br * KT + k
                    act.wait_ge(S[f"o_in{n % NO}"], 16 * (n // NO + 1))
                    act.activation(R.hhi[:, k, :], ost[:, n % NO, :], ACT.Copy).then_inc(S["o_hi"], 1)
                with act.Fori(0, KT // 2 - (1 if br else 0)) as i:
                    for s in range(2):
                        high(i + ((NM_ + br * KT) // 2 + 1), s, i * 2 * NG + base + (s + 1) * NG)

        @block.tensor
        def _(pe):
            def project(j, slot, free):
                pe.wait_ge(S["w_lo"], j + 1)
                for g in range(NG):
                    ts = slice(g * GW, (g + 1) * GW)
                    if free is not None:
                        pe.wait_ge(free[0], free[1] + g)
                    for k in range(KT):
                        mm = split_product(pe, bank[slot * NG + g][:, 0:GW], whi[:, slot, k, :], wlo[:, slot, k, :],
                                           R.hhi[:, k, ts], R.hlo[:, k, ts], k, k == KT - 1)
                    mm.then_inc(S["mm"], 1)

            def first_pair(br):
                pe.wait_ge(S["w_lo"], NM_ + br * KT + 2)
                if br:
                    pe.wait_ge(S["fold"], KT * NG)
                for step in range(KT + SKEW):
                    for s in range(2):
                        k = step - SKEW * s
                        if not 0 <= k < KT:
                            continue
                        if s == 0:
                            pe.wait_ge(S["o_lo"], br * KT + k + 1)
                        for g in range(NG):
                            ts = slice(g * GW, (g + 1) * GW)
                            mm = split_product(pe, bank[s * NG + g][:, 0:GW], whi[:, s, k, :], wlo[:, s, k, :],
                                               R.hhi[:, k, ts], R.hlo[:, k, ts], k, k == KT - 1)
                            if k == KT - 1:
                                mm.then_inc(S["mm"], 1)

            project(0, 0, None)
            project(1, 1, None)
            with pe.Fori(1, NM_ // 2) as i:
                for s in range(2):
                    project(i * 2 + s, s, (S["gate"], i * 2 * NG + (s - 2) * NG + 1))
            pe.wait_ge(S["gate"], NM_ * NG)
            for br in range(2):
                first = br * KT * NG
                first_pair(br)
                with pe.Fori(1, KT // 2) as i:
                    for s in range(2):
                        project(i * 2 + NM_ + br * KT + s, s, (S["fold"], i * 2 * NG + first + (s - 2) * NG + 1))

        @block.vector
        def _(dve):
            for s in range(2):
                dve.tensor_copy(bg[:, s:s + 1], R.par[:, PB_GATE + s:PB_GATE + s + 1]).then_inc(S["bias"], 1)
            with dve.Fori(1, NM_ // 2) as i:
                for s in range(2):
                    dve.wait_ge(S["gate"], i * 2 * NG)
                    dve.tensor_copy(bg[:, s:s + 1], R.par[:, bass.ds(i * 2 + (PB_GATE + s), 1)]).then_inc(S["bias"], 1)
            dve.wait_ge(S["gate"], NM_ * NG)
            def fold(br, i, first):
                    for s in range(2):
                        for g in range(NG):
                            gsl = slice(g * GW, (g + 1) * GW)
                            n = s * NG + g
                            at = lambda v: v[:, bass.ds(i * 2 + s, 1), gsl].rearrange("p a n -> p (a n)")
                            dve.wait_ge(S["mm"], i * 2 * NG + (NM_ + br * KT) * NG + n + 1)
                            ps = bank[s * NG + g][:, 0:GW]
                            if br == 0:
                                dve.scalar_tensor_tensor(out=at(mixed), in0=at(mixed), scalar=1.0, in1=ps,
                                                         op0=ALU.add, op1=ALU.mult).then_inc(S["fold"], 1)
                            else:
                                if n >= 2:
                                    dve.wait_ge(S["mix"], i * 2 * NG + n - 1)
                                elif not first:
                                    dve.wait_ge(S["mix"], i * 2 * NG)
                                dve.scalar_tensor_tensor(out=tmp[:, n % 2, :], in0=at(sgb), scalar=1.0, in1=ps,
                                                         op0=ALU.add, op1=ALU.mult).then_inc(S["fold"], 1)
                                dve.wait_ge(S["fold"], i * 2 * NG + KT * NG + n + 1)
                                dve.tensor_tensor(at(mixed), at(mixed), tmp[:, n % 2, :],
                                                  ALU.add).then_inc(S["mix"], 1)

            for br in range(2):
                fold(br, 0, True)
                with dve.Fori(1, KT // 2) as i:
                    fold(br, i, False)
            dve.wait_ge(S["mix"], NG * KT)


def output_stage(nc, R, A, gate_rows, mixed):
    with ExitStack() as ctx:
        sb = lambda name, shape, dt=F32: ctx.enter_context(nc.sbuf_tensor(name, shape, dt))
        sem = lambda name: ctx.enter_context(nc.semaphore(name))
        wst = sb("o_w", [P, 2, D])
        whi = sb("o_w_hi", [P, KT, D], F32R)
        wlo = sb("o_w_lo", [P, KT, D], F32R)
        gate = sb("o_gate", [P, 2, D])
        x = wst
        y, sq, fw = mixed[:, 0:2, 0:D], mixed[:, 2, 0:D], mixed[:, 3, 0:D]
        ss = sb("o_ss", [P, 2])
        ms = sb("o_ms", [P, 2])
        rs = sb("o_rs", [P, 2])
        mhalf = sb("o_mhalf", [P, 1])
        bank = [ctx.enter_context(nc.psum_tensor(f"ob{i}", [P, 512], F32)) for i in range(8)]
        S = {n: sem("o_" + n) for n in ("w_in0", "w_in1", "w_hi", "w_lo", "mix_hi", "mix_lo", "gate_in", "half", "x_in0", "x_in1", "mm", "scaled", "y", "ss", "ms",
                                        "rs", "out", "store0", "store1", "gate")}
        block = ctx.enter_context(nc.Block())
        HALF = D // 2

        @block.sync
        def _(sp):
            for k in range(KT):
                if k >= 2:
                    sp.wait_ge(S["w_lo"], k - 1)
                sp.dma_start(wst[:, k % 2, :], A["w_out"][0, k * P:(k + 1) * P, :]).then_inc(S[f"w_in{k % 2}"], 16)
            for a in range(2):
                sp.dma_start(gate[:, a, :], gate_rows[a:a + 1, :].broadcast_to([P, D])).then_inc(S["gate_in"], 16)
            sp.wait_ge(S["mix_lo"], 4)
            sp.dma_start(fw[:, :], A["final_norm_w"].unsqueeze(0).broadcast_to([P, D])).then_inc(S["gate_in"], 16)
            for t in range(NT + 1):
                if t < NT:
                    src = A["x_prompt"][0] if t == 0 else A["x_sample"][0, (t - 1) * P:t * P, :]
                    if t < 2:
                        sp.wait_ge(S["w_lo"], KT - 1 + t)
                    else:
                        sp.wait_ge(S["y"], t - 1)
                    sp.dma_start(x[:, t % 2, :], src).then_inc(S[f"x_in{t % 2}"], 16)
                if t:
                    dst = A["y_prompt"][0] if t == 1 else A["y_sample"][0, (t - 2) * P:(t - 1) * P, :]
                    sp.wait_ge(S["out"], t)
                    sp.dma_start(dst, y[:, (t - 1) % 2, :]).then_inc(S[f"store{(t - 1) % 2}"], 16)
            sp.wait_ge(S["store0"], 16 * ((NT + 1) // 2))
            sp.wait_ge(S["store1"], 16 * (NT // 2))

        @block.gpsimd
        def _(pool):
            pool.memset(mhalf[:, :], -0.5).then_inc(S["half"], 1)
            for k in range(KT):
                pool.wait_ge(S["mix_hi"], k + 1)
                pool.tensor_tensor(R.hlo[:, k, :], mixed[:, k, :], R.hhi[:, k, :].bitcast(F32),
                                   ALU.subtract).then_inc(S["mix_lo"], 1)
            pool.wait_ge(S["half"], 1)
            for t in range(NT):
                a = slice(t % 2, t % 2 + 1)
                pool.wait_ge(S["ss"], t + 1)
                pool.tensor_scalar(ms[:, a], ss[:, a], 1.0 / D, EPS, ALU.mult, ALU.add).then_inc(S["ms"], 1)
                pool.wait_ge(S["ms"], t + 1)
                if t >= 2:
                    pool.wait_ge(S["out"], t - 1)
                pool.tensor_tensor(rs[:, a], ms[:, a], mhalf[:, :], ALU.pow).then_inc(S["rs"], 1)

        @block.scalar
        def _(act):
            for k in range(KT):
                act.activation(R.hhi[:, k, :], mixed[:, k, :], ACT.Copy).then_inc(S["mix_hi"], 1)
                act.wait_ge(S[f"w_in{k % 2}"], 16 * (k // 2 + 1))
                act.activation(whi[:, k, :], wst[:, k % 2, :], ACT.Copy).then_inc(S["w_hi"], 1)
            for t in range(NT):
                act.wait_ge(S["y"], t + 1)
                if t:
                    act.wait_ge(S["ss"], t)
                if t >= 2:
                    act.wait_ge(S["ms"], t - 1)
                act.activation(sq[:, :], y[:, t % 2, :], ACT.Square, accum_out=ss[:, t % 2:t % 2 + 1]
                               ).then_inc(S["ss"], 1)

        @block.tensor
        def _(pe):
            def product(idx, k):
                t, n = divmod(idx, 2)
                ts, ns = slice(t * P, (t + 1) * P), slice(n * HALF, (n + 1) * HALF)
                mm = split_product(pe, bank[idx % 8][:, :], R.hhi[:, k, ts], R.hlo[:, k, ts],
                                   whi[:, k, ns], wlo[:, k, ns], k, k == KT - 1)
                if k == KT - 1:
                    mm.then_inc(S["mm"], 1)

            for k in range(KT):
                pe.wait_ge(S["w_lo"], k + 1)
                pe.wait_ge(S["mix_lo"], k + 1)
                for idx in range(8):
                    product(idx, k)
            for idx in range(8, 2 * NT):
                pe.wait_ge(S["scaled"], idx - 7)
                for k in range(KT):
                    product(idx, k)

        @block.vector
        def _(dve):
            for k in range(KT):
                dve.wait_ge(S["w_hi"], k + 1)
                dve.tensor_tensor(wlo[:, k, :], wst[:, k % 2, :], whi[:, k, :].bitcast(F32),
                                  ALU.subtract).then_inc(S["w_lo"], 1)
            dve.wait_ge(S["gate_in"], 48)
            dve.tensor_scalar(gate[:, :, :], gate[:, :, :], 0.5, None, ALU.mult).then_inc(S["gate"], 1)
            dve.wait_ge(S["gate"], 1)

            def finish(t):
                dve.wait_ge(S["rs"], t + 1)
                dve.scalar_tensor_tensor(out=y[:, t % 2, :], in0=y[:, t % 2, :], scalar=rs[:, t % 2:t % 2 + 1],
                                         in1=fw[:, :], op0=ALU.mult, op1=ALU.mult).then_inc(S["out"], 1)

            for t in range(NT):
                if t >= 2:
                    dve.wait_ge(S[f"store{t % 2}"], 16 * (t // 2))
                for n in range(2):
                    ns = slice(n * HALF, (n + 1) * HALF)
                    dve.wait_ge(S["mm"], 2 * t + n + 1)
                    dve.tensor_tensor(y[:, t % 2, ns], bank[(2 * t + n) % 8][:, :], gate[:, min(t, 1), ns],
                                      ALU.mult).then_inc(S["scaled"], 1)
                dve.wait_ge(S["scaled"], 2 * t + 2)
                dve.wait_ge(S[f"x_in{t % 2}"], 16 * (t // 2 + 1))
                dve.tensor_tensor(y[:, t % 2, :], y[:, t % 2, :], x[:, t % 2, :], ALU.add).then_inc(S["y"], 1)
                if t:
                    finish(t - 1)
            finish(NT - 1)


def build(nc, A):
    oa = nc.dram_tensor("branch_a", (D, TOK), F32, kind="Internal").ap()
    ob = nc.dram_tensor("branch_b", (D, TOK), F32, kind="Internal").ap()
    gate_rows = nc.dram_tensor("gate_rows", (2, D), F32, kind="Internal").ap()
    with ExitStack() as ctx:
        R = Resident(nc, ctx)
        setup_stage(nc, R, A, gate_rows)
        delta_stage(nc, R, A, oa)
        lru_stage(nc, R, A, ob)
        mixed = ctx.enter_context(nc.sbuf_tensor("mixed", [P, KT, TOK], F32))
        merge_stage(nc, R, A, oa, ob, mixed)
        output_stage(nc, R, A, gate_rows, mixed)


_INS = ["x_prompt", "x_sample", "state_a_fwd", "state_a_bwd", "state_b_fwd", "state_b_bwd", "c", "c_ctx", "norm_w",
        "w_mod", "b_mod", "w_in", "conv_a_w", "conv_a_b", "a_log_fwd", "dt_bias_fwd", "a_log_bwd", "dt_bias_bwd",
        "onorm_a_w", "conv_b_w", "conv_b_b", "lru_wa_fwd", "lru_ba_fwd", "lru_wx_fwd", "lru_bx_fwd", "lru_lambda_fwd",
        "lru_wa_bwd", "lru_ba_bwd", "lru_wx_bwd", "lru_bx_bwd", "lru_lambda_bwd", "w_proj_a", "w_proj_b", "w_gate",
        "b_gate", "w_out", "final_norm_w"]
_OUTS = [("y_prompt", (1, CTX, D)), ("y_sample", (1, LAT, D)), ("new_af", (1, 1, H, P, P)), ("new_ab", (1, 1, H, P, P)),
         ("new_bf", (1, 1, D)), ("new_bb", (1, 1, D))]


def kernel(**inputs):
    import concourse.bacc as _bacc
    from concourse.bass_utils import run_bass_kernel_spmd as _run

    nc = _bacc.Bacc("TRN2", target_bir_lowering=False, num_devices=1)
    arrays, args = {}, {}
    for name in _INS:
        a = np.ascontiguousarray(inputs[name])
        arrays[f"in_{name}"] = a
        args[name] = nc.dram_tensor(f"in_{name}", a.shape, mybir.dt.from_np(a.dtype), kind="ExternalInput").ap()
    arrays["in_consts"] = constants()
    args["consts"] = nc.dram_tensor("in_consts", (P, NM * P), F32, kind="ExternalInput").ap()
    for name, shape in _OUTS:
        args[name] = nc.dram_tensor(f"out_{name}", shape, F32, kind="ExternalOutput").ap()
    build(nc, args)
    r = _run(nc, [arrays], core_ids=[0])
    return tuple(r.results[0][f"out_{name}"] for name, _ in _OUTS)
```

```python
from contextlib import ExitStack

import concourse.bass as bass
import numpy as np
from concourse import mybir

F32 = mybir.dt.float32
F32R = mybir.dt.float32r
ALU = mybir.AluOpType
ACT = mybir.ActivationFunctionType
AX = mybir.AxisListType

P = 128
D = 1024
KT = D // P
H = 8
CTX, LAT = 128, 1024
TOK = CTX + LAT
NT = TOK // P
TG = 3
NG = NT // TG
GW = TG * P
DIRS = 2
NI = NT * DIRS
NGD = NG * DIRS
LEVELS = 7
GRID_W = 64
GRID_R = LAT // GRID_W
TAPS, PAD_L = 4, 2
GAP = TAPS - 1
RAW = PAD_L + CTX + GAP + LAT + 1
CONV = RAW - GAP
LAT0 = CTX + GAP
EPS = 1e-6
LRU_C = 8.0

PA_CONV = 0
PA_NORM = 120
PB = 128
PB_LRU = PB
PB_GATE = PB + 88
PB_ONORM = PB + 104
PC = 256
NLP = 11

G_DECAY, G_BETA, G_EXPCUM, G_EXPREST, G_EXPALL = range(5)


def tile_at(t):
    return 0 if t == 0 else LAT0 + (t - 1) * P


def constants():
    r, c = np.mgrid[0:P, 0:P]
    out = [r <= c, r >= c, r < c, r > c, r == c, np.ones((P, P))]
    for level in range(LEVELS):
        b = 1 << level
        pair = (c // b == r // b + 1) & ((r // b) % 2 == 0)
        fwd = (r == c).astype(np.float32) - pair.astype(np.float32)
        out += [fwd, fwd.T]
    return np.concatenate([np.asarray(m, np.float32) for m in out], axis=1)


M_TRIU, M_TRIL, M_STRIU, M_STRIL, M_ID, M_ONE, M_LEVEL = 0, 1, 2, 3, 4, 5, 6
NM = M_LEVEL + 2 * LEVELS


class Resident:

    def __init__(self, nc, ctx):
        sb = lambda name, shape, dt=F32: ctx.enter_context(nc.sbuf_tensor(name, shape, dt))
        self.masks = sb("masks", [P, NM * P])
        self.par = sb("par", [P, 3 * P])
        self.hhi = sb("h_hi", [P, KT, TOK], F32R)
        self.hlo = sb("h_lo", [P, KT, TOK], F32R)
        self.gates = sb("gates", [P, 5, NI, H])
        self.rate = sb("lru_rate", [P, 2, DIRS, H])
        self.newb = sb("new_state_b_cols", [P, DIRS, H])

    def m(self, k, n=1):
        return self.masks[:, k * P:(k + n) * P]

    def level(self, level, d):
        return self.m(M_LEVEL + 2 * level + d)


def bc(ap, n):
    return ap.unsqueeze(1).broadcast_to([P, n, P])


def cols(ap, n):
    return ap.unsqueeze(2).broadcast_to([P, n, P])


def v3(ap):
    return ap.rearrange("p (j c) -> p j c", c=P)


def setup_stage(nc, R, A, gate_rows):
    with ExitStack() as ctx:
        sb = lambda name, shape, dt=F32: ctx.enter_context(nc.sbuf_tensor(name, shape, dt))
        sems = []

        def sem(name):
            sems.append(nc.alloc_semaphore(name))
            return sems[-1]

        rows = sb("rows", [P, 3, P])
        NW, WH = 4, 3 * D // 2
        wmod = sb("wmod", [P, NW, WH])
        bmod = sb("bmod", [2, 3 * D])
        modrow = sb("modrow", [2, 3 * D])
        sc = sb("silu_c", [P, 2, KT])
        sct = sb("silu_c_tanh", [P, 2 * KT])
        mod = sb("mod_cols", [P, 2 * KT, 2])
        gain = sb("gain", [P, 2, KT])
        shift = sb("shift", [P, 2, KT])
        x = sb("x", [P, 2, D])
        xn = sb("xn", [P, D])
        ss = sb("ss", [P, 1])
        ms = sb("ms", [P, 1])
        rstd = sb("rstd", [P, 1])
        mhalf = sb("minus_half", [P, 1])
        crow = sb("c_rows", [2 * KT, P])
        craw = sb("c_cols", [P, 2, KT])
        hf = sb("hf", [P, 2, TOK])
        xsq = hf[:, 0, 0:D]
        xt = sb("xt", [P, KT, TOK])
        gfeat = sb("gate_rows_t", [4 * H, TOK])
        wg = sb("wg", [P, KT, 4 * H])
        graw = sb("graw", [P, NT, 4 * H])
        dtb = sb("dt_bias", [P, DIRS, H])
        alog = sb("a_log", [P, DIRS, H])
        ea = sb("exp_a_log", [P, DIRS, H])
        gx = sb("gate_x", [P, NT, DIRS, H])
        gu = sb("gate_u", [P, NT * DIRS * H])
        gw = sb("gate_w1", [P, NT * DIRS * H])
        gl = sb("gate_ln", [P, NT * DIRS * H])
        gr = sb("gate_r", [P, NT * DIRS * H])
        gt = sb("gate_t", [P, NT * DIRS * H])
        lu = sb("lam_u", [P, DIRS * H])
        lw = sb("lam_w", [P, DIRS * H])
        ll = sb("lam_l", [P, DIRS * H])
        lr = sb("lam_r", [P, DIRS * H])
        bank = [ctx.enter_context(nc.psum_tensor(f"sb{i}", [P, 512], F32)) for i in range(8)]

        consts_in, rows_in, rows_zero = sem("consts_in"), sem("rows_in"), sem("rows_zero")
        c_in, c_t, c_done, ident_in, x_e, h_lod, g_row, g_t = (sem(n) for n in (
            "c_in", "c_t", "c_done", "ident_in", "x_e", "h_lo_dve", "g_row", "g_t"))
        small_in, wmod_in, x_in = sem("small_in"), [sem(f"wmod_in{i}") for i in range(4)], [sem(f"x_in{i}") for i in range(2)]
        rows_t, par_done, silu_t, silu_done = sem("rows_t"), sem("par_done"), sem("silu_t"), sem("silu_done")
        mod_k, mod_row, mod_t, mod_done = sem("mod_k"), sem("mod_row"), sem("mod_t"), sem("mod_done")
        half_set, gate_out = sem("half_set"), sem("gate_out")
        x_sq, x_rstd, x_n, x_t, h_f, h_hi, h_lo, g_mm, g_copy = (sem(n) for n in (
            "x_sq", "x_rstd", "x_n", "x_t", "h_f", "h_hi", "h_lo", "g_mm", "g_copy"))
        dve_own, pool_own = sem("dve_own"), sem("pool_own")
        act_exp, dve_w, act_ln, act_th, gates_raw, cum_mm, cum_exp = (sem(n) for n in (
            "act_exp", "dve_w", "act_ln", "act_th", "gates_raw", "cum_mm", "cum_exp"))
        ctx.callback(nc.all_engine_barrier)
        ctx.callback(lambda: nc.clear_and_free_semaphores(sems))
        block = ctx.enter_context(nc.Block())
        PAR_AT = 7
        SPLIT = TOK // 2
        conv_a = A["conv_a_w"][0].rearrange("a (r p) -> (a r) p", p=P)
        row1 = lambda name: A[name][0].rearrange("(r p) -> r p", p=P)
        bcast = lambda name: A[name].broadcast_to([P, H])
        sources = [
            (0, 0, conv_a, 96), (0, 96, row1("conv_a_b"), 24), (0, 120, row1("norm_w"), KT),
            (1, 0, A["conv_b_w"][0].rearrange("a (r p) -> (a r) p", p=P), 32), (1, 32, row1("conv_b_b"), 8),
            (1, 40, row1("lru_ba_fwd"), 8), (1, 48, row1("lru_bx_fwd"), 8),
            (1, 56, row1("lru_ba_bwd"), 8), (1, 64, row1("lru_bx_bwd"), 8),
            (1, 72, row1("lru_lambda_fwd"), 8), (1, 80, row1("lru_lambda_bwd"), 8),
            (1, 88, row1("b_gate"), 16), (1, 104, row1("onorm_a_w"), 1),
            (2, 0, A["c_ctx"].rearrange("(r p) -> r p", p=P), 8), (2, 8, row1("c"), 8),
            (2, 16, A["state_b_fwd"][0, 0].rearrange("(r p) -> r p", p=P), 8),
            (2, 24, A["state_b_bwd"][0, 0].rearrange("(r p) -> r p", p=P), 8),
        ]
        small = [(dtb[:, 0, :], bcast("dt_bias_fwd")), (dtb[:, 1, :], bcast("dt_bias_bwd")),
                 (alog[:, 0, :], bcast("a_log_fwd")), (alog[:, 1, :], bcast("a_log_bwd")),
                 (bmod[:, :], A["b_mod"].broadcast_to([2, 3 * D])),
                 (wg[:, :, :], A["w_in"][0, :, 6 * D:6 * D + 4 * H].rearrange("(k p) n -> p k n", p=P))]

        @block.sync
        def _(sp):
            for a, src in enumerate((A["c_ctx"], A["c"][0])):
                sp.dma_start(crow[a * KT:(a + 1) * KT, :], src.rearrange("(k p) -> k p", p=P)).then_inc(c_in, 16)
            loads = [(rows[r:r + n, t, :], src, rows_in) for t, r, src, n in sources]
            loads += [(dst, src, small_in) for dst, src in small]
            loads += [(R.masks[:, at], A["consts"][:, at], consts_in)
                      for at in (slice(0, M_ID * P), slice((M_ID + 1) * P, NM * P))]
            share = -(-len(loads) // (PAR_AT - 1))
            sp.wait_ge(rows_zero, 1)
            for t in range(NT):
                for c in range(2 * t, 2 * t + 2) if t < KT else ():
                    if c >= NW:
                        sp.wait_ge(mod_k, c - NW + 1)
                    sp.dma_start(wmod[:, c % NW, :], A["w_mod"][0, t * P:(t + 1) * P, c % 2 * WH:(c % 2 + 1) * WH]
                                 ).then_inc(wmod_in[c % NW], 16)
                src = A["x_prompt"][0] if t == 0 else A["x_sample"][0, (t - 1) * P:t * P, :]
                if t >= 2:
                    sp.wait_ge(x_n, t - 1)
                sp.dma_start(x[:, t % 2, :], src).then_inc(x_in[t % 2], 16)
                for dst, src, done in loads[(t - 1) * share:t * share] if t else ():
                    sp.dma_start(dst, src).then_inc(done, 16)
            sp.wait_ge(mod_row, 1)
            sp.dma_start(gate_rows, modrow[:, 2 * D:3 * D]).then_inc(gate_out, 16)
            sp.wait_ge(gate_out, 16)

        @block.gpsimd
        def _(pool):
            pool.memset(rows[:, :, :], 0.0).then_inc(rows_zero, 1)
            pool.memset(mhalf[:, :], -0.5).then_inc(half_set, 1)
            pool.wait_ge(half_set, 1)
            for t in range(NT):
                pool.wait_ge(x_sq, t + 1)
                if t:
                    pool.wait_ge(x_n, t)
                pool.tensor_scalar(ms[:, :], ss[:, :], 1.0 / D, EPS, ALU.mult, ALU.add).then_inc(pool_own, 1)
                pool.wait_ge(pool_own, t + 1)
                pool.tensor_tensor(rstd[:, :], ms[:, :], mhalf[:, :], ALU.pow).then_inc(x_rstd, 1)
            for k in range(KT):
                pool.wait_ge(h_hi, k + 1)
                pool.tensor_tensor(R.hlo[:, k, 0:SPLIT], hf[:, k % 2, 0:SPLIT], R.hhi[:, k, 0:SPLIT].bitcast(F32),
                                   ALU.subtract).then_inc(h_lo, 1)

        @block.scalar
        def _(act):
            act.dma_start(R.m(M_ID), A["consts"][:, M_ID * P:(M_ID + 1) * P]).then_inc(ident_in, 16)
            act.wait_ge(c_done, 1)
            act.activation(sct[:, :], craw[:, :, :].rearrange("p a k -> p (a k)"), ACT.Tanh, scale=0.5
                           ).then_inc(silu_t, 1)
            for t in range(NT):
                act.wait_ge(x_in[t % 2], 16 * (t // 2 + 1))
                if t:
                    act.wait_ge(x_rstd, t)
                    act.wait_ge(x_sq, t)
                act.activation(xsq[:, :], x[:, t % 2, :], ACT.Square, accum_out=ss[:, :]).then_inc(x_sq, 1)
                act.wait_ge(x_rstd, t + 1)
                if t:
                    act.wait_ge(x_t, t)
                act.activation(xn[:, :], x[:, t % 2, :], ACT.Copy, scale=rstd[:, 0:1]).then_inc(x_n, 1)
            for k in range(KT):
                act.wait_ge(h_f, k + 1)
                act.activation(R.hhi[:, k, :], hf[:, k % 2, :], ACT.Copy).then_inc(h_hi, 1)
            for g in range(NG):
                act.wait_ge(g_mm, KT)
                act.activation(gfeat[:, g * GW:(g + 1) * GW], bank[g][0:4 * H, 0:GW], ACT.Copy).then_inc(g_row, 1)
            act.wait_ge(gates_raw, 1)
            act.activation(gu[:, :], gt[:, :], ACT.Exp, scale=-1.0).then_inc(act_exp, 1)
            act.activation(ea[:, :, :], alog[:, :, :], ACT.Exp).then_inc(act_exp, 1)
            act.activation(lu[:, :], lr[:, :], ACT.Exp, scale=-1.0).then_inc(act_exp, 1)
            act.wait_ge(dve_w, 2)
            act.activation(gl[:, :], gw[:, :], ACT.Ln).then_inc(act_ln, 1)
            act.activation(ll[:, :], lw[:, :], ACT.Ln).then_inc(act_ln, 1)
            beta = R.gates[:, G_BETA].rearrange("p (g d j) h -> p g d j h", g=NG, d=DIRS)
            for d in range(DIRS):
                for g in range(NG):
                    act.activation(beta[:, g, d], graw[:, TG * g:TG * (g + 1), (2 * d + 1) * H:(2 * d + 2) * H],
                                   ACT.Tanh, scale=0.5).then_inc(act_th, 1)
            kinds = (G_EXPCUM, G_EXPREST, G_EXPALL)
            for n, kind in enumerate(kinds):
                act.wait_ge(cum_mm, n + 1)
                act.activation(R.gates[:, kind], bank[5 + n][:, 0:NI * H].rearrange("p (n h) -> p n h", h=H),
                               ACT.Exp).then_inc(cum_exp, 1)

        @block.tensor
        def _(pe):
            pe.wait_ge(ident_in, 16)
            pe.wait_ge(c_in, 32)
            pe.transpose(bank[6][:, 0:2 * KT], crow[:, :], R.masks[0:2 * KT, M_ID * P:M_ID * P + 2 * KT]
                         ).then_inc(c_t, 1)
            pe.wait_ge(silu_done, 1)
            for t in range(NT):
                for c in range(2 * t, 2 * t + 2) if t < KT else ():
                    pe.wait_ge(wmod_in[c % NW], 16 * (c // NW + 1))
                    for n in range(3):
                        mm = pe.matmul(bank[c % 2 * 3 + n][0:2, :], sc[:, :, t], wmod[:, c % NW, n * 512:(n + 1) * 512],
                                       start=(t == 0), stop=(t == KT - 1))
                    mm.then_inc(mod_k, 1)
                if t:
                    pe.wait_ge(x_e, t)
                if t == PAR_AT:
                    pe.wait_ge(rows_in, 16 * len(sources))
                    for j in range(3):
                        pe.transpose(bank[6][:, j * P:(j + 1) * P], rows[:, j, :], R.m(M_ID)).then_inc(rows_t, 1)
                    pe.wait_ge(par_done, 3)
                pe.wait_ge(x_n, t + 1)
                for k in range(KT):
                    mm = pe.transpose(bank[6 + k // 4][:, (k % 4) * P:(k % 4 + 1) * P], xn[:, k * P:(k + 1) * P],
                                      R.m(M_ID))
                mm.then_inc(x_t, 1)
            pe.wait_ge(x_e, NT)
            pe.wait_ge(mod_row, 1)
            for n in range(2 * KT):
                mm = pe.transpose(bank[6][:, 2 * n:2 * n + 2], modrow[:, n * P:(n + 1) * P],
                                  R.masks[0:2, M_ID * P:M_ID * P + 2])
            mm.then_inc(mod_t, 1)
            for k in range(KT):
                pe.wait_ge(h_f, k + 1)
                if k == 0:
                    pe.wait_ge(small_in, 16 * len(small))
                for g in range(NG):
                    mm = pe.matmul(bank[g][0:4 * H, 0:GW], wg[:, k, :], hf[:, k % 2, g * GW:(g + 1) * GW],
                                   start=(k == 0), stop=(k == KT - 1))
                mm.then_inc(g_mm, 1)
            pe.wait_ge(g_row, NG)
            for t in range(NT):
                mm = pe.transpose(bank[3][:, t * 4 * H:(t + 1) * 4 * H], gfeat[:, t * P:(t + 1) * P],
                                  R.masks[0:4 * H, M_ID * P:M_ID * P + 4 * H])
            mm.then_inc(g_t, 1)
            pe.wait_ge(consts_in, 32)
            pe.wait_ge(gates_raw, 2)
            sums = ((M_TRIU, M_TRIL), (M_STRIL, M_STRIU), (M_ONE, M_ONE))
            gam = R.gates[:, G_DECAY].rearrange("p (g d j) h -> p g d (j h)", g=NG, d=DIRS)
            for n, pair in enumerate(sums):
                for d in range(DIRS):
                    out = bank[5 + n][:, 0:NI * H].rearrange("p (g d x) -> p g d x", g=NG, d=DIRS)[:, :, d, :]
                    mm = pe.matmul(out, R.m(pair[d]), gam[:, :, d, :], start=True, stop=True)
                mm.then_inc(cum_mm, 1)

        @block.vector
        def _(dve):
            links = [0]

            def link(ins):
                links[0] += 1
                ins.then_inc(dve_own, 1)
                dve.wait_ge(dve_own, links[0])

            dve.wait_ge(c_t, 1)
            dve.tensor_copy(craw[:, :, :].rearrange("p a k -> p (a k)"), bank[6][:, 0:2 * KT]).then_inc(c_done, 1)
            dve.wait_ge(silu_t, 1)
            dve.wait_ge(c_done, 1)
            link(dve.scalar_tensor_tensor(out=sct[:, :], in0=sct[:, :], scalar=1.0,
                                          in1=craw[:, :, :].rearrange("p a k -> p (a k)"), op0=ALU.add, op1=ALU.mult))
            dve.tensor_scalar(sc[:, :, :], sct[:, :].rearrange("p (a k) -> p a k", a=2), 0.5, None,
                              ALU.mult).then_inc(silu_done, 1)
            for t in range(NT):
                if t == PAR_AT:
                    for j in range(3):
                        dve.wait_ge(rows_t, 3)
                        dve.tensor_copy(R.par[:, j * P:(j + 1) * P], bank[6][:, j * P:(j + 1) * P]
                                        ).then_inc(par_done, 1)
                    dve.wait_ge(par_done, 3)
                    link(dve.tensor_scalar(R.par[:, PB + 40:PB + 72], R.par[:, PB + 40:PB + 72], 0.5, None, ALU.mult))
                    link(dve.tensor_scalar(R.par[:, PB_GATE:PB_GATE + 17], R.par[:, PB_GATE:PB_GATE + 17], 0.5, None,
                                           ALU.mult))
                dve.wait_ge(x_t, t + 1)
                for half in range(2):
                    ins = dve.tensor_copy(xt[:, 4 * half:4 * half + 4, t * P:(t + 1) * P],
                                          v3(bank[6 + half][:, :]))
                ins.then_inc(x_e, 1)
            dve.wait_ge(mod_k, 2 * KT)
            dve.wait_ge(small_in, 16 * len(small))
            for n in range(6):
                ns = slice(n * 512, (n + 1) * 512)
                mm = dve.tensor_tensor(modrow[:, ns], bank[n][0:2, :], bmod[:, ns], ALU.add)
            mm.then_inc(mod_row, 1)
            dve.wait_ge(mod_t, 1)
            link(dve.tensor_copy(mod[:, :, :], bank[6][:, 0:4 * KT].rearrange("p (k a) -> p k a", a=2)))
            for a in range(2):
                dve.scalar_tensor_tensor(out=gain[:, a, :], in0=mod[:, KT:2 * KT, a], scalar=1.0,
                                         in1=R.par[:, PA_NORM:PA_NORM + KT], op0=ALU.add, op1=ALU.mult)
                link(dve.tensor_copy(shift[:, a, :], mod[:, 0:KT, a]))
            dve.wait_ge(x_e, NT)

            def low(k):
                dve.wait_ge(h_hi, k + 1)
                dve.tensor_tensor(R.hlo[:, k, SPLIT:TOK], hf[:, k % 2, SPLIT:TOK], R.hhi[:, k, SPLIT:TOK].bitcast(F32),
                                  ALU.subtract).then_inc(h_lod, 1)

            for k in range(KT):
                if k >= 2:
                    dve.wait_ge(h_lo, k - 1)
                    dve.wait_ge(h_lod, k - 1)
                    dve.wait_ge(g_mm, k - 1)
                for a, ts in ((0, slice(0, CTX)), (1, slice(CTX, TOK))):
                    ins = dve.tensor_scalar(hf[:, k % 2, ts], xt[:, k, ts], gain[:, a, k:k + 1],
                                            shift[:, a, k:k + 1], ALU.mult, ALU.add)
                ins.then_inc(h_f, 1)
                if k:
                    low(k - 1)
            low(KT - 1)
            dve.wait_ge(g_t, 1)
            dve.tensor_copy(graw[:, :, :].rearrange("p t n -> p (t n)"), bank[3][:, 0:NT * 4 * H]).then_inc(g_copy, 1)
            dve.wait_ge(g_copy, 1)
            for d in range(DIRS):
                ins = dve.tensor_tensor(gx[:, :, d, :], graw[:, :, 2 * d * H:(2 * d + 1) * H],
                                        dtb[:, d, :].unsqueeze(1).broadcast_to([P, NT, H]), ALU.add)
            link(ins)
            gxf = gx[:, :, :, :].rearrange("p t d h -> p (t d h)")
            lam = R.par[:, PB + 72:PB + 88]
            link(dve.tensor_scalar(gt[:, :], gxf, -1.0, None, ALU.mult))
            dve.tensor_tensor(gt[:, :], gt[:, :], gxf, ALU.max).then_inc(dve_own, 1)
            links[0] += 1
            link(dve.tensor_scalar(lr[:, :], lam, -1.0, None, ALU.mult))
            dve.tensor_tensor(lr[:, :], lr[:, :], lam, ALU.max).then_inc(gates_raw, 1)
            dve.wait_ge(act_exp, 3)
            dve.tensor_scalar(gw[:, :], gu[:, :], 1.0, None, ALU.add).then_inc(dve_w, 1)
            dve.tensor_scalar(lw[:, :], lu[:, :], 1.0, None, ALU.add).then_inc(dve_w, 1)
            dve.wait_ge(dve_w, 2)
            for u, w, r, ln, xx, sign in ((gu, gw, gr, gl, gxf, 1.0), (lu, lw, lr, ll, lam, -1.0)):
                link(dve.reciprocal(r[:, :], w[:, :]))
                t_ = gt if u is gu else sct
                link(dve.tensor_scalar(t_[:, :], w[:, :], -1.0, None, ALU.add))
                link(dve.tensor_tensor(t_[:, :], u[:, :], t_[:, :], ALU.subtract))
                link(dve.tensor_tensor(t_[:, :], t_[:, :], r[:, :], ALU.mult))
                dve.wait_ge(act_ln, 2)
                link(dve.tensor_tensor(t_[:, :], t_[:, :], ln[:, :], ALU.add))
                link(dve.tensor_scalar(r[:, :], xx, sign, 0.0, ALU.mult, ALU.max))
                link(dve.tensor_tensor(t_[:, :], t_[:, :], r[:, :], ALU.add))
            rate = R.rate[:, :, :, :].rearrange("p s d h -> p s (d h)")
            dve.tensor_scalar(rate[:, 0], sct[:, :], LRU_C / 2, None, ALU.mult)
            dve.tensor_scalar(rate[:, 1], sct[:, :], -LRU_C / 2, None, ALU.mult)
            link(dve.tensor_scalar(ea[:, :, :], ea[:, :, :], -1.0, None, ALU.mult))
            gam = R.gates[:, G_DECAY].rearrange("p (g d j) h -> p g d j h", g=NG, d=DIRS)
            sp_ = gt[:, :].rearrange("p (g j d h) -> p g j d h", g=NG, j=TG, d=DIRS)
            for d in range(DIRS):
                for g in range(NG):
                    ins = dve.tensor_tensor(gam[:, g, d], sp_[:, g, :, d, :],
                                            ea[:, d, :].unsqueeze(1).broadcast_to([P, TG, H]), ALU.mult)
            ins.then_inc(gates_raw, 1)
            dve.wait_ge(act_th, DIRS * NG)
            dve.tensor_scalar(R.gates[:, G_BETA], R.gates[:, G_BETA], 1.0, 0.5, ALU.add, ALU.mult).then_inc(dve_own, 1)


def split_product(pe, out, hi, lo, rhi, rlo, k, last, stop=True):
    pe.matmul(out, hi, rhi, start=(k == 0), stop=False)
    pe.matmul(out, hi, rlo, start=False, stop=False)
    return pe.matmul(out, lo, rhi, start=False, stop=(last and stop))


def evacuate_lru(act, rows, src, q):
    g = q % NG
    if q >= NG:
        return act.activation(rows[:, 1, g * GW:(g + 1) * GW], src[:, 0:GW], ACT.Copy)
    if g == 0:
        act.activation(rows[:, 0, PAD_L:PAD_L + CTX], src[:, 0:CTX], ACT.Copy)
    t0 = max(g * GW, CTX)
    r0, r1 = (t0 - CTX) // GRID_W, ((g + 1) * GW - CTX) // GRID_W
    lat = rows[:, 0, PAD_L + LAT0:PAD_L + LAT0 + LAT].rearrange("p (w r) -> p r w", r=GRID_R)
    return act.activation(lat[:, r0:r1, :], src[:, t0 - g * GW:GW].rearrange("p (r w) -> p r w", w=GRID_W), ACT.Copy)


def delta_stage(nc, R, A, oa, rows):
    with ExitStack() as ctx:
        sb = lambda name, shape, dt=F32: ctx.enter_context(nc.sbuf_tensor(name, shape, dt))
        sem = lambda name: ctx.enter_context(nc.semaphore(name))
        wst = sb("d_w", [P, KT, P])
        whi = sb("d_w_hi", [P, 2, KT, P], F32R)
        wlo = sb("d_w_lo", [P, 2, KT, P], F32R)
        qraw = sb("d_raw", [P, RAW])
        raw = (rows[:, 0, :], rows[:, 1, :], qraw[:, :])
        zraw = sb("d_z", [P, TOK])
        q2 = sb("d_q", [P, CONV])
        ework = sb("d_e", [P, 2 * CONV])
        rwork = sb("d_r", [P, 2 * CONV])
        lmat = sb("d_l", [P, NI * P])
        xmat = sb("d_x", [P, NI * P])
        ymat = sb("d_y", [P, NI * P])
        kn = sb("d_kn", [P, NT, P])
        vt = sb("d_v", [P, NT, P])
        kacc = sb("d_kacc", [P, NT, P])
        gs = sb("d_gs", [P, 2, GW])
        state = sb("d_state", [P, DIRS, P])
        state0 = sb("d_state0", [P, DIRS, P])
        vn = sb("d_vn", [P, 2, DIRS, P])
        vk = sb("d_vk", [P, 2, DIRS, P])
        cw = sb("d_cw", [P, 5, 3, 1])
        gh = sb("d_gh", [P, 5, NI, 1])
        ssk = sb("d_ssk", [P, NT])
        rk = sb("d_rk", [P, NT])
        ssq = sb("d_ssq", [P, NT])
        sso = sb("d_sso", [P, NT])
        ro = sb("d_ro", [P, NT])
        mhalf = sb("d_mhalf", [P, NT])
        bank = [ctx.enter_context(nc.psum_tensor(f"db{i}", [P, 512], F32)) for i in range(8)]
        proj = bank[6:8]
        ca, cb_ = rwork[:, 0:CONV], rwork[:, CONV:2 * CONV]
        cc, cd = ework[:, 0:CONV], ework[:, CONV:2 * CONV]

        S = {n: sem("d_" + n) for n in (
            "w_in", "w_hi", "w_lo", "proj_mm", "proj_out", "pads", "half",
            "par", "cw", "taps", "silu_t", "silu", "sq", "ss_mm", "ssk", "rk", "ssq", "kt", "kn", "vt", "vt_out", "knt",
            "knt_out", "gs", "dec", "dexp", "dmask", "kk", "gq", "l_raw", "qk", "l_done", "lt", "y0", "x0", "r", "r_out",
            "xy", "xt", "x_out", "y_out", "yb", "ybe", "nw", "nw_out", "qt", "qt_out", "st_in", "vnew", "vn_out", "vk_out",
            "su", "st_new", "st0", "ov", "acc", "own", "own2", "st_store", "osq", "osum", "ro", "ofac", "ot", "z_t", "z_s", "fin",
            "oa_store")}
        block = ctx.enter_context(nc.Block())
        w_in = A["w_in"][0].rearrange("(k p) n -> p k n", p=P)
        QKV = (1, 2, 0)
        PRE, PERW = 3, 4
        KB = (4, 5, 3)
        g_ = PERW * NG
        levels = LEVELS - 1

        def turns(eng, body):
            body(0, True, False)
            with eng.Fori(1, H - 1) as i:
                body(i, False, False)
            body(H - 1, False, True)

        @block.sync
        def _(sp):
            def load(col, need):
                if need is not None:
                    sp.wait_ge(S["w_lo"], need)
                sp.dma_start(wst[:, :, :], w_in[:, :, bass.ds(col, P)]).then_inc(S["w_in"], 16)

            for j, c in enumerate(QKV + (3,)):
                load(c * D, j or None)

            def turn(i, first, last):
                val = int if first or last else sp.snap
                cols_ = [4 * D, 5 * D] if last else [val(i * P + (c * D + P)) for c in QKV + (3,)]
                need = [val(i * PERW + PERW + k) for k in range(PERW)]
                ov, row, st0 = val(i * NT), val(i * 1), val(i * 1 + 1)
                fin, orow = val(i * NG + NG), val(i * P)
                if not first:
                    sp.wait_ge(S["ov"], ov)
                for d, name in enumerate(("state_a_fwd", "state_a_bwd")):
                    sp.dma_start(state[:, d, :], A[name][0, 0, bass.ds(row, 1)].rearrange("a k v -> k (a v)")
                                 ).then_inc(S["st_in"], 16)
                for c, n in zip(cols_[:NG], need):
                    load(c, n)
                sp.wait_ge(S["st0"], st0)
                for d, name in enumerate(("new_af", "new_ab")):
                    sp.dma_start(A[name][0, 0, bass.ds(row, 1)].rearrange("a k v -> k (a v)"), state0[:, d, :]
                                 ).then_inc(S["st_store"], 16)
                if not last:
                    load(cols_[NG], need[NG])
                sp.wait_ge(S["fin"], fin)
                sp.dma_start(oa[bass.ds(orow, P), :], cc[:, 0:TOK]).then_inc(S["oa_store"], 16)

            turns(sp, turn)
            sp.wait_ge(S["st_store"], 16 * DIRS * H)
            sp.wait_ge(S["oa_store"], 16 * H)

        @block.gpsimd
        def _(pool):
            for padded in (rows[:, :, :], qraw[:, :].unsqueeze(1)):
                pool.memset(padded[:, :, 0:PAD_L], 0.0)
                pool.memset(padded[:, :, PAD_L + CTX:PAD_L + CTX + GAP], 0.0)
                pool.memset(padded[:, :, RAW - 1:RAW], 0.0).then_inc(S["pads"], 1)
            pool.memset(mhalf[:, :], -0.5).then_inc(S["half"], 1)
            pool.wait_ge(S["half"], 1)
            one = pool.to_reg(1.0)

            def low(j, slot):
                pool.wait_ge(S["w_hi"], j + 1)
                pool.tensor_tensor(wlo[:, slot], wst[:, :, :], whi[:, slot].bitcast(F32),
                                   ALU.subtract).then_inc(S["w_lo"], 1)

            for j in range(PRE + 1):
                low(j, j % 2)

            def rsqrt_k(j):
                pool.wait_ge(S["ssk"], j + 1)
                pool.tensor_tensor(rk[:, :], ssk[:, :], mhalf[:, :], ALU.pow).then_inc(S["rk"], 1)

            rsqrt_k(0)

            def turn(i, first, last):
                def steps(n):
                    if n == 0:
                        pool.wait_ge(S["par"], i + 1)
                    if n >= 2:
                        pool.wait_ge(S["dec"], i * NGD + n - 1)
                    elif not first:
                        pool.wait_ge(S["dec"], i * NGD)
                    pool.tensor_tensor(v3(gs[:, n % 2, :]), bc(R.m(M_STRIU if n % DIRS else M_STRIL), TG),
                                       gh[:, G_DECAY, n * TG:(n + 1) * TG, 0:1].broadcast_to([P, TG, P]),
                                       ALU.mult).then_inc(S["gs"], 1)

                def mask_decays(n):
                    ns = slice(n * GW, (n + 1) * GW)
                    pool.wait_ge(S["dexp"], i * NGD + n + 1)
                    pool.tensor_tensor(v3(ework[:, ns]), v3(ework[:, ns]),
                                       bc(R.m(M_TRIU if n % DIRS else M_TRIL), TG), ALU.mult).then_inc(S["dmask"], 1)

                for n in range(NGD):
                    steps(n)
                    if n >= 3:
                        mask_decays(n - 3)
                for n in range(NGD - 3, NGD):
                    if n == NGD - 1:
                        pool.wait_ge(S["l_raw"], i * NGD + 3)
                    mask_decays(n)

                def diagonal(n):
                    ns = slice(n * GW, (n + 1) * GW)
                    pool.affine_select(out=v3(lmat[:, ns]), in_=v3(lmat[:, ns]), compare_op=ALU.not_equal, fill=one,
                                       base=0, pattern=[[0, TG], [-1, P]], channel_multiplier=1
                                       ).then_inc(S["l_done"], 1)

                def first_inverse(n):
                    ns = slice(n * GW, (n + 1) * GW)
                    pool.wait_ge(S["l_done"], i * NGD + n + 1)
                    pool.tensor_tensor(v3(xmat[:, ns]), v3(lmat[:, ns]), bc(R.level(0, 1 - n % DIRS), TG),
                                       ALU.mult).then_inc(S["x0"], 1)

                for n in range(3):
                    diagonal(n)
                pool.wait_ge(S["l_raw"], i * NGD + NGD)
                first_inverse(0)
                for n in range(3, NGD):
                    diagonal(n)
                for n in range(1, NGD):
                    first_inverse(n)
                for k in (1, 2):
                    low(i * PERW + PRE + k, (PRE + k) % 2)
                for n in range(NGD):
                    ns = slice(n * GW, (n + 1) * GW)
                    pool.wait_ge(S["yb"], i * NGD + n + 1)
                    pool.tensor_tensor(v3(rwork[:, ns]), v3(ymat[:, ns]),
                                       gh[:, G_EXPCUM, n * TG:(n + 1) * TG, 0:1].broadcast_to([P, TG, P]),
                                       ALU.mult).then_inc(S["ybe"], 1)
                if not last:
                    low(i * PERW + PRE + 3, (PRE + 3) % 2)
                    low(i * PERW + PRE + 4, (PRE + 4) % 2)
                    rsqrt_k(i + 1)
                pool.wait_ge(S["osum"], i + 1)
                pool.tensor_tensor(ro[:, :], sso[:, :], mhalf[:, :], ALU.pow).then_inc(S["ro"], 1)

            turns(pool, turn)

        @block.scalar
        def _(act):
            def high(j, slot, mm):
                act.wait_ge(S["w_in"], 16 * j + 16)
                if mm is not None:
                    act.wait_ge(S["proj_mm"], mm)
                act.activation(whi[:, slot], wst[:, :, :], ACT.Copy).then_inc(S["w_hi"], 1)

            def evac(gidx, par, c, g):
                act.wait_ge(S["proj_mm"], gidx + 1)
                src = proj[par]
                if c is None:
                    act.activation(zraw[:, g * GW:(g + 1) * GW], src[:, 0:GW], ACT.Copy).then_inc(S["proj_out"], 1)
                elif g == 0:
                    act.activation(raw[c][:, PAD_L:PAD_L + CTX], src[:, 0:CTX], ACT.Copy)
                    act.activation(raw[c][:, PAD_L + LAT0:PAD_L + LAT0 + GW - CTX], src[:, CTX:GW],
                                   ACT.Copy).then_inc(S["proj_out"], 1)
                else:
                    at = PAD_L + GAP + g * GW
                    act.activation(raw[c][:, at:at + GW], src[:, 0:GW], ACT.Copy).then_inc(S["proj_out"], 1)

            act.wait_ge(S["pads"], 2)
            high(0, 0, None)
            high(1, 1, None)
            def silu_tanh(h, s):
                act.wait_ge(S["taps"], h * 3 + s + 1)
                act.activation(cb_, (ca, cd, q2[:, :])[s], ACT.Tanh, scale=0.5).then_inc(S["silu_t"], 1)

            def square(h, s):
                act.wait_ge(S["silu"], h * 3 + s + 1)
                src, dst = (ca, cc) if s == 0 else (q2[:, :], cb_)
                act.activation(dst, src, ACT.Square).then_inc(S["sq"], 1)

            for j in range(PRE):
                for g in range(NG):
                    evac(j * NG + g, (j * NG + g) % 2, j, g)
                if j < 2:
                    high(j + 2, j, (j + 1) * NG)
                if j == 1:
                    silu_tanh(0, 0)
                    square(0, 0)
            silu_tanh(0, 1)

            def turn(i, first, last):
                base = i * g_ + PRE * NG
                if not first:
                    act.wait_ge(S["fin"], i * NG)
                for g in range(2):
                    evac(base + g, (PRE * NG + g) % 2, None, g)
                for g in range(NG):
                    act.wait_ge(S["vt"], i * NG + g + 1)
                    act.activation(vt[:, TG * g:TG * (g + 1), :], v3(bank[g][:, 0:GW]), ACT.Copy,
                                   scale=0.5).then_inc(S["vt_out"], 1)
                for g in range(NG):
                    act.wait_ge(S["knt"], i * NG + g + 1)
                    act.activation(kacc[:, TG * g:TG * (g + 1), :], v3(bank[KB[g]][:, 0:GW]),
                                   ACT.Copy).then_inc(S["knt_out"], 1)
                if not first:
                    act.wait_ge(S["oa_store"], i * 16)
                for n in range(NGD):
                    act.wait_ge(S["dec"], i * NGD + n + 1)
                    act.activation(ework[:, n * GW:(n + 1) * GW], bank[n % 2][:, 0:GW], ACT.Exp).then_inc(S["dexp"], 1)
                    if n == 1:
                        silu_tanh(i, 2)
                    elif n == 3:
                        square(i, 2)
                evac(base + 2, (PRE * NG + 2) % 2, None, 2)
                high(i * PERW + PRE + 1, (PRE + 1) % 2, i * g_ + PRE * NG)
                for idx in range((levels - 1) * NGD + 1):
                    if idx == 2 * NGD:
                        high(i * PERW + PRE + 2, (PRE + 2) % 2, base + NG)
                    ns = slice(idx % NGD * GW, (idx % NGD + 1) * GW)
                    if idx < (levels - 1) * NGD:
                        act.wait_ge(S["xy"], i * levels * NGD + idx + 1)
                        act.activation(xmat[:, ns], bank[2 + idx % 2][:, 0:GW], ACT.Copy).then_inc(S["x_out"], 1)
                    if idx:
                        n = (idx - 1) % NGD
                        act.wait_ge(S["xt"], i * (levels - 1) * NGD + idx)
                        act.activation(ymat[:, n * GW:(n + 1) * GW], bank[4 + n % 2][:, 0:GW], ACT.Copy
                                       ).then_inc(S["y_out"], 1)
                for n in range(NGD):
                    act.wait_ge(S["nw"], i * NGD + n + 1)
                    act.activation(xmat[:, n * GW:(n + 1) * GW], bank[n % 2][:, 0:GW], ACT.Copy,
                                   scale=-1.0).then_inc(S["nw_out"], 1)
                for s in range(NT):
                    act.wait_ge(S["vnew"], i * NT + s + 1)
                    if s < NT - 1:
                        act.wait_ge(S["vk_out"], i * (NT - 1) + s + 1)
                    act.activation(vn[:, s % 2], bank[s % 2][:, 0:2 * P].rearrange("p (d v) -> p d v", d=DIRS),
                                   ACT.Copy).then_inc(S["vn_out"], 1)
                    if s == 0:
                        act.wait_ge(S["su"], i * (NT - 1) + 1)
                        if not first:
                            act.wait_ge(S["st_store"], i * 16 * DIRS)
                        act.activation(state0[:, :, :], bank[4][:, 0:2 * P].rearrange("p (d v) -> p d v", d=DIRS),
                                       ACT.Copy).then_inc(S["st0"], 1)
                    if not last:
                        if s == 5:
                            silu_tanh(i + 1, 0)
                        elif s == 6:
                            square(i + 1, 0)
                        elif s == 8:
                            silu_tanh(i + 1, 1)
                        c, g = s // NG, s % NG
                        evac(base + NG + s, (PRE * NG + NG + s) % 2, c, g)
                        if s == NG - 1:
                            high(i * PERW + PRE + 3, (PRE + 3) % 2, base + 2 * NG)
                        elif s == 6:
                            high(i * PERW + PRE + 4, (PRE + 4) % 2, base + 3 * NG)
                    elif s < 2 * NG:
                        act.wait_ge(S["proj_mm"], base + NG + s + 1)
                        evacuate_lru(act, rows, proj[(PRE * NG + NG + s) % 2], s).then_inc(S["proj_out"], 1)
                act.wait_ge(S["acc"], i * NT + NT)
                if not last:
                    act.wait_ge(S["silu"], i * 3 + 5)
                act.activation(cb_[:, 0:TOK], kacc[:, :, :].rearrange("p t c -> p (t c)"),
                               ACT.Square).then_inc(S["osq"], 1)
                if not last:
                    act.wait_ge(S["ss_mm"], i * 2 + 3)
                act.wait_ge(S["proj_out"], base + NG)
                act.activation(cc[:, 0:TOK], zraw[:, :], ACT.Tanh, scale=0.5).then_inc(S["z_t"], 1)

            turns(act, turn)

        @block.tensor
        def _(pe):
            ident = R.m(M_ID)

            def project(gidx, par, slot, g, ks):
                ts = slice(g * GW, (g + 1) * GW)
                for k in ks:
                    mm = split_product(pe, proj[par][:, 0:GW], whi[:, slot, k, :], wlo[:, slot, k, :],
                                       R.hhi[:, k, ts], R.hlo[:, k, ts], k, k == KT - 1)
                if ks[-1] == KT - 1:
                    mm.then_inc(S["proj_mm"], 1)

            for j in range(PRE):
                pe.wait_ge(S["w_lo"], j + 1)
                for g in range(NG):
                    n = j * NG + g
                    if n >= 2:
                        pe.wait_ge(S["proj_out"], n - 1)
                    project(n, n % 2, j % 2, g, range(KT))

            def sums(h, at, src):
                pe.wait_ge(S["sq"], h)
                for t in range(NT):
                    mm = pe.matmul(at[:, t:t + 1], src[:, tile_at(t):tile_at(t) + P],
                                   R.masks[:, M_ONE * P:M_ONE * P + 1], start=True, stop=True)
                mm.then_inc(S["ss_mm"], 1)

            def z_groups(h, gs_, ks=range(KT)):
                pe.wait_ge(S["w_lo"], h * PERW + PRE + 1)
                for g in gs_:
                    pe.wait_ge(S["proj_out"], h * g_ + (PRE * NG + g - 1))
                    project(None, (PRE * NG + g) % 2, PRE % 2, g, ks)

            z_groups(0, (0, 1))
            sums(1, bank[3], cc)

            def turn(i, first, last):
                base = i * g_ + PRE * NG
                pe.wait_ge(S["silu"], i * 3 + 2)
                for t in range(NT):
                    if t == 2 * TG:
                        pe.wait_ge(S["ssk"], i + 1)
                    mm = pe.transpose(bank[KB[t // TG]][:, (t % TG) * P:(t % TG + 1) * P],
                                      ca[:, tile_at(t):tile_at(t) + P], ident)
                    if t % TG == TG - 1:
                        mm.then_inc(S["kt"], 1)
                if not first:
                    pe.wait_ge(S["fin"], i * NG)
                for t in range(NT):
                    mm = pe.transpose(bank[t // TG][:, (t % TG) * P:(t % TG + 1) * P],
                                      cd[:, tile_at(t):tile_at(t) + P], ident)
                    if t % TG == TG - 1:
                        mm.then_inc(S["vt"], 1)
                z_groups(i, (2,), range(KT // 2))
                for t in range(NT):
                    if t % TG == 0:
                        pe.wait_ge(S["kn"], i * NG + t // TG + 1)
                    mm = pe.transpose(bank[KB[t // TG]][:, (t % TG) * P:(t % TG + 1) * P], kn[:, t, :], ident)
                    if t % TG == TG - 1:
                        mm.then_inc(S["knt"], 1)
                pe.wait_ge(S["vt_out"], i * NG + NG)
                for g in range(NG):
                    for d in range(DIRS):
                        n = g * DIRS + d
                        pe.wait_ge(S["gs"], i * NGD + n + 1)
                        if g:
                            pe.wait_ge(S["dexp"], i * NGD + n - 1)
                        pe.matmul(bank[d][:, 0:GW], R.m(M_TRIL if d else M_TRIU), gs[:, n % 2, :],
                                  start=True, stop=True).then_inc(S["dec"], 1)
                    if g == 0:
                        pe.wait_ge(S["knt_out"], i * NG + NG)
                    if g == 2:
                        pe.wait_ge(S["l_raw"], i * NGD + DIRS)
                    for j in range(TG):
                        t, js = TG * g + j, slice(j * P, (j + 1) * P)
                        mm = pe.matmul(bank[2 + g % 2][:, js], kacc[:, t, :], kacc[:, t, :], start=True, stop=True)
                    mm.then_inc(S["kk"], 1)
                z_groups(i, (2,), range(KT // 2, KT))
                pe.wait_ge(S["silu"], i * 3 + 3)
                for g in range(NG):
                    if g == 2:
                        pe.wait_ge(S["proj_out"], base + NG)
                        sums(i * 2 + 2, bank[6], cb_)
                        pe.wait_ge(S["qk"], i * NGD + DIRS)
                    for j in range(TG):
                        t, js = TG * g + j, slice(j * P, (j + 1) * P)
                        mm = pe.matmul(bank[4 + g % 2][:, js], q2[:, tile_at(t):tile_at(t) + P], kacc[:, t, :],
                                       start=True, stop=True)
                    mm.then_inc(S["gq"], 1)
                pe.wait_ge(S["dexp"], i * NGD + NGD)
                for n in range(NGD):
                    pe.wait_ge(S["l_done"], i * NGD + n + 1)
                    if n >= 2:
                        pe.wait_ge(S["y0"], i * NGD + n - 1)
                    for j in range(TG):
                        sl = slice((n * TG + j) * P, (n * TG + j + 1) * P)
                        mm = pe.transpose(bank[n % 2][:, j * P:(j + 1) * P], lmat[:, sl], ident)
                    mm.then_inc(S["lt"], 1)

                def factor(lev, n):
                    idx = lev * NGD + n
                    if lev == 0:
                        pe.wait_ge(S["y0"], i * NGD + min(NGD, n + NGD - 1))
                    else:
                        pe.wait_ge(S["y_out"], i * (levels - 1) * NGD + idx - NGD + 1)
                    if idx >= 2:
                        pe.wait_ge(S["r_out"], i * levels * NGD + idx - 1)
                    for j in range(TG):
                        sl = slice((n * TG + j) * P, (n * TG + j + 1) * P)
                        mm = pe.matmul(bank[n % 2][:, j * P:(j + 1) * P], lmat[:, sl], ymat[:, sl],
                                       start=True, stop=True)
                    mm.then_inc(S["r"], 1)

                def update(lev, n):
                    idx = lev * NGD + n
                    pe.wait_ge(S["r_out"], i * levels * NGD + idx + 1)
                    if lev == 0:
                        pe.wait_ge(S["x0"], i * NGD + n + 1)
                        if n == 0:
                            pe.wait_ge(S["qk"], i * NGD + NGD)
                    if idx >= 2:
                        pe.wait_ge(S["x_out"], i * (levels - 1) * NGD + (idx - 1 if lev < levels - 1 else (levels - 1) * NGD))
                    if lev == levels - 1:
                        if n >= 2:
                            pe.wait_ge(S["yb"], i * NGD + n - 1)
                        else:
                            pe.wait_ge(S["y_out"], i * (levels - 1) * NGD + ((levels - 1) * NGD - 1 + n))
                    for j in range(TG):
                        sl, js = slice((n * TG + j) * P, (n * TG + j + 1) * P), slice(j * P, (j + 1) * P)
                        if lev < levels - 1:
                            mm = pe.matmul(bank[2 + n % 2][:, js], rwork[:, sl], xmat[:, sl], start=True, stop=True)
                        else:
                            mm = pe.matmul(bank[4 + n % 2][:, js], xmat[:, sl], rwork[:, sl], start=True, stop=True)
                    mm.then_inc(S["xy"], 1)

                def turn_over(lev, n):
                    idx = lev * NGD + n
                    pe.wait_ge(S["x_out"], i * (levels - 1) * NGD + idx + 1)
                    if idx >= 2:
                        pe.wait_ge(S["y_out"], i * (levels - 1) * NGD + idx - 1)
                    for j in range(TG):
                        sl = slice((n * TG + j) * P, (n * TG + j + 1) * P)
                        mm = pe.transpose(bank[4 + n % 2][:, j * P:(j + 1) * P], xmat[:, sl], ident)
                    mm.then_inc(S["xt"], 1)

                for idx in range(levels * NGD + 1):
                    if idx < levels * NGD:
                        factor(idx // NGD, idx % NGD)
                    if idx:
                        update((idx - 1) // NGD, (idx - 1) % NGD)
                    if 2 <= idx < (levels - 1) * NGD + 2:
                        turn_over((idx - 2) // NGD, (idx - 2) % NGD)
                for step in range(NGD + 2):
                    if step < NGD:
                        n = step
                        if n >= 2:
                            pe.wait_ge(S["qt_out"], i * NGD + n - 1)
                        for j in range(TG):
                            sl = slice((n * TG + j) * P, (n * TG + j + 1) * P)
                            mm = pe.transpose(bank[2 + n % 2][:, j * P:(j + 1) * P], ework[:, sl], ident)
                        mm.then_inc(S["qt"], 1)
                    if step >= 2:
                        n = step - 2
                        pe.wait_ge(S["ybe"], i * NGD + n + 1)
                        if n >= 2:
                            pe.wait_ge(S["nw_out"], i * NGD + n - 1)
                        for j in range(TG):
                            t = TG * (n // DIRS) + j
                            sl = slice((n * TG + j) * P, (n * TG + j + 1) * P)
                            mm = pe.matmul(bank[n % 2][:, j * P:(j + 1) * P], kn[:, t, :], rwork[:, sl],
                                           start=True, stop=True)
                        mm.then_inc(S["nw"], 1)
                pe.wait_ge(S["nw_out"], i * NGD + NGD)
                pe.wait_ge(S["qt_out"], i * NGD + NGD)
                pe.wait_ge(S["st_in"], i * 16 * DIRS + 16 * DIRS)
                for s in range(NT):
                    b0, b1, b2 = bank[s % 2], bank[2 + s % 2], bank[4 + s % 2]
                    place = [step_tile(s, d) for d in range(DIRS)]
                    if s >= 2:
                        pe.wait_ge(S["st_new"], i * (NT - 2) + s - 1)
                        pe.wait_ge(S["acc"], i * NT + s - 1)
                    for d, (t, n) in enumerate(place):
                        sl, ds_ = slice(n * P, (n + 1) * P), slice(d * P, (d + 1) * P)
                        mm = pe.matmul(b0[:, ds_], ymat[:, sl], vt[:, t, :], start=True, stop=(s == 0))
                        if s:
                            mm = pe.matmul(b0[:, ds_], xmat[:, sl], state[:, d, :], start=False, stop=True)
                    mm.then_inc(S["vnew"], 1)
                    if s:
                        for d, (t, n) in enumerate(place):
                            pe.matmul(b1[:, d * P:(d + 1) * P], q2[:, tile_at(t):tile_at(t) + P], state[:, d, :],
                                      start=True, stop=True)
                    fill = not last or s < 2 * NG
                    if fill:
                        slot, par = (PRE + 1 + s // NG) % 2, (PRE * NG + NG + s) % 2
                        if s % NG == 0:
                            pe.wait_ge(S["w_lo"], i * PERW + PRE + 2 + s // NG)
                        pe.wait_ge(S["proj_out"], base + NG + s - 1)
                        project(None, par, slot, s % NG, range(KT // 2))
                    if s < NT - 1:
                        pe.wait_ge(S["vk_out"], i * (NT - 1) + s + 1)
                        if s == 2:
                            pe.wait_ge(S["st0"], i + 1)
                        for d, (t, n) in enumerate(place):
                            mm = pe.matmul(b2[:, d * P:(d + 1) * P], kn[:, t, :], vk[:, s % 2, d, :],
                                           start=True, stop=True)
                        mm.then_inc(S["su"], 1)
                    pe.wait_ge(S["vn_out"], i * NT + s + 1)
                    for d, (t, n) in enumerate(place):
                        mm = pe.matmul(b1[:, (2 + d) * P:(3 + d) * P], lmat[:, n * P:(n + 1) * P], vn[:, s % 2, d, :],
                                       start=True, stop=True)
                    mm.then_inc(S["ov"], 1)
                    if fill:
                        project(None, par, slot, s % NG, range(KT // 2, KT))
                if not last:
                    pe.wait_ge(S["acc"], i * NT + NT - 1)
                    sums(i * 2 + 3, bank[3], cc)
                    z_groups(i + 1, (0, 1))
                pe.wait_ge(S["ofac"], i + 1)
                for t in range(NT):
                    mm = pe.transpose(bank[t // TG][:, (t % TG) * P:(t % TG + 1) * P], kacc[:, t, :], ident)
                    if t % TG == TG - 1:
                        mm.then_inc(S["ot"], 1)

            turns(pe, turn)

        @block.vector
        def _(dve):
            n_own = [0]

            def link(ins, turn):
                n_own[0] += 1
                ins.then_inc(S["own"], 1)
                dve.wait_ge(S["own"], n_own[0] if turn is None else turn * DVE_OWN + (OWN0 + n_own[0]))

            def taps_in(h, hs):
                dve.tensor_copy(cw[:, :, :, :], R.par[:, PA_CONV:PA_CONV + 120].rearrange(
                    "p (a b c) -> p a b c", a=5, b=3)[:, :, :, hs]).then_inc(S["cw"], 1)
                dve.wait_ge(S["cw"], h + 1)

            def conv(h, s, taps, turn):
                dst, c = (ca, cd, q2[:, :])[s], QKV[s]
                for a in taps:
                    if a == 0:
                        dve.wait_ge(S["proj_out"], h * g_ + (s + 1) * NG)
                        ins = dve.tensor_scalar(dst, raw[s][:, 0:CONV], cw[:, 0, c, 0:1], cw[:, 4, c, 0:1],
                                                ALU.mult, ALU.add)
                    else:
                        ins = dve.scalar_tensor_tensor(out=dst, in0=raw[s][:, a:a + CONV], scalar=cw[:, a, c, 0:1],
                                                       in1=dst, op0=ALU.mult, op1=ALU.add)
                    if a < TAPS - 1:
                        link(ins, turn)
                    else:
                        ins.then_inc(S["taps"], 1)

            def silu(h, s):
                dst = (ca, cd, q2[:, :])[s]
                dve.wait_ge(S["silu_t"], h * 3 + s + 1)
                dve.scalar_tensor_tensor(out=dst, in0=cb_, scalar=1.0, in1=dst, op0=ALU.add,
                                         op1=ALU.mult).then_inc(S["silu"], 1)

            def norm_k(h):
                dve.wait_ge(S["ss_mm"], h * 2 + 1)
                dve.tensor_scalar(ssk[:, :], bank[3][:, 0:NT], 4 * EPS, None, ALU.add).then_inc(S["ssk"], 1)

            taps_in(0, slice(0, 1))
            for s in range(2):
                conv(0, s, range(TAPS), None)
                silu(0, s)
            norm_k(0)
            OWN0 = n_own[0]

            def turn(i, first, last):
                n_own[0] = 0
                hs = slice(i, i + 1) if first or last else bass.ds(i, 1)
                if not first:
                    dve.wait_ge(S["ybe"], i * NGD)
                dve.tensor_copy(gh[:, :, :, :], R.gates[:, :, :, hs]).then_inc(S["par"], 1)
                dve.wait_ge(S["par"], i + 1)
                dve.wait_ge(S["rk"], i + 1)
                for g in range(NG):
                    dve.wait_ge(S["kt"], i * NG + g + 1)
                    gsl = slice(TG * g, TG * (g + 1))
                    dve.tensor_tensor(kn[:, gsl, :], v3(bank[KB[g]][:, 0:GW]), cols(rk[:, gsl], TG),
                                      ALU.mult).then_inc(S["kn"], 1)
                conv(i, 2, range(TAPS), i)
                for n in range(NGD):
                    g = n // DIRS
                    dve.wait_ge(S["dmask"], i * NGD + n + 1)
                    dve.wait_ge(S["kk"], i * NG + g + 1)
                    for j in range(TG):
                        sl = slice((n * TG + j) * P, (n * TG + j + 1) * P)
                        ins = dve.scalar_tensor_tensor(out=lmat[:, sl], in0=bank[2 + g % 2][:, j * P:(j + 1) * P],
                                                       scalar=gh[:, G_BETA, n * TG + j, 0:1], in1=ework[:, sl],
                                                       op0=ALU.mult, op1=ALU.mult)
                    ins.then_inc(S["l_raw"], 1)
                    if n == 1:
                        silu(i, 2)
                dve.wait_ge(S["l_raw"], i * NGD + NGD)
                for n in range(NGD):
                    g, ns = n // DIRS, slice(n * GW, (n + 1) * GW)
                    dve.wait_ge(S["gq"], i * NG + g + 1)
                    dve.tensor_tensor(ework[:, ns], bank[4 + g % 2][:, 0:GW], ework[:, ns], ALU.mult
                                      ).then_inc(S["qk"], 1)
                dve.wait_ge(S["ss_mm"], i * 2 + 2)
                dve.tensor_scalar(ssq[:, :], bank[6][:, 0:NT], P * EPS, P * EPS * 4 * EPS, ALU.mult,
                                  ALU.add).then_inc(S["ssq"], 1)
                for n in range(NGD):
                    dve.wait_ge(S["lt"], i * NGD + n + 1)
                    dve.tensor_tensor(v3(ymat[:, n * GW:(n + 1) * GW]), v3(bank[n % 2][:, 0:GW]),
                                      bc(R.level(0, n % DIRS), TG), ALU.mult).then_inc(S["y0"], 1)
                for lev in range(levels):
                    for n in range(NGD):
                        idx = lev * NGD + n
                        dve.wait_ge(S["r"], i * levels * NGD + idx + 1)
                        if lev:
                            dve.wait_ge(S["xy"], i * levels * NGD + idx - NGD + 1)
                        dve.tensor_tensor(v3(rwork[:, n * GW:(n + 1) * GW]), v3(bank[n % 2][:, 0:GW]),
                                          bc(R.level(lev + 1, n % DIRS), TG), ALU.mult).then_inc(S["r_out"], 1)
                        if lev == levels - 1 and n:
                            inverse_out(i, n - 1)
                inverse_out(i, NGD - 1)
                for n in range(NGD):
                    dve.wait_ge(S["qt"], i * NGD + n + 1)
                    dve.tensor_copy(lmat[:, n * GW:(n + 1) * GW], bank[2 + n % 2][:, 0:GW]).then_inc(S["qt_out"], 1)
                for s in range(NT):
                    b0, b1, b2 = bank[s % 2], bank[2 + s % 2], bank[4 + s % 2]
                    place = [step_tile(s, d) for d in range(DIRS)]
                    if s < NT - 1:
                        dve.wait_ge(S["vnew"], i * NT + s + 1)
                        for d, (t, n) in enumerate(place):
                            ins = dve.tensor_scalar(vk[:, s % 2, d, :], b0[:, d * P:(d + 1) * P],
                                                    gh[:, G_EXPREST, n, 0:1], None, ALU.mult)
                        ins.then_inc(S["vk_out"], 1)
                        if s:
                            dve.wait_ge(S["su"], i * (NT - 1) + s + 1)
                            if s >= 2:
                                dve.wait_ge(S["st_new"], i * (NT - 2) + s - 1)
                            for d, (t, n) in enumerate(place):
                                ins = dve.scalar_tensor_tensor(out=state[:, d, :], in0=state[:, d, :],
                                                               scalar=gh[:, G_EXPALL, n, 0:1],
                                                               in1=b2[:, d * P:(d + 1) * P], op0=ALU.mult, op1=ALU.add)
                            ins.then_inc(S["st_new"], 1)
                    dve.wait_ge(S["ov"], i * NT + s + 1)
                    if s:
                        for d, (t, n) in enumerate(place):
                            eg = gh[:, G_EXPCUM, n, 0:1]
                            if s <= NT // 2:
                                ins = dve.tensor_scalar(kacc[:, t, :], b1[:, d * P:(d + 1) * P], eg, None, ALU.mult)
                            else:
                                ins = dve.scalar_tensor_tensor(out=kacc[:, t, :], in0=b1[:, d * P:(d + 1) * P], scalar=eg,
                                                               in1=kacc[:, t, :], op0=ALU.mult, op1=ALU.add)
                        link(ins, i)
                        for d, (t, n) in enumerate(place):
                            ins = dve.tensor_tensor(kacc[:, t, :], b1[:, (2 + d) * P:(3 + d) * P], kacc[:, t, :], ALU.add)
                        ins.then_inc(S["acc"], 1)
                        dve.wait_ge(S["acc"], i * NT + s + 1)
                    else:
                        link(dve.tensor_copy(kacc[:, 0, :], b1[:, 2 * P:3 * P]), i)
                        dve.tensor_tensor(kacc[:, 0, :], b1[:, 3 * P:4 * P], kacc[:, 0, :], ALU.add).then_inc(S["acc"], 1)
                    if not last:
                        if s == 2:
                            taps_in(i + 1, slice(1, 2) if first else bass.ds(i + 1, 1))
                        elif s == 5:
                            silu(i + 1, 0)
                        elif s == 8:
                            silu(i + 1, 1)
                            norm_k(i + 1)
                        elif s > 2:
                            conv(i + 1, s // 5, ((0, 1), (2, 3))[(s - 3) % 3], i)
                dve.wait_ge(S["osq"], i + 1)
                link(dve.tensor_reduce(sso[:, :], v3(cb_[:, 0:TOK]), AX.X, ALU.add), i)
                dve.scalar_tensor_tensor(out=sso[:, :], in0=sso[:, :], scalar=1.0 / P, in1=ssq[:, :], op0=ALU.mult,
                                         op1=ALU.add).then_inc(S["osum"], 1)
                dve.wait_ge(S["ro"], i + 1)
                dve.tensor_tensor(kacc[:, :, :], kacc[:, :, :], cols(ro[:, :], NT), ALU.mult).then_inc(S["ofac"], 1)
                dve.wait_ge(S["z_t"], i + 1)
                link(dve.scalar_tensor_tensor(out=zraw[:, :], in0=cc[:, 0:TOK], scalar=1.0, in1=zraw[:, :],
                                              op0=ALU.add, op1=ALU.mult), i)
                for g in range(NG):
                    gsl = slice(g * GW, (g + 1) * GW)
                    dve.wait_ge(S["ot"], i * NG + g + 1)
                    dve.scalar_tensor_tensor(out=cc[:, gsl], in0=bank[g][:, 0:GW], scalar=R.par[:, PB_ONORM:PB_ONORM + 1],
                                             in1=zraw[:, gsl], op0=ALU.mult, op1=ALU.mult).then_inc(S["fin"], 1)
                assert last or n_own[0] == DVE_OWN

            def inverse_out(i, n):
                dve.wait_ge(S["xy"], i * levels * NGD + (levels - 1) * NGD + n + 1)
                dve.tensor_tensor(v3(ymat[:, n * GW:(n + 1) * GW]), v3(bank[4 + n % 2][:, 0:GW]),
                                  gh[:, G_BETA, n * TG:(n + 1) * TG, 0:1].broadcast_to([P, TG, P]),
                                  ALU.mult).then_inc(S["yb"], 1)

            DVE_OWN = 3 * (TAPS - 1) + NT + 2
            turns(dve, turn)


def step_tile(s, d):
    t = s if (s == 0 or d == 0) else NT - s
    return t, (t // TG * DIRS + d) * TG + t % TG


class Shared:

    def __init__(self, nc, ctx):
        sb = lambda name, shape, dt=F32: ctx.enter_context(nc.sbuf_tensor(name, shape, dt))
        self.wst = sb("s_w", [P, 2, KT, P])
        self.whi = sb("s_w_hi", [P, 2, KT, P], F32R)
        self.wlo = sb("s_w_lo", [P, 2, KT, P], F32R)
        self.bank = [ctx.enter_context(nc.psum_tensor(f"mb{i}", [P, 512], F32)) for i in range(8)]
        self.sems = {n: ctx.enter_context(nc.semaphore("m_" + n)) for n in ("w_in0", "w_in1", "w_hi", "w_lo", "mm")}


def lru_stage(nc, R, A, ob, shared, rows):
    with ExitStack() as ctx:
        sb = lambda name, shape, dt=F32: ctx.enter_context(nc.sbuf_tensor(name, shape, dt))
        sem = lambda name: ctx.enter_context(nc.semaphore(name))
        wst, whi, wlo, bank, M = shared.wst, shared.whi, shared.wlo, shared.bank, shared.sems
        gw = sb("l_gate_w", [P, 4, P])
        raw = rows[:, 0, :]
        zraw = rows[:, 1, 0:TOK]
        z2 = sb("l_z2", [P, TOK])
        xc = sb("l_xc", [P, CONV])
        tg = sb("l_tg", [P, 4, CONV])
        a = sb("l_a", [P, DIRS, CONV])
        th = sb("l_th", [P, DIRS, CONV])
        out = sb("l_out", [P, TOK])
        lp = sb("l_par", [P, NLP, 1])
        rate = sb("l_rate", [P, 2, DIRS, 1])
        h0 = sb("l_h0", [P, DIRS, 1])
        nb = sb("l_newb", [DIRS * H, P])
        proj = bank[6:8]
        S = {n: sem("l_" + n) for n in (
            "w_in0", "w_in1", "gw_in", "w_hi", "w_lo", "proj_mm", "proj_out", "par", "taps", "own", "gate_mm", "gate_t",
            "z_t", "z2", "a", "th", "a2", "m", "root", "p", "b", "scan", "states", "out", "store", "nb_t", "nb")}
        block = ctx.enter_context(nc.Block())
        w_in = A["w_in"][0].rearrange("(k p) n -> p k n", p=P)
        w_gate = A["w_gate"][0].rearrange("(k p) n -> p k n", p=P)
        gate_w = [A[n][0] for n in ("lru_wa_fwd", "lru_wx_fwd", "lru_wa_bwd", "lru_wx_bwd")]
        PER = 2
        g_ = PER * NG
        GN = CONV // NG
        NGATE = 4 * NG

        def turns(eng, body):
            body(0, True, False)
            with eng.Fori(1, H - 1) as i:
                body(i, False, False)
            body(H - 1, False, True)

        @block.sync
        def _(sp):
            for k in range(4):
                sp.dma_start(gw[:, k, :], gate_w[k][0]).then_inc(S["gw_in"], 16)
            for j in range(PER):
                sp.dma_start(wst[:, j, :, :], w_in[:, :, bass.ds((4 + j) * D + P, P)]).then_inc(S[f"w_in{j}"], 16)

            def turn(i, ahead):
                val = int if isinstance(i, int) else sp.snap
                outs, row = val(i * 2 + 2), val(i * P)
                if ahead == 0:
                    for j in range(2):
                        sp.wait_ge(M["w_lo"], j + 1)
                        sp.dma_start(wst[:, j, :, :], w_gate[:, :, (2 + j) * P:(3 + j) * P]).then_inc(M[f"w_in{j}"], 16)
                if ahead > 1:
                    c = [val(i * P + ((4 + j) * D + 2 * P)) for j in range(PER)]
                    need = [val(i * PER + j + 1) for j in range(PER)]
                    for j in range(PER):
                        sp.wait_ge(S["w_lo"], need[j])
                        sp.dma_start(wst[:, j, :, :], w_in[:, :, bass.ds(c[j], P)]).then_inc(S[f"w_in{j}"], 16)
                if ahead == 1:
                    for j in range(2):
                        sp.wait_ge(S["w_lo"], i * PER + j + 1)
                        sp.dma_start(wst[:, j, :, :], w_gate[:, :, j * P:(j + 1) * P]).then_inc(M[f"w_in{j}"], 16)
                if ahead > 0:
                    nxt, gm = val(i * 1 + 1), val(i * NGATE + NGATE)
                    sp.wait_ge(S["gate_mm"], gm)
                    for k in range(4):
                        sp.dma_start(gw[:, k, :], gate_w[k][bass.ds(nxt, 1)].rearrange("a i j -> i (a j)")
                                     ).then_inc(S["gw_in"], 16)
                sp.wait_ge(S["out"], outs)
                sp.dma_start(ob[bass.ds(row, P), :], out[:, :]).then_inc(S["store"], 16)

            turn(0, 2)
            with sp.Fori(1, H - 2) as i:
                turn(i, 2)
            turn(H - 2, 1)
            turn(H - 1, 0)
            for d, name in enumerate(("new_bf", "new_bb")):
                sp.wait_ge(S["nb"], 1)
                sp.dma_start(A[name][0, 0].rearrange("(r p) -> r p", p=P), nb[d * H:(d + 1) * H, :]
                             ).then_inc(S["store"], 16)
            sp.wait_ge(S["store"], 16 * (H + DIRS))

        @block.gpsimd
        def _(pool):
            def low(j, slot):
                pool.wait_ge(S["w_hi"], j + 1)
                pool.tensor_tensor(wlo[:, slot], wst[:, slot], whi[:, slot].bitcast(F32),
                                   ALU.subtract).then_inc(S["w_lo"], 1)

            def turn(i, first, last):
                if not last:
                    for j in range(PER):
                        low(i * PER + j, j)
                else:
                    for j in range(2):
                        pool.wait_ge(M["w_hi"], j + 1)
                        pool.tensor_tensor(wlo[:, j], wst[:, j], whi[:, j].bitcast(F32),
                                           ALU.subtract).then_inc(M["w_lo"], 1)
                    pool.wait_ge(M["w_hi"], 3)
                    pool.tensor_tensor(wlo[:, 0], wst[:, 0], whi[:, 0].bitcast(F32), ALU.subtract
                                       ).then_inc(M["w_lo"], 1)

            turns(pool, turn)

        @block.scalar
        def _(act):
            def high(turn, slot, mm):
                act.wait_ge(S[f"w_in{slot}"], 16 * turn + 16)
                if mm is not None:
                    act.wait_ge(S["proj_mm"], mm)
                act.activation(whi[:, slot], wst[:, slot], ACT.Copy).then_inc(S["w_hi"], 1)

            def evac(gidx, par, q):
                act.wait_ge(S["proj_mm"], gidx + 1)
                evacuate_lru(act, rows, proj[par], q).then_inc(S["proj_out"], 1)

            def turn(i, first, last):
                base = i * g_
                if not last:
                    for j in range(PER):
                        high(i, j, None if first else i * g_ + ((j + 1) * NG - g_))
                else:
                    for j in range(2):
                        act.wait_ge(M[f"w_in{j}"], 16)
                        act.wait_ge(S["proj_mm"], (H - 1) * g_)
                        act.activation(whi[:, j], wst[:, j], ACT.Copy).then_inc(M["w_hi"], 1)
                if not first:
                    act.wait_ge(S["z2"], i)
                if not first:
                    act.wait_ge(S["b"], i * DIRS)
                if not first:
                    act.wait_ge(S["proj_out"], base)
                act.activation(th[:, 0, 0:TOK], zraw[:, :], ACT.Tanh, scale=0.5).then_inc(S["z_t"], 1)
                act.wait_ge(S["taps"], i + 1)
                if not first:
                    act.wait_ge(S["scan"], i * 4)
                if not first:
                    act.wait_ge(S["out"], i * 2)
                for n in range(NGATE):
                    kind, g = n % 4, n // 4
                    act.wait_ge(S["gate_mm"], i * NGATE + n + 1)
                    act.activation(tg[:, kind, g * GN:(g + 1) * GN], bank[n % 6][:, 0:GN], ACT.Tanh, scale=0.5,
                                   bias=lp[:, 5 + kind, 0:1]).then_inc(S["gate_t"], 1)
                act.wait_ge(S["gate_t"], i * NGATE + NGATE)
                act.wait_ge(S["z2"], i + 1)
                for d in range(DIRS):
                    act.activation(a[:, d, :], tg[:, 2 * d, :], ACT.Exp, scale=rate[:, 1, d, 0:1],
                                   bias=rate[:, 1, d, 0:1]).then_inc(S["a"], 1)
                    act.activation(th[:, d, :], tg[:, 2 * d, :], ACT.Tanh, scale=rate[:, 0, d, 0:1],
                                   bias=rate[:, 0, d, 0:1]).then_inc(S["th"], 1)
                if not last:
                    evac(base, 0, 0)
                for d in range(DIRS):
                    act.wait_ge(S["a"], i * DIRS + d + 1)
                    act.wait_ge(S["th"], i * DIRS + d + 1)
                    act.activation(tg[:, 2 * d, :], a[:, d, :], ACT.Square).then_inc(S["a2"], 1)
                if not last:
                    evac(base + 1, 1, 1)
                for d in range(DIRS):
                    act.wait_ge(S["m"], i * DIRS + d + 1)
                    act.activation(th[:, d, :], th[:, d, :], ACT.Sqrt, scale=0.25).then_inc(S["root"], 1)
                if not last:
                    for q in range(2, g_):
                        evac(base + q, q % 2, q)
                else:
                    act.wait_ge(M["w_in0"], 32)
                    act.wait_ge(M["mm"], NG)
                    act.activation(whi[:, 0], wst[:, 0], ACT.Copy).then_inc(M["w_hi"], 1)

            turns(act, turn)

        @block.tensor
        def _(pe):
            def project(base, q):
                slot, g = q // NG, q % NG
                ts = slice(g * GW, (g + 1) * GW)
                for k in range(KT):
                    mm = split_product(pe, proj[q % 2][:, 0:GW], whi[:, slot, k, :], wlo[:, slot, k, :],
                                       R.hhi[:, k, ts], R.hlo[:, k, ts], k, k == KT - 1)
                mm.then_inc(S["proj_mm"], 1)

            def turn(i, first, last):
                base = i * g_
                for n in range(NGATE):
                    kind, g = n % 4, n // 4
                    if n == 0:
                        pe.wait_ge(S["taps"], i + 1)
                        pe.wait_ge(S["gw_in"], i * 64 + 64)
                    if n >= 6:
                        pe.wait_ge(S["gate_t"], i * NGATE + n - 5)
                    elif n == 0 and not first:
                        pe.wait_ge(S["gate_t"], i * NGATE)
                    pe.matmul(bank[n % 6][:, 0:GN], gw[:, kind, :], xc[:, g * GN:(g + 1) * GN],
                              start=True, stop=True).then_inc(S["gate_mm"], 1)
                if not last:
                    for q in range(g_):
                        if q % NG == 0:
                            pe.wait_ge(S["w_lo"], i * PER + q // NG + 1)
                        if not first or q >= 2:
                            pe.wait_ge(S["proj_out"], base + q - 1)
                        project(base, q)
                else:
                    pe.wait_ge(S["gate_t"], H * NGATE)
                    for j in range(2):
                        pe.wait_ge(M["w_lo"], j + 1)
                        for g in range(NG):
                            ts = slice(g * GW, (g + 1) * GW)
                            for k in range(KT):
                                mm = split_product(pe, bank[j * NG + g][:, 0:GW], whi[:, j, k, :], wlo[:, j, k, :],
                                                   R.hhi[:, k, ts], R.hlo[:, k, ts], k, k == KT - 1)
                            mm.then_inc(M["mm"], 1)

            turns(pe, turn)
            pe.wait_ge(S["states"], H * DIRS)
            pe.wait_ge(S["proj_out"], (H - 1) * g_)
            pe.transpose(bank[7][0:DIRS * H, 0:P], R.newb[:, :, :].rearrange("p d h -> p (d h)"),
                         R.m(M_ID)).then_inc(S["nb_t"], 1)

        @block.vector
        def _(dve):
            OWN = TAPS

            n_own = [0]

            def link(ins, turn):
                n_own[0] += 1
                ins.then_inc(S["own"], 1)
                dve.wait_ge(S["own"], n_own[0] if turn is None else turn * OWN + (TAPS - 1 + n_own[0]))

            def convolve(i, turn, hs):
                dve.tensor_copy(lp[:, :, :], R.par[:, PB_LRU:PB_LRU + NLP * H].rearrange(
                    "p (a c) -> p a c", c=H)[:, :, hs]).then_inc(S["par"], 1)
                dve.tensor_copy(rate[:, :, :, :], R.rate[:, :, :, hs]).then_inc(S["par"], 1)
                dve.tensor_copy(h0[:, :, :], R.par[:, PC + 16:PC + 32].rearrange(
                    "p (d c) -> p d c", c=H)[:, :, hs]).then_inc(S["par"], 1)
                dve.wait_ge(S["par"], i * 3 + 3)
                if turn is not None:
                    dve.wait_ge(S["proj_out"], turn * g_ + NG)
                link(dve.tensor_scalar(xc[:, :], raw[:, 0:CONV], lp[:, 0, 0:1], lp[:, 4, 0:1], ALU.mult, ALU.add), turn)
                for k in range(1, TAPS):
                    ins = dve.scalar_tensor_tensor(out=xc[:, :], in0=raw[:, k:k + CONV], scalar=lp[:, k, 0:1],
                                                   in1=xc[:, :], op0=ALU.mult, op1=ALU.add)
                    if k < TAPS - 1:
                        link(ins, turn)
                ins.then_inc(S["taps"], 1)

            convolve(0, None, slice(0, 1))

            def turn(i, first, last):
                n_own[0] = 0
                hs = slice(i, i + 1) if first or last else bass.ds(i, 1)
                dve.wait_ge(S["z_t"], i + 1)
                if not first:
                    dve.wait_ge(S["out"], i * 2)
                dve.scalar_tensor_tensor(out=z2[:, :], in0=th[:, 0, 0:TOK], scalar=1.0, in1=zraw[:, :], op0=ALU.add,
                                         op1=ALU.mult).then_inc(S["z2"], 1)
                dve.wait_ge(S["gate_t"], i * NGATE + NGATE)
                dve.wait_ge(S["taps"], i + 1)
                for d in range(DIRS):
                    dve.scalar_tensor_tensor(out=tg[:, 2 * d + 1, :], in0=tg[:, 2 * d + 1, :], scalar=1.0,
                                             in1=xc[:, :], op0=ALU.add, op1=ALU.mult).then_inc(S["p"], 1)
                for d in range(DIRS):
                    dve.wait_ge(S["a2"], i * DIRS + d + 1)
                    dve.scalar_tensor_tensor(out=th[:, d, :], in0=tg[:, 2 * d, :], scalar=1.0, in1=th[:, d, :],
                                             op0=ALU.add, op1=ALU.mult).then_inc(S["m"], 1)
                for d in range(DIRS):
                    dve.wait_ge(S["root"], i * DIRS + d + 1)
                    dve.wait_ge(S["p"], i * DIRS + d + 1)
                    dve.tensor_tensor(tg[:, 2 * d + 1, :], tg[:, 2 * d + 1, :], th[:, d, :],
                                      ALU.mult).then_inc(S["b"], 1)
                for d in range(DIRS):
                    dve.wait_ge(S["b"], i * DIRS + d + 1)
                    for c0, c1, init in ((0, CTX, 0.0), (LAT0, CONV, h0[:, d, 0:1])):
                        rows = [v[:, c0:c1] if d == 0 else v[:, c0:c1][:, ::-1]
                                for v in (tg[:, 2 * d, :], a[:, d, :], tg[:, 2 * d + 1, :])]
                        dve.tensor_tensor_scan(rows[0], rows[1], rows[2], init, ALU.mult, ALU.add
                                               ).then_inc(S["scan"], 1)
                dve.wait_ge(S["scan"], i * 4 + 4)
                for d in range(DIRS):
                    end = CTX - 1 if d == 0 else 0
                    dve.tensor_copy(R.newb[:, d, hs], tg[:, 2 * d, end:end + 1]).then_inc(S["states"], 1)
                if not last:
                    convolve(i + 1, i, slice(1, 2) if first else bass.ds(i + 1, 1))
                if not first:
                    dve.wait_ge(S["store"], i * 16)
                link(dve.tensor_tensor(tg[:, 1, :], tg[:, 0, :], tg[:, 2, :], ALU.add), i)
                dve.scalar_tensor_tensor(out=out[:, 0:CTX], in0=tg[:, 1, 0:CTX], scalar=0.5, in1=z2[:, 0:CTX],
                                         op0=ALU.mult, op1=ALU.mult).then_inc(S["out"], 1)
                rw = lambda v: v.rearrange("p (r w) -> p r w", w=GRID_W)
                dve.scalar_tensor_tensor(
                    out=rw(out[:, CTX:TOK]), in0=tg[:, 1, LAT0:CONV].rearrange("p (w r) -> p r w", r=GRID_R),
                    scalar=0.5, in1=rw(z2[:, CTX:TOK]), op0=ALU.mult, op1=ALU.mult).then_inc(S["out"], 1)
                assert last or n_own[0] == OWN

            turns(dve, turn)
            dve.wait_ge(S["nb_t"], 1)
            dve.tensor_copy(nb[:, :], bank[7][0:DIRS * H, 0:P]).then_inc(S["nb"], 1)


def merge_stage(nc, R, A, oa, ob, mixed, shared, rows):
    with ExitStack() as ctx:
        sb = lambda name, shape, dt=F32: ctx.enter_context(nc.sbuf_tensor(name, shape, dt))
        sem = lambda name: ctx.enter_context(nc.semaphore(name))
        NO = 3
        wst, whi, wlo, bank = shared.wst, shared.whi, shared.wlo, shared.bank
        sgb = sb("m_gates", [P, KT, TOK])
        ost2 = sb("m_o", [P, TOK])
        ost = (rows[:, 0, 0:TOK], rows[:, 1, 0:TOK], ost2[:, :])
        tmp = sb("m_tmp", [P, 2, GW])
        bg = sb("m_bias", [P, 2])
        S = {n: sem("m_" + n) for n in ("gate", "bias", "o_in0", "o_in1", "o_in2", "o_hi", "o_lo", "fold", "mix")}
        S.update(shared.sems)
        block = ctx.enter_context(nc.Block())
        w_gate = A["w_gate"][0].rearrange("(k p) n -> p k n", p=P)
        w_br = [A[n][0].rearrange("(k p) n -> p k n", p=P) for n in ("w_proj_a", "w_proj_b")]
        NM_ = 2 * KT
        SKEW = 2

        @block.sync
        def _(sp):
            def load(src, col, slot, need):
                sp.wait_ge(S["w_lo"], need)
                sp.dma_start(wst[:, slot, :, :], src[:, :, bass.ds(col, P)]).then_inc(S[f"w_in{slot}"], 16)

            with sp.Fori(2, NM_ // 2) as i:
                c = [sp.snap(i * 2 * P + s * P) for s in range(2)]
                need = [sp.snap(i * 2 + s - 1) for s in range(2)]
                for s in range(2):
                    load(w_gate, c[s], s, need[s])
            for br in range(2):
                for s in range(2):
                    load(w_br[br], s * P, s, NM_ + br * KT + s - 1)
                for k in range(KT):
                    n = br * KT + k
                    if n >= NO:
                        sp.wait_ge(S["o_lo"], n - NO + 1)
                    sp.dma_start(ost[n % NO], (oa, ob)[br][k * P:(k + 1) * P, :]).then_inc(S[f"o_in{n % NO}"], 16)
                with sp.Fori(1, KT // 2) as i:
                    c = [sp.snap(i * 2 * P + s * P) for s in range(2)]
                    need = [sp.snap(i * 2 + NM_ + br * KT + s - 1) for s in range(2)]
                    for s in range(2):
                        load(w_br[br], c[s], s, need[s])

        @block.gpsimd
        def _(pool):
            def low(j, slot):
                pool.wait_ge(S["w_hi"], j + 1)
                pool.tensor_tensor(wlo[:, slot], wst[:, slot], whi[:, slot].bitcast(F32),
                                   ALU.subtract).then_inc(S["w_lo"], 1)

            low(3, 1)
            with pool.Fori(2, NM_) as i:
                for s in range(2):
                    low(i * 2 + s, s)

        @block.scalar
        def _(act):
            def high(turn, slot, mm):
                act.wait_ge(S[f"w_in{slot}"], 16 * turn + 16)
                if mm is not None:
                    act.wait_ge(S["mm"], mm)
                act.activation(whi[:, slot], wst[:, slot], ACT.Copy).then_inc(S["w_hi"], 1)

            def gates(br, i, head):
                    sg = (mixed, sgb)[br]
                    for s in range(2):
                        act.wait_ge(S["bias"], i * 2 + br * KT + s + 1)
                        for g in range(NG):
                            n = s * NG + g
                            act.wait_ge(S["mm"], i * 2 * NG + br * KT * NG + n + 1)
                            act.activation(sg[:, bass.ds(i * 2 + s, 1), g * GW:(g + 1) * GW].rearrange("p a n -> p (a n)"),
                                           bank[n][:, 0:GW], ACT.Tanh, scale=0.5,
                                           bias=bg[:, s:s + 1]).then_inc(S["gate"], 1)
                        if not head or s:
                            high(i + (br * KT // 2 + 1), s, i * 2 * NG + br * KT * NG + (s + 1) * NG)

            gates(0, 0, True)
            with act.Fori(1, KT // 2) as i:
                gates(0, i, False)
            with act.Fori(0, KT // 2) as i:
                gates(1, i, False)
            for br in range(2):
                base = (NM_ + br * KT) * NG
                act.wait_ge(S["mm"], base)
                for k in range(KT):
                    n = br * KT + k
                    act.wait_ge(S[f"o_in{n % NO}"], 16 * (n // NO + 1))
                    act.activation(R.hhi[:, k, :], ost[n % NO], ACT.Copy).then_inc(S["o_hi"], 1)
                with act.Fori(0, KT // 2 - (1 if br else 0)) as i:
                    for s in range(2):
                        high(i + ((NM_ + br * KT) // 2 + 1), s, i * 2 * NG + base + (s + 1) * NG)

        @block.tensor
        def _(pe):
            def project(j, slot, free):
                pe.wait_ge(S["w_lo"], j + 1)
                for g in range(NG):
                    ts = slice(g * GW, (g + 1) * GW)
                    if free is not None:
                        pe.wait_ge(free[0], free[1] + g)
                    for k in range(KT):
                        mm = split_product(pe, bank[slot * NG + g][:, 0:GW], whi[:, slot, k, :], wlo[:, slot, k, :],
                                           R.hhi[:, k, ts], R.hlo[:, k, ts], k, k == KT - 1)
                    mm.then_inc(S["mm"], 1)

            def first_pair(br):
                pe.wait_ge(S["w_lo"], NM_ + br * KT + 2)
                if br:
                    pe.wait_ge(S["fold"], KT * NG)
                for step in range(KT + SKEW):
                    for s in range(2):
                        k = step - SKEW * s
                        if not 0 <= k < KT:
                            continue
                        if s == 0:
                            pe.wait_ge(S["o_lo"], br * KT + k + 1)
                        for g in range(NG):
                            ts = slice(g * GW, (g + 1) * GW)
                            mm = split_product(pe, bank[s * NG + g][:, 0:GW], whi[:, s, k, :], wlo[:, s, k, :],
                                               R.hhi[:, k, ts], R.hlo[:, k, ts], k, k == KT - 1)
                            if k == KT - 1:
                                mm.then_inc(S["mm"], 1)

            with pe.Fori(1, NM_ // 2) as i:
                for s in range(2):
                    project(i * 2 + s, s, (S["gate"], i * 2 * NG + (s - 2) * NG + 1))
            pe.wait_ge(S["gate"], NM_ * NG)
            for br in range(2):
                first = br * KT * NG
                first_pair(br)
                with pe.Fori(1, KT // 2) as i:
                    for s in range(2):
                        project(i * 2 + NM_ + br * KT + s, s, (S["fold"], i * 2 * NG + first + (s - 2) * NG + 1))

        @block.vector
        def _(dve):
            for s in range(2):
                dve.tensor_copy(bg[:, s:s + 1], R.par[:, PB_GATE + s:PB_GATE + s + 1]).then_inc(S["bias"], 1)
            with dve.Fori(1, NM_ // 2) as i:
                for s in range(2):
                    dve.wait_ge(S["gate"], i * 2 * NG)
                    dve.tensor_copy(bg[:, s:s + 1], R.par[:, bass.ds(i * 2 + (PB_GATE + s), 1)]).then_inc(S["bias"], 1)
            dve.wait_ge(S["gate"], NM_ * NG)
            def fold(br, i, first):
                    for s in range(2):
                        for g in range(NG):
                            gsl = slice(g * GW, (g + 1) * GW)
                            n = s * NG + g
                            at = lambda v: v[:, bass.ds(i * 2 + s, 1), gsl].rearrange("p a n -> p (a n)")
                            dve.wait_ge(S["mm"], i * 2 * NG + (NM_ + br * KT) * NG + n + 1)
                            ps = bank[s * NG + g][:, 0:GW]
                            if br == 0:
                                dve.scalar_tensor_tensor(out=at(mixed), in0=at(mixed), scalar=1.0, in1=ps,
                                                         op0=ALU.add, op1=ALU.mult).then_inc(S["fold"], 1)
                            else:
                                if n >= 2:
                                    dve.wait_ge(S["mix"], i * 2 * NG + n - 1)
                                elif not first:
                                    dve.wait_ge(S["mix"], i * 2 * NG)
                                dve.scalar_tensor_tensor(out=tmp[:, n % 2, :], in0=at(sgb), scalar=1.0, in1=ps,
                                                         op0=ALU.add, op1=ALU.mult).then_inc(S["fold"], 1)
                                dve.wait_ge(S["fold"], i * 2 * NG + KT * NG + n + 1)
                                dve.tensor_tensor(at(mixed), at(mixed), tmp[:, n % 2, :],
                                                  ALU.add).then_inc(S["mix"], 1)

            for br in range(2):
                for k in range(KT):
                    n = br * KT + k
                    dve.wait_ge(S["o_hi"], n + 1)
                    dve.tensor_tensor(R.hlo[:, k, :], ost[n % NO], R.hhi[:, k, :].bitcast(F32),
                                      ALU.subtract).then_inc(S["o_lo"], 1)
                fold(br, 0, True)
                with dve.Fori(1, KT // 2) as i:
                    fold(br, i, False)
            dve.wait_ge(S["mix"], NG * KT)


def output_stage(nc, R, A, gate_rows, mixed, shared, rows):
    with ExitStack() as ctx:
        sb = lambda name, shape, dt=F32: ctx.enter_context(nc.sbuf_tensor(name, shape, dt))
        sem = lambda name: ctx.enter_context(nc.semaphore(name))
        wst = shared.wst[:, :, :, :].rearrange("p a k n -> p a (k n)")
        whi_more = sb("o_w_hi", [P, KT - 2, D], F32R)
        wlo_more = sb("o_w_lo", [P, KT - 2, D], F32R)
        w_at = lambda first, more, k, ns: (
            first[:, k].rearrange("p k n -> p (k n)")[:, ns] if k < 2 else more[:, k - 2, ns])
        whi = lambda k, ns=slice(0, D): w_at(shared.whi, whi_more, k, ns)
        wlo = lambda k, ns=slice(0, D): w_at(shared.wlo, wlo_more, k, ns)
        bank = shared.bank
        gate = rows[:, :, 0:D]
        x = wst
        y, sq, fw = mixed[:, 0:2, 0:D], mixed[:, 2, 0:D], mixed[:, 3, 0:D]
        ss = sb("o_ss", [P, 2])
        ms = sb("o_ms", [P, 2])
        rs = sb("o_rs", [P, 2])
        mhalf = sb("o_mhalf", [P, 1])
        S = {n: sem("o_" + n) for n in ("w_in0", "w_in1", "w_hi", "w_lo", "mix_hi", "mix_lo", "gate_in", "half", "x_in0", "x_in1", "mm", "scaled", "y", "ss", "ms",
                                        "rs", "out", "store0", "store1", "gate")}
        block = ctx.enter_context(nc.Block())
        HALF = D // 2

        @block.sync
        def _(sp):
            for k in range(KT):
                if k >= 2:
                    sp.wait_ge(S["w_lo"], k - 1)
                sp.dma_start(wst[:, k % 2, :], A["w_out"][0, k * P:(k + 1) * P, :]).then_inc(S[f"w_in{k % 2}"], 16)
            for a in range(2):
                sp.dma_start(gate[:, a, :], gate_rows[a:a + 1, :].broadcast_to([P, D])).then_inc(S["gate_in"], 16)
            sp.wait_ge(S["mix_lo"], 4)
            sp.dma_start(fw[:, :], A["final_norm_w"].unsqueeze(0).broadcast_to([P, D])).then_inc(S["gate_in"], 16)
            for t in range(NT + 1):
                if t < NT:
                    src = A["x_prompt"][0] if t == 0 else A["x_sample"][0, (t - 1) * P:t * P, :]
                    if t < 2:
                        sp.wait_ge(S["w_lo"], KT - 1 + t)
                    else:
                        sp.wait_ge(S["y"], t - 1)
                    sp.dma_start(x[:, t % 2, :], src).then_inc(S[f"x_in{t % 2}"], 16)
                if t:
                    dst = A["y_prompt"][0] if t == 1 else A["y_sample"][0, (t - 2) * P:(t - 1) * P, :]
                    sp.wait_ge(S["out"], t)
                    sp.dma_start(dst, y[:, (t - 1) % 2, :]).then_inc(S[f"store{(t - 1) % 2}"], 16)
            sp.wait_ge(S["store0"], 16 * ((NT + 1) // 2))
            sp.wait_ge(S["store1"], 16 * (NT // 2))

        @block.gpsimd
        def _(pool):
            pool.memset(mhalf[:, :], -0.5).then_inc(S["half"], 1)
            for k in range(KT):
                pool.wait_ge(S["mix_hi"], k + 1)
                pool.tensor_tensor(R.hlo[:, k, :], mixed[:, k, :], R.hhi[:, k, :].bitcast(F32),
                                   ALU.subtract).then_inc(S["mix_lo"], 1)
            pool.wait_ge(S["half"], 1)
            for t in range(NT):
                a = slice(t % 2, t % 2 + 1)
                pool.wait_ge(S["ss"], t + 1)
                pool.tensor_scalar(ms[:, a], ss[:, a], 1.0 / D, EPS, ALU.mult, ALU.add).then_inc(S["ms"], 1)
                pool.wait_ge(S["ms"], t + 1)
                if t >= 2:
                    pool.wait_ge(S["out"], t - 1)
                pool.tensor_tensor(rs[:, a], ms[:, a], mhalf[:, :], ALU.pow).then_inc(S["rs"], 1)

        @block.scalar
        def _(act):
            for k in range(KT):
                act.activation(R.hhi[:, k, :], mixed[:, k, :], ACT.Copy).then_inc(S["mix_hi"], 1)
                act.wait_ge(S[f"w_in{k % 2}"], 16 * (k // 2 + 1))
                act.activation(whi(k), wst[:, k % 2, :], ACT.Copy).then_inc(S["w_hi"], 1)
            for t in range(NT):
                act.wait_ge(S["y"], t + 1)
                if t:
                    act.wait_ge(S["ss"], t)
                if t >= 2:
                    act.wait_ge(S["ms"], t - 1)
                act.activation(sq[:, :], y[:, t % 2, :], ACT.Square, accum_out=ss[:, t % 2:t % 2 + 1]
                               ).then_inc(S["ss"], 1)

        @block.tensor
        def _(pe):
            def product(idx, k):
                t, n = divmod(idx, 2)
                ts, ns = slice(t * P, (t + 1) * P), slice(n * HALF, (n + 1) * HALF)
                mm = split_product(pe, bank[idx % 8][:, :], R.hhi[:, k, ts], R.hlo[:, k, ts],
                                   whi(k, ns), wlo(k, ns), k, k == KT - 1)
                if k == KT - 1:
                    mm.then_inc(S["mm"], 1)

            for k in range(KT):
                pe.wait_ge(S["w_lo"], k + 1)
                pe.wait_ge(S["mix_lo"], k + 1)
                for idx in range(8):
                    product(idx, k)
            for idx in range(8, 2 * NT):
                pe.wait_ge(S["scaled"], idx - 7)
                for k in range(KT):
                    product(idx, k)

        @block.vector
        def _(dve):
            for k in range(KT):
                dve.wait_ge(S["w_hi"], k + 1)
                dve.tensor_tensor(wlo(k), wst[:, k % 2, :], whi(k).bitcast(F32),
                                  ALU.subtract).then_inc(S["w_lo"], 1)
            dve.wait_ge(S["gate_in"], 48)
            dve.tensor_scalar(gate[:, :, :], gate[:, :, :], 0.5, None, ALU.mult).then_inc(S["gate"], 1)
            dve.wait_ge(S["gate"], 1)

            def finish(t):
                dve.wait_ge(S["rs"], t + 1)
                dve.scalar_tensor_tensor(out=y[:, t % 2, :], in0=y[:, t % 2, :], scalar=rs[:, t % 2:t % 2 + 1],
                                         in1=fw[:, :], op0=ALU.mult, op1=ALU.mult).then_inc(S["out"], 1)

            for t in range(NT):
                if t >= 2:
                    dve.wait_ge(S[f"store{t % 2}"], 16 * (t // 2))
                for n in range(2):
                    ns = slice(n * HALF, (n + 1) * HALF)
                    dve.wait_ge(S["mm"], 2 * t + n + 1)
                    dve.tensor_tensor(y[:, t % 2, ns], bank[(2 * t + n) % 8][:, :], gate[:, min(t, 1), ns],
                                      ALU.mult).then_inc(S["scaled"], 1)
                dve.wait_ge(S["scaled"], 2 * t + 2)
                dve.wait_ge(S[f"x_in{t % 2}"], 16 * (t // 2 + 1))
                dve.tensor_tensor(y[:, t % 2, :], y[:, t % 2, :], x[:, t % 2, :], ALU.add).then_inc(S["y"], 1)
                if t:
                    finish(t - 1)
            finish(NT - 1)


def build(nc, A):
    oa = nc.dram_tensor("branch_a", (D, TOK), F32, kind="Internal").ap()
    ob = nc.dram_tensor("branch_b", (D, TOK), F32, kind="Internal").ap()
    gate_rows = nc.dram_tensor("gate_rows", (2, D), F32, kind="Internal").ap()
    with ExitStack() as ctx:
        R = Resident(nc, ctx)
        setup_stage(nc, R, A, gate_rows)
        rows = ctx.enter_context(nc.sbuf_tensor("padded_rows", [P, 2, RAW], F32))
        delta_stage(nc, R, A, oa, rows)
        shared = Shared(nc, ctx)
        lru_stage(nc, R, A, ob, shared, rows)
        mixed = ctx.enter_context(nc.sbuf_tensor("mixed", [P, KT, TOK], F32))
        merge_stage(nc, R, A, oa, ob, mixed, shared, rows)
        output_stage(nc, R, A, gate_rows, mixed, shared, rows)


_INS = ["x_prompt", "x_sample", "state_a_fwd", "state_a_bwd", "state_b_fwd", "state_b_bwd", "c", "c_ctx", "norm_w",
        "w_mod", "b_mod", "w_in", "conv_a_w", "conv_a_b", "a_log_fwd", "dt_bias_fwd", "a_log_bwd", "dt_bias_bwd",
        "onorm_a_w", "conv_b_w", "conv_b_b", "lru_wa_fwd", "lru_ba_fwd", "lru_wx_fwd", "lru_bx_fwd", "lru_lambda_fwd",
        "lru_wa_bwd", "lru_ba_bwd", "lru_wx_bwd", "lru_bx_bwd", "lru_lambda_bwd", "w_proj_a", "w_proj_b", "w_gate",
        "b_gate", "w_out", "final_norm_w"]
_OUTS = [("y_prompt", (1, CTX, D)), ("y_sample", (1, LAT, D)), ("new_af", (1, 1, H, P, P)), ("new_ab", (1, 1, H, P, P)),
         ("new_bf", (1, 1, D)), ("new_bb", (1, 1, D))]


def kernel(**inputs):
    import concourse.bacc as _bacc
    from concourse.bass_utils import run_bass_kernel_spmd as _run

    nc = _bacc.Bacc("TRN2", target_bir_lowering=False, num_devices=1)
    arrays, args = {}, {}
    for name in _INS:
        a = np.ascontiguousarray(inputs[name])
        arrays[f"in_{name}"] = a
        args[name] = nc.dram_tensor(f"in_{name}", a.shape, mybir.dt.from_np(a.dtype), kind="ExternalInput").ap()
    arrays["in_consts"] = constants()
    args["consts"] = nc.dram_tensor("in_consts", (P, NM * P), F32, kind="ExternalInput").ap()
    for name, shape in _OUTS:
        args[name] = nc.dram_tensor(f"out_{name}", shape, F32, kind="ExternalOutput").ap()
    build(nc, args)
    r = _run(nc, [arrays], core_ids=[0])
    return tuple(r.results[0][f"out_{name}"] for name, _ in _OUTS)
```
